# Optimizing a Trainium2 kernel written in Bass

```python
import jax
import jax.numpy as jnp
from jax import lax
import numpy as np

D_MODEL = 1024
BATCH = 1
SEQ = 256
DEPTH = 2

HEAD_DIM = 64
N_HEADS_A = 8
WIDTH_A = N_HEADS_A * HEAD_DIM
DILATION_PATTERNS = ((128, 1), (512, 4), (2048, 16))
ROPE_DIM = HEAD_DIM // 4
ROPE_THETA = 500000.0
N_HEADS_B = 8
WIDTH_B = N_HEADS_B * HEAD_DIM
DECAY_LORA = 64
ICLR_LORA = 64
GATE_LORA = 128
RWKV_LN_EPS = 64e-5
WIDTH_C = 512
CONV_WIDTH = 3
N_HEADS_D = 4
HEAD_DIM_D = 128
WIDTH_D = N_HEADS_D * HEAD_DIM_D
DN_CHUNK = 64
D_FF_DENSE = 2816
N_EXPERTS = 8
TOP_K = 2
D_FF_EXPERT = 3584
EVEN_IN = 3 * WIDTH_A + 3 * WIDTH_B
ODD_SPLITS = (WIDTH_C, 2 * WIDTH_C, 3 * WIDTH_C, 3 * WIDTH_C + 3 * WIDTH_D, 3 * WIDTH_C + 4 * WIDTH_D, 3 * WIDTH_C + 4 * WIDTH_D + 2 * N_HEADS_D)
ODD_IN = ODD_SPLITS[-1] + 2 * N_HEADS_D
NORM_EPS = 1e-6
NEG_INF = -1e30

kernel_name = "hybrid_dilated_rwkv7_conv_deltanet_moe"

def rmsnorm(x, w, eps=NORM_EPS):
    xf = x.astype(jnp.float32)
    y = xf * lax.rsqrt(jnp.mean(xf * xf, axis=-1, keepdims=True) + eps)
    return (y * w.astype(jnp.float32)).astype(x.dtype)

def l2norm(x, eps=1e-6):
    xf = x.astype(jnp.float32)
    return (xf * lax.rsqrt(jnp.sum(xf * xf, axis=-1, keepdims=True) + eps)).astype(x.dtype)

def shift_prev(t):
    return jnp.pad(t, ((0, 0), (1, 0), (0, 0)))[:, :-1]

def shift_next(t):
    return jnp.pad(t, ((0, 0), (0, 1), (0, 0)))[:, 1:]

def conv3_centred(t, w):
    return w[0] * shift_prev(t) + w[1] * t + w[2] * shift_next(t)

def both(t, seq_axis):
    return jnp.stack([t, jnp.flip(t, axis=seq_axis)])

def orient(t, seq_axis):
    return jnp.stack([t[0], jnp.flip(t[1], axis=seq_axis)])

def unorient(t, seq_axis):
    return t[0] + jnp.flip(t[1], axis=seq_axis)

def swiglu(h, w_gate, w_up, w_down):
    return (jax.nn.silu(h @ w_gate) * (h @ w_up)) @ w_down

def partial_rope(t, positions):
    half = ROPE_DIM // 2
    inv_freq = jnp.power(ROPE_THETA, -jnp.arange(half, dtype=jnp.float32) / half)
    ang = positions[:, None, :, None].astype(jnp.float32) * inv_freq
    cos, sin = jnp.cos(ang), jnp.sin(ang)
    tf = t[..., :ROPE_DIM].astype(jnp.float32)
    x1, x2 = tf[..., :half], tf[..., half:]
    rot = jnp.concatenate([x1 * cos - x2 * sin, x2 * cos + x1 * sin], axis=-1)
    return jnp.concatenate([rot.astype(t.dtype), t[..., ROPE_DIM:]], axis=-1)

def banded_attention(q, k, v, radius):
    Bb, H, R, L, Dh = q.shape
    blk = radius
    nb = -(-L // blk)
    pad = nb * blk - L
    cfg = lambda lo, hi: ((0, 0), (0, 0), (0, 0), (lo, hi), (0, 0))
    qb = jnp.pad(q, cfg(0, pad)).reshape(Bb, H, R, nb, blk, Dh)

    def windows(t):
        tp = jnp.pad(t, cfg(blk, blk + pad)).reshape(Bb, H, R, nb + 2, blk, Dh)
        return jnp.concatenate([tp[:, :, :, :-2], tp[:, :, :, 1:-1], tp[:, :, :, 2:]], axis=-2)

    kw, vw = windows(k), windows(v)
    s = jnp.einsum('bhrnid,bhrnjd->bhrnij', qb, kw).astype(jnp.float32)
    qi = (jnp.arange(nb)[:, None] * blk + jnp.arange(blk)[None, :])[:, :, None]
    kj = (jnp.arange(nb)[:, None] * blk - blk + jnp.arange(3 * blk)[None, :])[:, None, :]
    valid = (jnp.abs(qi - kj) <= radius) & (kj >= 0) & (kj < L)
    s = jnp.where(valid, s, NEG_INF)
    m = jnp.max(s, axis=-1)
    p = jnp.exp(s - m[..., None])
    l = jnp.sum(p, axis=-1)
    acc = jnp.einsum('bhrnij,bhrnjd->bhrnid', p, vw.astype(jnp.float32))
    m = m.reshape(Bb, H, R, nb * blk)[..., :L]
    l = l.reshape(Bb, H, R, nb * blk)[..., :L]
    acc = acc.reshape(Bb, H, R, nb * blk, Dh)[..., :L, :]
    return m, l, acc

def dilated_branch(q, k, v, window, dilation):
    Bb, H, S, Dh = q.shape
    radius = window // (2 * dilation)
    L = S // dilation
    to_sub = lambda t: t.reshape(Bb, H, L, dilation, Dh).transpose(0, 1, 3, 2, 4)
    m, l, acc = banded_attention(to_sub(q), to_sub(k), to_sub(v), radius)
    m = m.transpose(0, 1, 3, 2).reshape(Bb, H, S)
    l = l.transpose(0, 1, 3, 2).reshape(Bb, H, S)
    acc = acc.transpose(0, 1, 3, 2, 4).reshape(Bb, H, S, Dh)
    return m, l, acc

def dilated_attention(q, k, v):
    branches = [dilated_branch(q, k, v, w, d) for (w, d) in DILATION_PATTERNS]
    m_all = branches[0][0]
    for m, _, _ in branches[1:]:
        m_all = jnp.maximum(m_all, m)
    num = jnp.zeros(q.shape, jnp.float32)
    den = jnp.zeros(q.shape[:-1], jnp.float32)
    for m, l, acc in branches:
        scale = jnp.exp(m - m_all)
        num = num + scale[..., None] * acc
        den = den + scale * l
    return (num / den[..., None]).astype(q.dtype)

def rwkv7_bidir_scan(r, w, k, a, b, v):
    Z, Bb, S, H, N = r.shape
    xs = tuple(jnp.moveaxis(t.astype(jnp.float32), 2, 0) for t in (r, w, k, a, b, v))
    state0 = jnp.zeros((Z, Bb, H, N, N), jnp.float32)

    def step(state, inp):
        rt, wt, kt, at, bt, vt = inp
        sa = jnp.einsum('zbhvk,zbhk->zbhv', state, at)
        state = state * wt[..., None, :] + sa[..., None] * bt[..., None, :] + vt[..., None] * kt[..., None, :]
        return state, jnp.einsum('zbhvk,zbhk->zbhv', state, rt)

    _, ys = lax.scan(step, state0, xs)
    return jnp.moveaxis(ys, 0, 2)

def rwkv7_mixer(h, rkv, shift_mu, lora_mu, w0, w1, w2, a0, a1, a2, g1, g2, k_k, k_a, r_k, ln_w, ln_b):
    Bb, S, _ = h.shape
    rkv = rkv + shift_mu[0] * (shift_prev(rkv) - rkv) + shift_mu[1] * (shift_next(rkv) - rkv)
    r, k, v = jnp.split(rkv, 3, axis=-1)
    hx = h + lora_mu[0] * (shift_prev(h) - h) + lora_mu[1] * (shift_next(h) - h)
    w_pre = w0[:, None, None, :] + jnp.einsum('zbsr,zrc->zbsc', jnp.tanh(jnp.einsum('bsd,zdr->zbsr', hx, w1)), w2)
    decay = jnp.exp(-jnp.exp(-jax.nn.softplus(-w_pre.astype(jnp.float32)) - 0.5))
    iclr = jax.nn.sigmoid(a0[:, None, None, :] + jnp.einsum('zbsr,zrc->zbsc', jnp.einsum('bsd,zdr->zbsr', hx, a1), a2))
    gate = jax.nn.sigmoid(hx @ g1) @ g2
    heads = lambda t: t.reshape(*t.shape[:-1], N_HEADS_B, HEAD_DIM)
    kk = l2norm(heads(k * k_k))
    k_dir = heads(k[None] * (1.0 + (iclr - 1.0) * k_a))
    r_h, v_h = heads(r), heads(v)
    b_vec = kk[None] * heads(iclr)
    a_vec = jnp.broadcast_to(-kk[None], b_vec.shape)
    ys = rwkv7_bidir_scan(both(r_h, 1), orient(heads(decay), 1), orient(k_dir, 1), orient(a_vec, 1), orient(b_vec, 1), both(v_h, 1))
    yf = unorient(ys, 1)
    mu = jnp.mean(yf, axis=-1, keepdims=True)
    var = jnp.mean(jnp.square(yf - mu), axis=-1, keepdims=True)
    yn = ((yf - mu) * lax.rsqrt(var + RWKV_LN_EPS)).reshape(Bb, S, WIDTH_B) * ln_w + ln_b
    bonus = (jnp.sum(r_h * (k_dir[0] + k_dir[1]) * r_k, axis=-1, keepdims=True) * v_h).reshape(Bb, S, WIDTH_B)
    return ((yn + bonus) * gate).astype(h.dtype)

def even_mixer(h, positions, w_in, q_norm, k_norm, shift_mu, lora_mu, w0, w1, w2, a0, a1, a2, g1, g2, k_k, k_a, r_k, ln_w, ln_b, w_out):
    Bb, S, _ = h.shape
    proj = h @ w_in
    a_qkv, b_rkv = proj[..., :3 * WIDTH_A], proj[..., 3 * WIDTH_A:]
    q, k, v = (t.reshape(Bb, S, N_HEADS_A, HEAD_DIM).transpose(0, 2, 1, 3) for t in jnp.split(a_qkv, 3, axis=-1))
    q = partial_rope(rmsnorm(q, q_norm), positions) * HEAD_DIM ** -0.5
    k = partial_rope(rmsnorm(k, k_norm), positions)
    y_a = dilated_attention(q, k, v).transpose(0, 2, 1, 3).reshape(Bb, S, WIDTH_A)
    y_b = rwkv7_mixer(h, b_rkv, shift_mu, lora_mu, w0, w1, w2, a0, a1, a2, g1, g2, k_k, k_a, r_k, ln_w, ln_b)
    return jnp.concatenate([y_a, y_b], axis=-1) @ w_out

def chunk_gated_delta_rule(q, k, v, g, beta):
    out_dtype = v.dtype
    q, k, v, g, beta = (t.astype(jnp.float32) for t in (q, k, v, g, beta))
    Z, Bb, H, T, Dk = q.shape
    Dv = v.shape[-1]
    C = DN_CHUNK
    n = T // C
    q = q.reshape(Z, Bb, H, n, C, Dk)
    k = k.reshape(Z, Bb, H, n, C, Dk)
    v = v.reshape(Z, Bb, H, n, C, Dv)
    g = g.reshape(Z, Bb, H, n, C)
    beta = beta.reshape(Z, Bb, H, n, C)
    gc = jnp.cumsum(g, axis=-1)
    incl = jnp.tril(jnp.ones((C, C), bool))
    strict = jnp.tril(jnp.ones((C, C), bool), -1)
    diff = gc[..., :, None] - gc[..., None, :]
    decay = jnp.where(incl, jnp.exp(jnp.where(incl, diff, 0.0)), 0.0)
    kb = k * beta[..., None]
    lhs = jnp.where(strict, jnp.einsum('zbhnid,zbhnjd->zbhnij', kb, k) * decay, 0.0) + jnp.eye(C, dtype=jnp.float32)
    u_base = lax.linalg.triangular_solve(lhs, v * beta[..., None], left_side=True, lower=True, unit_diagonal=True)
    k_cum = lax.linalg.triangular_solve(lhs, kb * jnp.exp(gc)[..., None], left_side=True, lower=True, unit_diagonal=True)
    attn = jnp.einsum('zbhnid,zbhnjd->zbhnij', q, k) * decay
    xs = tuple(jnp.moveaxis(t, 3, 0) for t in (q, k, gc, u_base, k_cum, attn))

    def step(state, inp):
        qc, kc, gcc, ub, kcm, at = inp
        u = ub - jnp.einsum('zbhcd,zbhdv->zbhcv', kcm, state)
        o = jnp.einsum('zbhcd,zbhdv->zbhcv', qc * jnp.exp(gcc)[..., None], state) + jnp.einsum('zbhij,zbhjv->zbhiv', at, u)
        glast = gcc[..., -1]
        state = state * jnp.exp(glast)[..., None, None] + jnp.einsum('zbhcd,zbhcv->zbhdv', kc * jnp.exp(glast[..., None] - gcc)[..., None], u)
        return state, o

    state0 = jnp.zeros((Z, Bb, H, Dk, Dv), jnp.float32)
    _, o = lax.scan(step, state0, xs)
    return jnp.moveaxis(o, 0, 3).reshape(Z, Bb, H, T, Dv).astype(out_dtype)

def odd_mixer(h, w_in, conv_c, conv_dn, A_log, dt_bias, dn_norm, w_out):
    Bb, S, _ = h.shape
    c_b, c_c, c_x, dn_qkv, dn_z, dn_beta, dn_alpha = jnp.split(h @ w_in, ODD_SPLITS, axis=-1)
    y_c = c_b * conv3_centred(c_c * c_x, conv_c)
    qkv = jax.nn.silu(conv3_centred(dn_qkv, conv_dn))
    q, k, v = (t.reshape(Bb, S, N_HEADS_D, HEAD_DIM_D).transpose(0, 2, 1, 3) for t in jnp.split(qkv, 3, axis=-1))
    q = l2norm(q) * HEAD_DIM_D ** -0.5
    k = l2norm(k)
    beta = jax.nn.sigmoid(dn_beta).reshape(Bb, S, 2, N_HEADS_D).transpose(2, 0, 3, 1)
    alpha = dn_alpha.reshape(Bb, S, 2, N_HEADS_D).transpose(2, 0, 3, 1).astype(jnp.float32)
    g = -jnp.exp(A_log.astype(jnp.float32))[:, None, :, None] * jax.nn.softplus(alpha + dt_bias[:, None, :, None])
    o = chunk_gated_delta_rule(both(q, 2), both(k, 2), both(v, 2), orient(g, 2), orient(beta, 2))
    o = unorient(o, 2).transpose(0, 2, 1, 3)
    y_d = (rmsnorm(o, dn_norm) * jax.nn.silu(dn_z.reshape(Bb, S, N_HEADS_D, HEAD_DIM_D))).reshape(Bb, S, WIDTH_D)
    return jnp.concatenate([y_c, y_d], axis=-1) @ w_out

def moe_swiglu(h, router, w_gate, w_up, w_down):
    logits = (h @ router).astype(jnp.float32)
    probs = jax.nn.softmax(logits, axis=-1)
    top_p, top_i = lax.top_k(probs, TOP_K)
    top_p = top_p / jnp.sum(top_p, axis=-1, keepdims=True)
    gates = jnp.einsum('bsk,bske->bse', top_p, jax.nn.one_hot(top_i, N_EXPERTS, dtype=jnp.float32)).astype(h.dtype)
    out = jnp.zeros_like(h)
    for e in range(N_EXPERTS):
        out = out + gates[..., e:e + 1] * swiglu(h, w_gate[e], w_up[e], w_down[e])
    return out

def setup_inputs(seed: int = 0) -> dict:
    key = jax.random.key(seed)
    ks = iter(jax.random.split(key, 64))
    ne, no = (DEPTH + 1) // 2, DEPTH // 2
    D = D_MODEL

    def nrm(shape, scale):
        return scale * jax.random.normal(next(ks), shape, jnp.float32)

    def gain(shape):
        return 1.0 + 0.05 * jax.random.normal(next(ks), shape, jnp.float32)

    def unif(shape, lo, hi):
        return jax.random.uniform(next(ks), shape, jnp.float32, lo, hi)

    return {
        "x": nrm((BATCH, SEQ, D), 1.0),
        "positions": jnp.broadcast_to(jnp.arange(SEQ, dtype=jnp.int32), (BATCH, SEQ)),
        "ev_mix_norm": gain((ne, D)),
        "ev_w_in": nrm((ne, D, EVEN_IN), D ** -0.5),
        "ev_q_norm": gain((ne, HEAD_DIM)),
        "ev_k_norm": gain((ne, HEAD_DIM)),
        "ev_shift_mu": unif((ne, 2, 3 * WIDTH_B), 0.0, 0.5),
        "ev_lora_mu": unif((ne, 2, D), 0.0, 0.5),
        "ev_w0": unif((ne, 2, WIDTH_B), -4.0, 1.0),
        "ev_w1": nrm((ne, 2, D, DECAY_LORA), D ** -0.5),
        "ev_w2": nrm((ne, 2, DECAY_LORA, WIDTH_B), 0.5 * DECAY_LORA ** -0.5),
        "ev_a0": nrm((ne, 2, WIDTH_B), 0.5),
        "ev_a1": nrm((ne, 2, D, ICLR_LORA), D ** -0.5),
        "ev_a2": nrm((ne, 2, ICLR_LORA, WIDTH_B), 0.5 * ICLR_LORA ** -0.5),
        "ev_g1": nrm((ne, D, GATE_LORA), D ** -0.5),
        "ev_g2": nrm((ne, GATE_LORA, WIDTH_B), GATE_LORA ** -0.5),
        "ev_k_k": gain((ne, WIDTH_B)),
        "ev_k_a": gain((ne, WIDTH_B)),
        "ev_r_k": nrm((ne, N_HEADS_B, HEAD_DIM), 0.1),
        "ev_ln_w": gain((ne, WIDTH_B)),
        "ev_ln_b": nrm((ne, WIDTH_B), 0.02),
        "ev_w_out": nrm((ne, WIDTH_A + WIDTH_B, D), (WIDTH_A + WIDTH_B) ** -0.5),
        "ev_ffn_norm": gain((ne, D)),
        "ev_ffn_gate": nrm((ne, D, D_FF_DENSE), D ** -0.5),
        "ev_ffn_up": nrm((ne, D, D_FF_DENSE), D ** -0.5),
        "ev_ffn_down": nrm((ne, D_FF_DENSE, D), D_FF_DENSE ** -0.5),
        "od_mix_norm": gain((no, D)),
        "od_w_in": nrm((no, D, ODD_IN), D ** -0.5),
        "od_conv_c": nrm((no, CONV_WIDTH, WIDTH_C), CONV_WIDTH ** -0.5),
        "od_conv_dn": nrm((no, CONV_WIDTH, 3 * WIDTH_D), CONV_WIDTH ** -0.5),
        "od_A_log": jnp.log(unif((no, 2, N_HEADS_D), 1.0, 16.0)),
        "od_dt_bias": jnp.log(jnp.expm1(unif((no, 2, N_HEADS_D), 0.001, 0.1))),
        "od_dn_norm": gain((no, HEAD_DIM_D)),
        "od_w_out": nrm((no, WIDTH_C + WIDTH_D, D), (WIDTH_C + WIDTH_D) ** -0.5),
        "od_ffn_norm": gain((no, D)),
        "od_router": nrm((no, D, N_EXPERTS), D ** -0.5),
        "od_moe_gate": nrm((no, N_EXPERTS, D, D_FF_EXPERT), D ** -0.5),
        "od_moe_up": nrm((no, N_EXPERTS, D, D_FF_EXPERT), D ** -0.5),
        "od_moe_down": nrm((no, N_EXPERTS, D_FF_EXPERT, D), D_FF_EXPERT ** -0.5),
    }

def reference(x, positions, ev_mix_norm, ev_w_in, ev_q_norm, ev_k_norm, ev_shift_mu, ev_lora_mu, ev_w0, ev_w1, ev_w2, ev_a0, ev_a1, ev_a2, ev_g1, ev_g2, ev_k_k, ev_k_a, ev_r_k, ev_ln_w, ev_ln_b, ev_w_out, ev_ffn_norm, ev_ffn_gate, ev_ffn_up, ev_ffn_down, od_mix_norm, od_w_in, od_conv_c, od_conv_dn, od_A_log, od_dt_bias, od_dn_norm, od_w_out, od_ffn_norm, od_router, od_moe_gate, od_moe_up, od_moe_down):
    for layer in range(DEPTH):
        i = layer // 2
        if layer % 2 == 0:
            h = rmsnorm(x, ev_mix_norm[i])
            x = x + even_mixer(h, positions, ev_w_in[i], ev_q_norm[i], ev_k_norm[i], ev_shift_mu[i], ev_lora_mu[i], ev_w0[i], ev_w1[i], ev_w2[i], ev_a0[i], ev_a1[i], ev_a2[i], ev_g1[i], ev_g2[i], ev_k_k[i], ev_k_a[i], ev_r_k[i], ev_ln_w[i], ev_ln_b[i], ev_w_out[i])
            h = rmsnorm(x, ev_ffn_norm[i])
            x = x + swiglu(h, ev_ffn_gate[i], ev_ffn_up[i], ev_ffn_down[i])
        else:
            h = rmsnorm(x, od_mix_norm[i])
            x = x + odd_mixer(h, od_w_in[i], od_conv_c[i], od_conv_dn[i], od_A_log[i], od_dt_bias[i], od_dn_norm[i], od_w_out[i])
            h = rmsnorm(x, od_ffn_norm[i])
            x = x + moe_swiglu(h, od_router[i], od_moe_gate[i], od_moe_up[i], od_moe_down[i])
    return x


_drawn_inputs = setup_inputs


def setup_inputs(seed=0):
    import zlib

    import numpy as np

    out = dict(_drawn_inputs(seed))
    spreads = {}
    factors = {'ev_q_norm': 7.022,
     'ev_k_norm': 8.0,
     'ev_k_k': 11.891,
     'od_dn_norm': 3.9,
     'ev_ln_b': 3.323}
    for name, (base, spread) in spreads.items():
        noise = np.random.default_rng([zlib.crc32(name.encode()), seed]).standard_normal(out[name].shape)
        drawn = base * np.exp(spread * noise) if base else spread * noise
        out[name] = jnp.asarray(drawn.astype(out[name].dtype))
    for name, factor in factors.items():
        out[name] = (out[name] * factor).astype(out[name].dtype)
    return out
```

```python
import numpy as np
import concourse.bass as bass
from concourse import mybir
from contextlib import ExitStack

F32 = mybir.dt.float32
I32 = mybir.dt.int32
ACT = mybir.ActivationFunctionType
ALU = mybir.AluOpType
AX = mybir.AxisListType
ADD, SUB, MUL, MAX, MIN = ALU.add, ALU.subtract, ALU.mult, ALU.max, ALU.min

P = 128
D = 1024
SEQ = 256
TT = SEQ // P
KT = D // P
HA, DH = 8, 64
WA = HA * DH
HD, DHD = 4, 128
WC = 512
FF = 2816
FE = 3584
NE = 8
ROPE_HALF = 8
NORM_EPS = 1e-6
L2_EPS = 1e-6
LN_EPS = 64e-5
NEG = -1e30
UPTO = 4

SLOT = 4096
NSLOT = 7
NSTAT = 4
EC = 512
NC_E = FE // EC
NLEV = 7

VEC0 = [("ev_mix_norm", 8), ("ev_shift_mu", 24), ("ev_lora_mu", 16), ("ev_w0", 8), ("ev_a0", 8), ("ev_k_k", 4),
        ("ev_k_a", 4), ("ev_r_k", 4), ("ev_ffn_norm", 8), ("od_mix_norm", 8), ("od_ffn_norm", 8)]
VEC1 = [("od_conv_c", 12), ("od_conv_dn", 36)]


def layout():
    at, out = 0, {}
    for name, n in VEC0 + VEC1:
        out[name] = at
        at += n
    return out, at


def expert_chunks():
    out = []
    for j in range(NC_E):
        out += [("gate", j), ("up", j)]
        if j:
            out.append(("down", j - 1))
    return out + [("down", NC_E - 1)]


def static_chunks():
    out = [("ev_in", n, 1) for n in range(6)] + [("lora1", 0, 5), ("lora2", 0, 3)]
    out += [("ev_out", n, 1) for n in range(2)]
    if UPTO >= 2:
        for n in range(FF // 256):
            out.append(("ffn_in", n, 2))
            if n and n % 2 == 0:
                out.append(("ffn_down", n // 2 - 1, 1))
        out.append(("ffn_down", FF // 512, 1))
    if UPTO >= 3:
        out += [("od_in", n, 1) for n in range(7)] + [("od_out", n, 1) for n in range(2)]
    return out


def hybrid_trunk(nc, A, out):
    COL, NCOL = layout()
    N0 = sum(n for _, n in VEC0)
    N1 = sum(n for _, n in VEC1)
    chunks = static_chunks()
    before, count, where = [None] * NSLOT, [0] * NSLOT, {}
    for i, (kind, n, dmas) in enumerate(chunks):
        s = i % NSTAT
        count[s] += 16 * dmas
        where[kind, n] = (s, before[s], count[s])
        before[s] = (kind, n)
    order = expert_chunks()

    ctx = ExitStack()
    with ctx:
        def sb(name, shape, dt=F32):
            return ctx.enter_context(nc.sbuf_tensor(name, shape, dt))

        def sem(name):
            return ctx.enter_context(nc.semaphore(name))

        ring = sb("ring", [P, NSLOT * SLOT])
        x_sb = sb("x_sb", [P, TT, D])
        xn = sb("xn", [P, TT, D])
        hT = sb("hT", [P, KT, SEQ])
        arena = sb("arena", [P, 11400])
        eps_col = sb("eps_col", [P, 2])
        router_w = sb("router_w", [P, KT, NE])
        ba_w = sb("ba_w", [P, KT, 16])
        flag = sb("flag", [P, 1], I32)
        vecrows = sb("vecrows", [P, 2, P])
        cols = sb("cols", [P, NCOL])
        cmix = sb("cmix", [P, 24])
        ident = sb("ident", [P, P])
        ones = sb("ones", [P, P])
        bones = sb("bones", [P, P])
        head_ind = sb("head_ind", [P, 4, HA])
        tri = sb("tri", [P, 4, P])
        smask = sb("smask", [P, 2, 4, P])
        levmask = sb("levmask", [P, 2, NLEV, P])
        iot = sb("iot", [P, P])
        iota_i = sb("iota_i", [P, P], I32)
        xor_i = sb("xor_i", [P, P], I32)
        rows = sb("rows", [P, 64 + 64 + 512 + 512 + 128 + 8 + 8])
        pos_i = sb("pos_i", [P, TT], I32)
        small = sb("small", [P, 768])

        BC_QN, BC_KN, BC_LW, BC_LB, BC_DN, BC_AL, BC_DT = np.cumsum([0, 64, 64, 512, 512, 128, 8]).tolist()
        qn_row, kn_row = rows[:, BC_QN:BC_QN + 64], rows[:, BC_KN:BC_KN + 64]
        lnw_row, lnb_row = rows[:, BC_LW:BC_LW + 512], rows[:, BC_LB:BC_LB + 512]
        dn_row = rows[:, BC_DN:BC_DN + 128]
        alog_row, dt_row = rows[:, BC_AL:BC_AL + 8], rows[:, BC_DT:BC_DT + 8]

        B = [ctx.enter_context(nc.psum_tensor(f"bank{i}", [P, 512], F32)) for i in range(8)]

        class Region:

            def __init__(self, base, at, size):
                self.base, self.at, self.end = base, at, at + size

            def take(self, *shape):
                n = int(np.prod(shape))
                assert self.at + n <= self.end, (self.at, n, self.end)
                v = self.base[:, self.at:self.at + n]
                self.at += n
                if len(shape) > 1:
                    names = "abcd"[:len(shape)]
                    spec = f"p ({' '.join(names)}) -> p {' '.join(names)}"
                    v = v.rearrange(spec, **dict(zip(names, shape)))
                return v

        sm = Region(small, 0, 768)
        ssq, std, rstd = sm.take(TT), sm.take(TT), sm.take(TT)
        cosT, sinT = sm.take(TT, ROPE_HALF), sm.take(TT, ROPE_HALF)
        ang, red, freq = sm.take(TT, ROPE_HALF), sm.take(TT, ROPE_HALF), sm.take(ROPE_HALF)
        posf = sm.take(TT)
        hs, hsr = sm.take(TT, 16), sm.take(TT, 16)
        mx, nmx, den = sm.take(TT, HA), sm.take(TT, HA), sm.take(TT, HA)
        bonus = sm.take(TT, HA)
        sfac = sm.take(2, 4)
        cmid, emid, eend, sscale = sm.take(HA), sm.take(HA), sm.take(HA), sm.take(HA)

        SCR0 = NSTAT * SLOT
        g_vtok = Region(ring, SCR0, 4096)
        vtok, gate = g_vtok.take(TT, WA), g_vtok.take(TT, WA)
        yab = g_vtok.take(TT, D)
        FZ = SCR0 + 4096
        g_f = Region(ring, FZ, 8192)
        qkv = g_f.take(TT, 3 * WA)
        qT, kTt = g_f.take(4, SEQ), g_f.take(4, SEQ)
        sm_s, sm_p, att_pT = g_f.take(2, 512), g_f.take(2, 512), g_f.take(2, 512)
        g_f2 = Region(ring, FZ, 8192)
        arF = [g_f2.take(4, TT, 2, P) for _ in range(2)]
        bF = [g_f2.take(4, TT, P) for _ in range(2)]
        kF = [g_f2.take(4, TT, P) for _ in range(2)]
        g_g = Region(arena, 0, 11400)
        raw, mix, hxT = g_g.take(12, SEQ), g_g.take(12, SEQ), g_g.take(KT, SEQ)
        sw, lora = g_g.take(2, 4, SEQ), g_g.take(3, SEQ)
        g_g2 = Region(arena, 0, 11400)
        ic, kk = g_g2.take(2, 4, SEQ), g_g2.take(4, SEQ)
        kd = hxT.rearrange("p (z j) s -> p z j s", z=2)
        g_g3 = Region(arena, 0, 11400)
        scg = [g_g3.take(4, 4, P) for _ in range(2)]
        Tm = [g_g3.take(4, P) for _ in range(2)]
        Pm = [g_g3.take(4, P) for _ in range(2)]
        Xm = [g_g3.take(4, P) for _ in range(2)]
        Am = [g_g3.take(4, P) for _ in range(2)]
        Rm = [g_g3.take(4, DH) for _ in range(2)]
        Um = [g_g3.take(4, DH) for _ in range(2)]
        tokbk = g_g3.take(2, 4, P)
        S0 = [g_g3.take(4, P) for _ in range(2)]
        Cw = xn[:, 0, :].rearrange("p (j c s) -> p j c s", j=4, c=TT)
        Ew = xn[:, 1, :].rearrange("p (j c s) -> p j c s", j=4, c=TT)
        Hw = hT[:, 0:4, :].rearrange("p j (c s) -> p j c s", c=TT)
        Cw_f, Ew_f = xn[:, 0, :], xn[:, 1, :]
        Hw_f = hT[:, 0:4, :].rearrange("p j s -> p (j s)")
        amask = yab[:, 1, WA:2 * WA]
        dist = arena[:, 0:512].bitcast(I32)
        bits = arena[:, 512:1024].bitcast(I32)
        mw1, mw2 = arena[:, 1024:1536], arena[:, 1536:2048]
        yT = arena[:, 0:KT * SEQ].rearrange("p (k s) -> p k s", k=KT)

        g_n = Region(arena, 2048, 9000)
        hf, fsil = g_n.take(8, SEQ), g_n.take(3, SEQ)
        g_o = Region(arena, 0, 11400)
        qkvr, qkvc, cbx = g_o.take(12, SEQ), g_o.take(12, SEQ), g_o.take(12, SEQ)
        cu, zt = g_o.take(4, SEQ), g_o.take(TT, 512)
        g_o2 = Region(arena, 0, 3072)
        Ao = [g_o2.take(4, P) for _ in range(2)]
        attn = [g_o2.take(4, P) for _ in range(2)]
        Do = [g_o2.take(4, P) for _ in range(2)]
        g_o3 = Region(arena, 6144, 4096)
        INVB = [(Tm, Pm, Xm, Am)] * 4 + [tuple([g_o3.take(4, P) for _ in range(2)] for _ in range(4))] * 2
        g_o4 = Region(ring, SCR0, 3 * SLOT)
        yTo, ktok, vto, osum = g_o4.take(KT, SEQ), g_o4.take(TT, 512), g_o4.take(TT, 512), g_o4.take(TT, 512)
        kkm = [g_o4.take(4, P) for _ in range(TT)]
        kqm = [g_o4.take(4, P) for _ in range(TT)]
        Ro = [g_o4.take(4, P) for _ in range(2)]
        Uo = [g_o4.take(4, P) for _ in range(2)]
        S0o = [g_o4.take(4, P) for _ in range(2)]
        qe = [g_o4.take(4, P) for _ in range(2)]
        ke = [g_o4.take(4, P) for _ in range(2)]
        beta, alpha, gl_, gc = sm.take(TT, 8), sm.take(TT, 8), sm.take(TT, 8), sm.take(TT, 8)
        gt, gs, ea, ge = sm.take(TT, 8), sm.take(TT, 8), sm.take(8), sm.take(TT, 8)
        glog = sm.take(TT, 8)
        g_e = Region(arena, 0, 11400)
        xg = g_e.take(KT, P)
        esil, ehr, ehT = g_e.take(2, 512), g_e.take(2, 512), g_e.take(2, 4, P)
        ysb, sel, selg, selgT = g_e.take(D), g_e.take(TT, P), g_e.take(TT, P), g_e.take(TT * P)
        prob, oh1, oh2, esc = sm.take(TT, NE), sm.take(TT, NE), sm.take(TT, NE), sm.take(TT, NE)
        gates, rank, asg, ew = sm.take(TT, NE), sm.take(TT, NE), sm.take(TT, NE), sm.take(NE)
        m1, m2, esum = sm.take(TT), sm.take(TT), sm.take(TT)
        cntf = sm.take(1)

        landed = [sem(f"landed{i}") for i in range(NSLOT)]
        x_in = sem("x_in")
        vec_in = sem("vec_in")
        rows_in = sem("rows_in")
        pos_in = sem("pos_in")
        stored = sem("stored")
        dve_chain = sem("dve_chain")
        act_chain = sem("act_chain")
        pool_chain = sem("pool_chain")
        pool_const = sem("pool_const")
        dve_const = sem("dve_const")
        vec_tp = sem("vec_tp")
        cols_rdy = sem("cols_rdy")
        std_rdy = sem("std_rdy")
        xn_rdy = sem("xn_rdy")
        xnT_ps = sem("xnT_ps")
        hT_act = sem("hT_act")
        hT_dve = sem("hT_dve")
        x_rdy = sem("x_rdy")
        qkv_ps = sem("qkv_ps")
        qkv_sb = sem("qkv_sb")
        raw_ps = sem("raw_ps")
        raw_sb = sem("raw_sb")
        hx_rdy = sem("hx_rdy")
        mix_rdy = sem("mix_rdy")
        lora_ps = sem("lora_ps")
        lora_sb = sem("lora_sb")
        wa_ps = sem("wa_ps")
        wa_sb = sem("wa_sb")
        gate_ps = sem("gate_ps")
        gate_sb = sem("gate_sb")
        vt_ps = sem("vt_ps")
        vt_sb = sem("vt_sb")
        kk_sq = sem("kk_sq")
        kk_ps = sem("kk_ps")
        kk_std = sem("kk_std")
        bon_rdy = sem("bon_rdy")
        bon_ps = sem("bon_ps")
        bon_cp = sem("bon_cp")
        red_rdy = sem("red_rdy")
        sin_rdy = sem("sin_rdy")
        qk_sum = sem("qk_sum")
        qk_std = sem("qk_std")
        qk_rdy = sem("qk_rdy")
        qkT_ps = sem("qkT_ps")
        qkT_sb = sem("qkT_sb")
        att_s = sem("att_s")
        att_m = sem("att_m")
        att_e = sem("att_e")
        att_t = sem("att_t")
        att_c = sem("att_c")
        att_o = sem("att_o")
        ya_rdy = sem("ya_rdy")
        dec_c = sem("dec_c")
        dec_e = sem("dec_e")
        fac_rdy = sem("fac_rdy")
        tok_ps = sem("tok_ps")
        tok_sb = sem("tok_sb")
        sc_ps = sem("sc_ps")
        sc_sb = sem("sc_sb")
        t0_rdy = sem("t0_rdy")
        p0_ps = sem("p0_ps")
        p0_sb = sem("p0_sb")
        am_rdy = sem("am_rdy")
        x_ps = sem("x_ps")
        x_cp = sem("x_cp")
        pt_ps = sem("pt_ps")
        tp_sb = sem("tp_sb")
        r_ps = sem("r_ps")
        r_sb = sem("r_sb")
        u_ps = sem("u_ps")
        u_sb = sem("u_sb")
        y_ps = sem("y_ps")
        y_sb = sem("y_sb")
        s_ps = sem("s_ps")
        s_sb = sem("s_sb")
        ln_sum = sem("ln_sum")
        ln_std = sem("ln_std")
        yab_rdy = sem("yab_rdy")
        yT_ps = sem("yT_ps")
        yT_sb = sem("yT_sb")
        o_ps = sem("o_ps")
        gu_ps = sem("gu_ps")
        gu_act = sem("gu_act")
        gu_sb = sem("gu_sb")
        dn_ps = sem("dn_ps")
        cv_ps = sem("cv_ps")
        mask_rdy = sem("mask_rdy")
        wsmall_in, cv_sb, z_ps, z_sb, ba_ps, ba_sb = (sem(n) for n in (
            "wsmall_in", "cv_sb", "z_ps", "z_sb", "ba_ps", "ba_sb"))
        sp_y, sp_l, g_rdy, gc_ps, gc_rdy, ge_rdy = (sem(n) for n in ("sp_y", "sp_l", "g_rdy", "gc_ps", "gc_rdy", "ge_rdy"))
        conv_rdy, silu_rdy, l2_sq, l2_ps, l2_std, qk2_rdy = (sem(n) for n in (
            "conv_rdy", "silu_rdy", "l2_sq", "l2_ps", "l2_std", "qk2_rdy"))
        kk2_ps, kk2_sb, tk_ps, tk_sb = (sem(n) for n in ("kk2_ps", "kk2_sb", "tk_ps", "tk_sb"))
        row_ps, dd_rdy, dd_exp, oa_rdy = (sem(n) for n in ("row_ps", "dd_rdy", "dd_exp", "oa_rdy"))
        ks_ps, or_rdy, ou_ps, ou_sb, ous_rdy, os_ps, os_sb, oo_ps, oo_sb = (sem(n) for n in (
            "ks_ps", "or_rdy", "ou_ps", "ou_sb", "ous_rdy", "os_ps", "os_sb", "oo_ps", "oo_sb"))
        on_sum, on_std, yc_rdy, yd_rdy, yd_ps, yd_sb = (sem(n) for n in (
            "on_sum", "on_std", "yc_rdy", "yd_rdy", "yd_ps", "yd_sb"))
        rt_ps, rt_max, rt_exp, as_rdy, rank_ps, flag_rdy = (sem(n) for n in (
            "rt_ps", "rt_max", "rt_exp", "as_rdy", "rank_ps", "flag_rdy"))
        sel_rdy, xg_ps, xg_sb, st_ps, st_sb = (sem(n) for n in ("sel_rdy", "xg_ps", "xg_sb", "st_ps", "st_sb"))
        eg_ps, eu_ps, ed_ps, eg_act, eh_rdy, ht_ps, ht_sb = (sem(n) for n in (
            "eg_ps", "eu_ps", "ed_ps", "eg_act", "eh_rdy", "ht_ps", "ht_sb"))
        ey_sb, cmb_ps, cmb_sb = (sem(n) for n in ("ey_sb", "cmb_ps", "cmb_sb"))

        def odd_even(m, lev, odd):
            b = 1 << lev
            return m.rearrange("p u (k two b) -> p u k two b", two=2, b=b)[:, :, :, 1 if odd else 0, :]

        def packed(bank, lev, at):
            b = 1 << lev
            return bank[:, :].rearrange("p (u w) -> p u w", u=4)[:, :, at:at + 64].rearrange(
                "p u (k b) -> p u k b", b=b)

        RW = [(0, 0), (1, 1), (0, 1), (1, 0)]
        INV = [[(z, c), (z, c)] for z, c in RW] + [[(0, 0), (1, 1)], [(0, 1), (1, 0)]]

        def inv_seq(p, lev, g):
            return (p * (NLEV - 1) + lev - 1) * 2 + g + 1

        def used_up(kind, n):
            return {"ev_in": (qkv_ps, 2 * n + 2) if n < 3 else (raw_ps, 2 * (n - 3) + 2), "lora1": (lora_ps, 3),
                    "lora2": (gate_ps, 2), "ev_out": (o_ps, 2 * n + 2), "ffn_in": (gu_ps, 2 * n + 2),
                    "ffn_down": (dn_ps, n + 1) if n < FF // 512 else (o_ps, 8),
                    "od_in": (cv_ps, 2 * n + 2) if n < 6 else (z_ps, 2), "od_out": (o_ps, 8 + 2 * n + 2)}[kind]

        block = ctx.enter_context(nc.Block())

        @block.sync
        def _(sp):
            def load(kind, n):
                s, prev, _ = where[kind, n]
                if prev:
                    sp.wait_ge(*used_up(*prev))
                v = ring[:, s * SLOT:(s + 1) * SLOT]
                v8 = v.rearrange("p (k n) -> p k n", k=KT)
                kt = "o (k p) n -> p (o k) n"
                if kind == "ev_in":
                    parts = [(v8, A["ev_w_in"][:, :, 512 * n:512 * n + 512].rearrange(kt, p=P))]
                elif kind == "lora1":
                    w = v[:, 0:KT * 384].rearrange("p (k n) -> p k n", k=KT)
                    parts = [(w[:, :, 64 * z:64 * z + 64], A["ev_w1"][:, z].rearrange(kt, p=P)) for z in range(2)]
                    parts += [(w[:, :, 128 + 64 * z:192 + 64 * z], A["ev_a1"][:, z].rearrange(kt, p=P)) for z in range(2)]
                    parts += [(w[:, :, 256:384], A["ev_g1"].rearrange(kt, p=P))]
                elif kind == "lora2":
                    parts = [(v[:, 0:512], A["ev_w2"].rearrange("o z r c -> (o z r) c")),
                             (v[:, 512:1024], A["ev_a2"].rearrange("o z r c -> (o z r) c")),
                             (v[:, 1024:1536], A["ev_g2"].rearrange("o r c -> (o r) c"))]
                elif kind in ("ev_out", "od_out"):
                    w = A["ev_w_out" if kind == "ev_out" else "od_w_out"]
                    parts = [(v8, w[:, :, 512 * n:512 * n + 512].rearrange(kt, p=P))]
                elif kind == "ffn_in":
                    parts = [(v8[:, :, 256 * i:256 * i + 256],
                              A[w][:, :, 256 * n:256 * n + 256].rearrange(kt, p=P))
                             for i, w in enumerate(("ev_ffn_gate", "ev_ffn_up"))]
                elif kind == "ffn_down":
                    k = min(4, FF // P - 4 * n)
                    parts = [(v[:, 0:k * D].rearrange("p (k n) -> p k n", k=k),
                              A["ev_ffn_down"][:, 512 * n:512 * n + k * P, :].rearrange(kt, p=P))]
                elif kind == "od_in":
                    parts = [(v8, A["od_w_in"][:, :, 512 * n:512 * n + 512].rearrange(kt, p=P))]
                for dst, src in parts:
                    sp.dma_start(dst, src).then_inc(landed[s], 16)

            sp.dma_start(x_sb[:, :, :], A["x"].rearrange("b (a p) n -> p (b a) n", p=P)).then_inc(x_in, 16)
            for r0, vecs, t in ((0, VEC0, 0), (N0, VEC1, 1)):
                for name, n in vecs:
                    a = A[name]
                    if name == "ev_r_k":
                        src = a.rearrange("o (t h) d -> (o t) (h d)", h=2)
                    elif len(a.shape) == 2:
                        src = a.rearrange("o (t p) -> (o t) p", p=P)
                    else:
                        src = a.rearrange("o m (t p) -> (o m t) p", p=P)
                    r = COL[name] - r0
                    sp.dma_start(vecrows[r:r + n, t, :], src).then_inc(vec_in, 16)
            load(*chunks[0][:2])
            sp.dma_start(pos_i[:, :], A["positions"].rearrange("b (a p) -> p (b a)", p=P),
                         allow_slow_non_contiguous=True).then_inc(pos_in, 16)
            for name, at, n in (("ev_q_norm", BC_QN, 64), ("ev_k_norm", BC_KN, 64), ("ev_ln_w", BC_LW, 512),
                                ("ev_ln_b", BC_LB, 512), ("od_dn_norm", BC_DN, 128)):
                sp.dma_start(rows[:, at:at + n], A[name].to_broadcast([P, n])).then_inc(rows_in, 16)
            for name, at in (("od_A_log", BC_AL), ("od_dt_bias", BC_DT)):
                sp.dma_start(rows[:, at:at + 8],
                             A[name].rearrange("o z h -> o (z h)").to_broadcast([P, 8])).then_inc(rows_in, 16)
            if UPTO >= 3:
                sp.dma_start(ba_w[:, :, :], A["od_w_in"][:, :, 7 * 512:7 * 512 + 16].rearrange(
                    "o (k p) n -> p (o k) n", p=P)).then_inc(wsmall_in, 16)
                sp.dma_start(router_w[:, :, :], A["od_router"].rearrange(
                    "o (k p) n -> p (o k) n", p=P)).then_inc(wsmall_in, 16)
            for kind, n, _ in chunks[1:]:
                load(kind, n)
            if UPTO >= 4:
                wg, wu, wd = (A[n][0] for n in ("od_moe_gate", "od_moe_up", "od_moe_down"))

                def expert_load(ps, e, i, r):
                    kind, j = order[r]
                    v = ring[:, (r % NSLOT) * SLOT:(r % NSLOT + 1) * SLOT]
                    if kind == "down":
                        src = wd[e, EC * j:EC * j + EC, :].rearrange("o (k p) n -> p (o k) n", p=P)
                        v = v.rearrange("p (k n) -> p k n", k=EC // P)
                    else:
                        src = (wg if kind == "gate" else wu)[e, :, EC * j:EC * j + EC].rearrange(
                            "o (k p) n -> p (o k) n", p=P)
                        v = v.rearrange("p (k n) -> p k n", k=KT)
                    sp.dma_start(v, src).then_inc(landed[r % NSLOT], 16)

                def expert_wait(ps, i, r):
                    kind, j = order[r]
                    sp.wait_ge({"gate": eg_ps, "up": eu_ps, "down": ed_ps}[kind], i * NC_E + (NE * NC_E * ps + j + 1))

                def expert_pass(ps):
                    for r in range(NSLOT):
                        if ps:
                            expert_wait(ps - 1, NE - 1, len(order) - NSLOT + r)
                        elif r < NSTAT:
                            sp.wait_ge(*used_up(*before[r]))
                        elif r == NSTAT:
                            sp.wait_ge(o_ps, 12)
                        expert_load(ps, slice(0, 1), 0, r)
                    with sp.Fori(0, NE - 1) as i:
                        for r in range(NSLOT, len(order)):
                            expert_wait(ps, i, r - NSLOT)
                            expert_load(ps, bass.ds(i, 1), i, r)
                        for r in range(NSLOT):
                            expert_wait(ps, i, len(order) - NSLOT + r)
                            expert_load(ps, bass.ds(i + 1, 1), i, r)
                    for r in range(NSLOT, len(order)):
                        expert_wait(ps, NE - 1, r - NSLOT)
                        expert_load(ps, slice(NE - 1, NE), NE - 1, r)

                expert_pass(0)
                sp.wait_ge(flag_rdy, 1)
                with sp.If(sp.value_load(flag[0:1, 0:1], min_val=0, max_val=1) > 0):
                    expert_pass(1)
            sp.wait_ge(x_rdy, 2 * UPTO)
            sp.dma_start(out.rearrange("b (a p) n -> p (b a) n", p=P), x_sb[:, :, :]).then_inc(stored, 16)
            sp.wait_ge(stored, 16)

        @block.gpsimd
        def _(pool):
            chain = [0]

            def link(ins):
                chain[0] += 1
                ins.then_inc(pool_chain, 1)
                pool.wait_ge(pool_chain, chain[0])

            link(pool.memset(ident[:, :], 0.0))
            link(pool.affine_select(out=ident[:, :], in_=ident[:, :], compare_op=ALU.not_equal, fill=1.0, base=0,
                                    pattern=[[-1, P]], channel_multiplier=1))
            link(pool.memset(ones[:, :], 1.0))
            pool.iota(iot[:, :], pattern=[[1, P]], base=0, channel_multiplier=0,
                      allow_small_or_imprecise_dtypes=True)
            pool.iota(iota_i[:, :], pattern=[[1, P]], base=0, channel_multiplier=0)
            for a in range(TT):
                pool.iota(dist[:, SEQ * a:SEQ * a + SEQ], pattern=[[-1, SEQ]], base=SEQ + P * a, channel_multiplier=1)
            link(pool.iota(xor_i[:, :], pattern=[[0, P]], base=0, channel_multiplier=1))
            pool.affine_select(out=tri[:, 0, :], in_=ones[:, :], compare_op=ALU.is_gt, fill=0.0, base=0,
                               pattern=[[-1, P]], channel_multiplier=1)
            pool.affine_select(out=tri[:, 1, :], in_=ones[:, :], compare_op=ALU.is_gt, fill=0.0, base=0,
                               pattern=[[1, P]], channel_multiplier=-1)
            pool.affine_select(out=tri[:, 2, :], in_=ones[:, :], compare_op=ALU.is_ge, fill=0.0, base=0,
                               pattern=[[1, P]], channel_multiplier=-1)
            pool.affine_select(out=tri[:, 3, :], in_=ones[:, :], compare_op=ALU.is_ge, fill=0.0, base=0,
                               pattern=[[-1, P]], channel_multiplier=1)
            link(pool.memset(bones[:, :], 0.0))
            link(pool.memset(head_ind[:, :, :], 0.0))
            link(pool.memset(bones[0:64, 0:64], 1.0))
            link(pool.memset(bones[64:128, 64:128], 1.0))
            for j in range(4):
                link(pool.memset(head_ind[0:64, j, 2 * j:2 * j + 1], 1.0))
                link(pool.memset(head_ind[64:128, j, 2 * j + 1:2 * j + 2], 1.0))
            for z in range(2):
                s, i = (1, 2) if z == 0 else (0, 3)
                pool.tensor_copy(smask[:, z, 0, :], tri[:, s, :])
                pool.tensor_copy(smask[:, z, 1, :], tri[:, i, :])
                pool.tensor_copy(smask[:, z, 2, :], tri[:, i, :])
                last = pool.tensor_copy(smask[:, z, 3, :], tri[:, 1 - s, :])
            last.then_inc(pool_const, 1)

            def invert(p, mats):
                for g in range(2):
                    z = INV[p][g][0]
                    pool.wait_ge(*mats[g][1])
                    if p:
                        pool.wait_ge(pt_ps, inv_seq(p - 1, NLEV - 1, g))
                    m0 = levmask[:, z, 0, :].unsqueeze(1).to_broadcast([P, 4, P])
                    Tm, Am = INVB[p][0], INVB[p][3]
                    link(pool.tensor_tensor(Tm[g], mats[g][0], m0, MUL))
                    pool.tensor_tensor(Tm[g], Tm[g], ident[:, :].unsqueeze(1).to_broadcast([P, 4, P]),
                                       ADD).then_inc(t0_rdy, 1)
                for lev in range(1, NLEV):
                    for g in range(2):
                        z = INV[p][g][0]
                        if lev > 1:
                            pool.wait_ge(x_ps, inv_seq(p, lev - 1, g))
                        m = levmask[:, z, lev, :].unsqueeze(1).to_broadcast([P, 4, P])
                        pool.tensor_tensor(Am[g], mats[g][0], m, MUL).then_inc(am_rdy, 1)

            pool.wait_ge(dve_const, 1)
            for p in range(4):
                invert(p, [(scg[g][:, :, 3, :], (sc_sb, 8 * p + 4 * g + 4)) for g in range(2)])
            if UPTO >= 3:
                for p in range(4, 6):
                    invert(p, [(Ao[g], (oa_rdy, 2 * (p - 4) + g + 1)) for g in range(2)])

        @block.scalar
        def _(act):
            chain = [0]

            def link(ins):
                chain[0] += 1
                ins.then_inc(act_chain, 1)
                act.wait_ge(act_chain, chain[0])

            def norm(ni, name):
                if ni == 0:
                    act.wait_ge(x_in, 16)
                else:
                    act.wait_ge(x_rdy, 2 * ni)
                act.activation(xn[:, 0, :], x_sb[:, 0, :], ACT.Square, accum_out=ssq[:, 0:1])
                link(act.activation(xn[:, 1, :], x_sb[:, 1, :], ACT.Square, accum_out=ssq[:, 1:2]))
                act.activation(std, ssq, ACT.Sqrt, scale=1.0 / D, bias=eps_col[:, 0:1]).then_inc(std_rdy, 1)
                if ni == 0:
                    act.wait_ge(cols_rdy, 1)
                for k in range(KT // 2):
                    act.wait_ge(xnT_ps, 4 * ni + k // 2 + 1)
                    last = act.activation(hT[:, k, :], B[k // 2][:, SEQ * (k % 2):SEQ * (k % 2) + SEQ], ACT.Copy,
                                          scale=cols[:, COL[name] + k:COL[name] + k + 1])
                last.then_inc(hT_act, 1)

            act.wait_ge(dve_const, 1)
            norm(0, "ev_mix_norm")
            for i in range(6):
                act.wait_ge(qkv_ps, i + 1)
                act.activation(qkv[:, i % 2, 512 * (i // 2):512 * (i // 2) + 512], B[i][:, :],
                               ACT.Copy).then_inc(qkv_sb, 1)
            act.wait_ge(red_rdy, 1)
            act.activation(sinT, red, ACT.Sin)
            act.activation(cosT, ang, ACT.Sin).then_inc(sin_rdy, 1)
            act.wait_ge(qk_sum, 1)
            act.activation(hsr, hs, ACT.Sqrt, scale=1.0 / DH, bias=eps_col[:, 0:1]).then_inc(qk_std, 1)
            act.wait_ge(mask_rdy, 1)
            for m in range(6):
                act.wait_ge(raw_ps, m + 1)
                act.activation(raw[:, 2 * m:2 * m + 2, :], B[6 + m % 2][:, :].rearrange("p (t s) -> p t s", t=2),
                               ACT.Copy).then_inc(raw_sb, 1)
            for i, f in enumerate((ACT.Tanh, ACT.Copy, ACT.Sigmoid)):
                act.wait_ge(lora_ps, i + 1)
                act.activation(lora[:, i, :], B[i][:, 0:SEQ], f).then_inc(lora_sb, 1)
            for i in range(2):
                if i:
                    act.wait_ge(mix_rdy, 1)
                for z in range(2):
                    for j in range(4):
                        m = i * 8 + z * 4 + j
                        act.wait_ge(wa_ps, m // 2 + 1)
                        b = COL["ev_w0" if i == 0 else "ev_a0"] + 4 * z + j
                        src = B[3 + (m // 2) % 3][:, SEQ * (m % 2):SEQ * (m % 2) + SEQ]
                        act.activation((sw, ic)[i][:, z, j, :], src, ACT.Sigmoid,
                                       bias=cols[:, b:b + 1]).then_inc(wa_sb, 1)
            for a in range(TT):
                act.wait_ge(gate_ps, a + 1)
                act.activation(gate[:, a, :], B[a][:, :], ACT.Copy).then_inc(gate_sb, 1)
            for i in range(4):
                act.wait_ge(qkT_ps, i + 1)
                dst = (qT, kTt)[i // 2][:, 2 * (i % 2):2 * (i % 2) + 2, :]
                act.activation(dst, B[4 + i][:, :].rearrange("p (j s) -> p j s", j=2), ACT.Copy).then_inc(qkT_sb, 1)
            for h in range(HA):
                act.wait_ge(att_m, h + 1)
                for a in range(TT):
                    last = act.activation(sm_p[:, h % 2, SEQ * a:SEQ * a + SEQ], sm_s[:, h % 2, SEQ * a:SEQ * a + SEQ],
                                          ACT.Exp, bias=nmx[:, a, h:h + 1], accum_out=den[:, a, h:h + 1])
                last.then_inc(att_e, 1)
                act.wait_ge(att_t, h + 1)
                act.activation(att_pT[:, h % 2, :], B[2 + 2 * (h % 2)][:, :], ACT.Copy).then_inc(att_c, 1)
            act.wait_ge(kk_ps, 2)
            for i in range(2):
                last = act.activation(Ew_f[:, 512 * i:512 * i + 512], B[6 + i][:, :], ACT.Sqrt, bias=eps_col[:, 0:1])
            last.then_inc(kk_std, 1)
            for z in range(2):
                act.wait_ge(dec_c, z + 1)
                act.activation(Ew, Cw, ACT.Exp, scale=-1.0)
                act.activation(emid, cmid, ACT.Exp)
                act.activation(eend, sscale, ACT.Exp)
                link(act.activation(Cw, Cw, ACT.Exp))
                act.activation(Hw, Hw, ACT.Exp).then_inc(dec_e, 1)

            def inv_copies(p):
                Pm, Xm = INVB[p][1], INVB[p][2]
                for g in range(2):
                    act.wait_ge(p0_ps, 2 * p + g + 1)
                    act.activation(Pm[g], B[2 + g][:, :].rearrange("p (u s) -> p u s", u=4),
                                   ACT.Copy).then_inc(p0_sb, 1)
                for lev in range(1, NLEV):
                    for g in range(2):
                        n = inv_seq(p, lev, g)
                        act.wait_ge(x_ps, n)
                        if lev < NLEV - 1:
                            act.activation(Xm[g], B[g][:, :].rearrange("p (u s) -> p u s", u=4),
                                           ACT.Copy).then_inc(x_cp, 1)
                        else:
                            odd = INV[p][g][0] == 0
                            act.activation(odd_even(Xm[g], lev, odd)[:, :, 0, :], packed(B[g], lev, 0)[:, :, 0, :],
                                           ACT.Copy).then_inc(x_cp, 1)

            for p, (z, c) in enumerate(RW):
                first = p < 2
                if first:
                    for i in range(2):
                        act.wait_ge(tok_ps, 2 * p + i + 1)
                        act.activation(tokbk[:, i, :, :], B[6 + i][:, :].rearrange("p (j s) -> p j s", j=4),
                                       ACT.Copy).then_inc(tok_sb, 1)
                inv_copies(p)
                for g in range(2):
                    act.wait_ge(r_ps, 2 * p + g + 1)
                    act.activation(Rm[g], B[4 + g][:, 0:256].rearrange("p (u v) -> p u v", u=4), ACT.Copy,
                                   scale=-1.0).then_inc(r_sb, 1)
                for g in range(2):
                    act.wait_ge(u_ps, 2 * p + g + 1)
                    act.activation(Um[g], B[6 + g][:, 0:256].rearrange("p (u v) -> p u v", u=4),
                                   ACT.Copy).then_inc(u_sb, 1)
            act.wait_ge(ln_sum, 1)
            act.activation(hsr[:, :, 0:8], hs[:, :, 0:8], ACT.Sqrt, scale=1.0 / DH,
                           bias=eps_col[:, 1:2]).then_inc(ln_std, 1)
            for i in range(4):
                act.wait_ge(yT_ps, i + 1)
                act.activation(yT[:, 2 * i:2 * i + 2, :], B[i][:, :].rearrange("p (j s) -> p j s", j=2),
                               ACT.Copy).then_inc(yT_sb, 1)
            if UPTO >= 2:
                norm(1, "ev_ffn_norm")
                for i in range(FF // P):
                    act.wait_ge(gu_ps, i + 1)
                    if i >= 3:
                        act.wait_ge(gu_sb, i - 2)
                    act.activation(fsil[:, i % 3, :], B[i % 3][:, 0:SEQ], ACT.Silu).then_inc(gu_act, 1)
            if UPTO >= 3:
                norm(2, "od_mix_norm")
                for m in range(12):
                    act.wait_ge(cv_ps, m + 1)
                    dst = cbx[:, 2 * m:2 * m + 2, :] if m < 6 else qkvr[:, 2 * m - 12:2 * m - 10, :]
                    act.activation(dst, B[m % 4][:, :].rearrange("p (t s) -> p t s", t=2), ACT.Copy).then_inc(cv_sb, 1)
                for a in range(TT):
                    act.wait_ge(z_ps, a + 1)
                    act.activation(zt[:, a, :], B[4 + a][:, :], ACT.Silu).then_inc(z_sb, 1)
                act.wait_ge(ba_ps, 1)
                ba = B[6][:, 0:TT * 16].rearrange("p (a n) -> p a n", a=TT)
                act.activation(beta, ba[:, :, 0:8], ACT.Sigmoid)
                act.activation(alpha, ba[:, :, 8:16], ACT.Copy).then_inc(ba_sb, 1)
                act.wait_ge(sp_y, 1)
                link(act.activation(gs, gs, ACT.Exp, scale=-1.0))
                act.activation(ea, alog_row, ACT.Exp)
                act.activation(gs, gs, ACT.Ln, bias=1.0).then_inc(sp_l, 1)
                act.wait_ge(gc_rdy, 1)
                act.activation(ge, gt, ACT.Exp).then_inc(ge_rdy, 1)
                for i in range(3):
                    act.wait_ge(conv_rdy, i + 1)
                    v = qkvc[:, 4 * i:4 * i + 4, :]
                    act.activation(v, v, ACT.Silu).then_inc(silu_rdy, 1)
                for i in range(4):
                    act.wait_ge(l2_ps, i + 1)
                    act.activation(xn[:, i // 2, 512 * (i % 2):512 * (i % 2) + 512], B[i][:, :], ACT.Sqrt,
                                   bias=eps_col[:, 0:1]).then_inc(l2_std, 1)
                for c in range(TT):
                    act.wait_ge(kk2_ps, c + 1)
                    act.activation(kkm[c], B[c][:, :].rearrange("p (u s) -> p u s", u=4), ACT.Copy)
                    act.activation(kqm[c], B[2 + c][:, :].rearrange("p (u s) -> p u s", u=4),
                                   ACT.Copy).then_inc(kk2_sb, 1)
                for i in range(4):
                    act.wait_ge(tk_ps, i + 1)
                    act.activation((ktok, vto)[i // 2][:, i % 2, :], B[4 + i][:, :], ACT.Copy).then_inc(tk_sb, 1)
                for p in range(4, 6):
                    for g in range(2):
                        n = 2 * (p - 4) + g + 1
                        act.wait_ge(dd_rdy, n)
                        act.activation(attn[g], attn[g], ACT.Exp)
                        last = act.activation(Do[g], Do[g], ACT.Exp, scale=-1.0)
                        if p == 5:
                            act.activation(qe[g], B[4 + g][:, :].rearrange("p (u s) -> p u s", u=4), ACT.Exp)
                            last = act.activation(ke[g], B[4 + g][:, :].rearrange("p (u s) -> p u s", u=4), ACT.Exp)
                        last.then_inc(dd_exp, 1)
                    inv_copies(p)
                    for g in range(2):
                        act.wait_ge(ou_ps, 2 * (p - 4) + g + 1)
                        act.activation(Uo[g], B[6 + g][:, :].rearrange("p (u s) -> p u s", u=4),
                                       ACT.Copy).then_inc(ou_sb, 1)
                act.wait_ge(on_sum, 1)
                act.activation(hsr[:, :, 0:4], hs[:, :, 0:4], ACT.Sqrt, scale=1.0 / DHD,
                               bias=eps_col[:, 0:1]).then_inc(on_std, 1)
                for i in range(2):
                    act.wait_ge(yd_ps, i + 1)
                    act.activation(yTo[:, 4 + 2 * i:6 + 2 * i, :], B[i][:, :].rearrange("p (j s) -> p j s", j=2),
                                   ACT.Copy).then_inc(yd_sb, 1)
            if UPTO >= 4:
                norm(3, "od_ffn_norm")
                act.wait_ge(rt_max, 1)
                for a in range(TT):
                    last = act.activation(prob[:, a, :], B[7][:, NE * a:NE * a + NE], ACT.Exp, bias=m2[:, a:a + 1],
                                          accum_out=esum[:, a:a + 1])
                last.then_inc(rt_exp, 1)

                def expert(ps, i):
                    b1, b2, b7 = NE * ps + 1, 2 * NE * ps + 1, NC_E * NE * ps + 1
                    act.wait_ge(st_ps, i + b1)
                    act.activation(selgT, B[4][:, 0:TT * P], ACT.Copy).then_inc(st_sb, 1)

                    def turned(j):
                        act.wait_ge(ht_ps, i * NC_E + b7 + j)
                        act.activation(ehT[:, j % 2], B[6 + j % 2][:, :].rearrange("p (k s) -> p k s", k=4),
                                       ACT.Copy).then_inc(ht_sb, 1)

                    for j in range(NC_E):
                        act.wait_ge(eg_ps, i * NC_E + b7 + j)
                        act.activation(esil[:, j % 2, :], B[j % 2][:, :], ACT.Silu).then_inc(eg_act, 1)
                        if j:
                            turned(j - 1)
                    turned(NC_E - 1)
                    for n in range(2):
                        act.wait_ge(ed_ps, i * NC_E + b7 + NC_E - 1)
                        act.activation(ysb[:, 512 * n:512 * n + 512], B[4 + n][:, :], ACT.Copy).then_inc(ey_sb, 1)

                with act.Fori(0, NE) as i:
                    expert(0, i)
                act.wait_ge(flag_rdy, 1)
                with act.If(act.value_load(flag[0:1, 0:1], min_val=0, max_val=1) > 0):
                    with act.Fori(0, NE) as i:
                        expert(1, i)

        @block.vector
        def _(dve):
            chain = [0]

            def link(ins):
                chain[0] += 1
                ins.then_inc(dve_chain, 1)
                dve.wait_ge(dve_chain, chain[0])

            def norm(ni, name):
                dve.wait_ge(std_rdy, ni + 1)
                link(dve.reciprocal(rstd, std))
                dve.tensor_scalar(xn[:, 0, :], x_sb[:, 0, :], rstd[:, 0:1], None, MUL)
                dve.tensor_scalar(xn[:, 1, :], x_sb[:, 1, :], rstd[:, 1:2], None, MUL).then_inc(xn_rdy, 1)
                for k in range(KT // 2, KT):
                    dve.wait_ge(xnT_ps, 4 * ni + k // 2 + 1)
                    last = dve.tensor_scalar(hT[:, k, :], B[k // 2][:, SEQ * (k % 2):SEQ * (k % 2) + SEQ],
                                             cols[:, COL[name] + k:COL[name] + k + 1], None, MUL)
                last.then_inc(hT_dve, 1)
                dve.wait_ge(hT_dve, ni + 1)
                dve.wait_ge(hT_act, ni + 1)

            dve.memset(eps_col[:, 0:1], NORM_EPS)
            dve.memset(eps_col[:, 1:2], LN_EPS)
            inv_freq = np.power(np.float32(500000.0), -np.arange(ROPE_HALF, dtype=np.float32) / np.float32(ROPE_HALF))
            for i in range(ROPE_HALF):
                dve.memset(freq[:, i:i + 1], float(inv_freq[i]))
            dve.wait_ge(pool_const, 1)
            link(dve.tensor_tensor(xor_i[:, :], xor_i[:, :], iota_i[:, :], ALU.bitwise_xor))
            for lev in range(NLEV):
                link(dve.tensor_scalar(iota_i[:, :], xor_i[:, :], lev, None, ALU.logical_shift_right))
                for z in range(2):
                    link(dve.scalar_tensor_tensor(levmask[:, z, lev, :], iota_i[:, :], 1.0, tri[:, z, :],
                                                  ALU.is_equal, MUL))
            dve.tensor_scalar(levmask[:, :, :, :].rearrange("p z l s -> p (z l s)"),
                              levmask[:, :, :, :].rearrange("p z l s -> p (z l s)"), -1.0, None,
                              MUL).then_inc(dve_const, 1)
            link(dve.tensor_copy(mw1, dist))
            link(dve.tensor_scalar(mw2, mw1, float(SEQ - 64), None, ALU.is_ge))
            link(dve.scalar_tensor_tensor(mw2, mw1, float(SEQ + 64), mw2, ALU.is_le, MUL))
            for dil in (4, 16):
                link(dve.tensor_scalar(bits, dist, dil - 1, None, ALU.bitwise_and))
                link(dve.scalar_tensor_tensor(mw2, bits, 0.0, mw2, ALU.is_equal, ADD))
            link(dve.tensor_scalar(mw1, mw2, 0.5, NEG, ALU.is_lt, MUL))
            link(dve.tensor_scalar(amask, mw2, 1.5, float(np.log(2.0)), ALU.is_ge, MUL))
            link(dve.tensor_tensor(amask, amask, mw1, ADD))
            link(dve.tensor_scalar(mw1, mw2, 2.5, float(np.log(1.5)), ALU.is_ge, MUL))
            dve.tensor_tensor(amask, amask, mw1, ADD).then_inc(mask_rdy, 1)
            dve.wait_ge(mask_rdy, 1)
            dve.wait_ge(vec_tp, 1)
            dve.tensor_copy(cols[:, 0:N0], B[7][:, 0:N0])
            dve.tensor_copy(cols[:, N0:NCOL], B[7][:, P:P + N1]).then_inc(cols_rdy, 1)
            dve.wait_ge(cols_rdy, 1)
            mu, lm = COL["ev_shift_mu"], COL["ev_lora_mu"]
            dve.scalar_tensor_tensor(cmix[:, 0:12], cols[:, mu:mu + 12], -1.0, cols[:, mu + 12:mu + 24], MUL, SUB)
            dve.scalar_tensor_tensor(cmix[:, 12:20], cols[:, lm:lm + 8], -1.0, cols[:, lm + 8:lm + 16], MUL, SUB)
            ka = COL["ev_k_a"]
            link(dve.tensor_scalar(cmix[:, 20:24], cols[:, ka:ka + 4], -1.0, None, MUL))
            link(dve.tensor_scalar(cmix[:, :], cmix[:, :], 1.0, None, ADD))
            norm(0, "ev_mix_norm")

            def shift_mix(dst, src, k, c0, m0, m1):
                link(dve.tensor_scalar(dst[:, k, :], src[:, k, :], c0, None, MUL))
                link(dve.scalar_tensor_tensor(dst[:, k, 1:SEQ], src[:, k, 0:SEQ - 1], m0, dst[:, k, 1:SEQ], MUL, ADD))
                link(dve.scalar_tensor_tensor(dst[:, k, 0:SEQ - 1], src[:, k, 1:SEQ], m1, dst[:, k, 0:SEQ - 1],
                                              MUL, ADD))

            for k in range(KT):
                shift_mix(hxT, hT, k, cmix[:, 12 + k:13 + k], cols[:, lm + k:lm + k + 1],
                          cols[:, lm + 8 + k:lm + 9 + k])
            dve.memset(bonus[:, :, :], 0.0).then_inc(hx_rdy, 1)
            dve.wait_ge(pos_in, 16)
            link(dve.tensor_copy(posf, pos_i[:, :]))
            for a in range(TT):
                link(dve.tensor_scalar(ang[:, a, :], freq, posf[:, a:a + 1], None, MUL))
            MAGIC = 12582912.0
            link(dve.tensor_scalar(red, ang, 1.0 / (2 * np.pi), MAGIC, MUL, ADD))
            link(dve.tensor_scalar(red, red, -MAGIC, None, ADD))
            C1 = 6.28125
            C2 = float(np.float32(0.0019353071795864769).view(np.int32) & -4096 and
                       np.array(np.float32(0.0019353071795864769).view(np.int32) & -4096, np.int32).view(np.float32))
            C3 = float(2 * np.pi - C1 - C2)
            for cc in (C1, C2, C3):
                link(dve.scalar_tensor_tensor(ang, red, -cc, ang, MUL, ADD))
            PI = 3.1415925
            link(dve.tensor_scalar(red, ang, PI, -PI, MIN, MAX))
            link(dve.tensor_scalar(ang, red, -1.0, None, MUL))
            link(dve.tensor_tensor(ang, ang, red, MAX))
            dve.tensor_scalar(ang, ang, -1.0, float(np.pi / 2), MUL, ADD).then_inc(red_rdy, 1)
            dve.wait_ge(rows_in, 16 * 7)
            dve.wait_ge(qkv_sb, 6)
            link(dve.tensor_tensor(xn[:, :, :], qkv[:, :, 0:D], qkv[:, :, 0:D], MUL))
            dve.tensor_reduce(hs, xn[:, :, :].rearrange("p a (h d) -> p a h d", d=DH), AX.X, ADD).then_inc(qk_sum, 1)
            dve.wait_ge(qk_std, 1)
            link(dve.reciprocal(hsr, hsr))
            qk4 = qkv[:, :, 0:D].rearrange("p a (h d) -> p a h d", d=DH)
            for a in range(TT):
                link(dve.tensor_tensor(qk4[:, a], qk4[:, a], hsr[:, a, :].unsqueeze(2).to_broadcast([P, 16, DH]), MUL))
                for i, row in enumerate((qn_row, kn_row)):
                    v = qk4[:, a, 8 * i:8 * i + 8, :]
                    link(dve.tensor_tensor(v, v, row.unsqueeze(1).to_broadcast([P, 8, DH]), MUL))
            dve.wait_ge(sin_rdy, 1)
            rt = xn[:, :, 0:4 * 16 * ROPE_HALF].rearrange("p a (i h e) -> p a i h e", i=4, h=16)
            for a in range(TT):
                x1, x2 = qk4[:, a, :, 0:ROPE_HALF], qk4[:, a, :, ROPE_HALF:2 * ROPE_HALF]
                co = cosT[:, a, :].unsqueeze(1).to_broadcast([P, 16, ROPE_HALF])
                si = sinT[:, a, :].unsqueeze(1).to_broadcast([P, 16, ROPE_HALF])
                dve.tensor_tensor(rt[:, a, 0], x1, co, MUL)
                dve.tensor_tensor(rt[:, a, 1], x2, si, MUL)
                dve.tensor_tensor(rt[:, a, 2], x2, co, MUL)
                link(dve.tensor_tensor(rt[:, a, 3], x1, si, MUL))
                dve.tensor_tensor(x1, rt[:, a, 0], rt[:, a, 1], SUB)
                last = dve.tensor_tensor(x2, rt[:, a, 2], rt[:, a, 3], ADD)
            last.then_inc(qk_rdy, 1)
            dve.wait_ge(raw_sb, 6)
            for t in range(12):
                shift_mix(mix, raw, t, cmix[:, t:t + 1], cols[:, mu + t:mu + t + 1], cols[:, mu + 12 + t:mu + 13 + t])
            dve.memset(bonus[:, :, :], 0.0).then_inc(mix_rdy, 1)
            for h in range(HA):
                dve.wait_ge(att_s, h + 1)
                if h > 1:
                    dve.wait_ge(att_e, h - 1)
                s2 = sm_s[:, h % 2, :].rearrange("p (a s) -> p a s", a=TT)
                link(dve.scalar_tensor_tensor(sm_s[:, h % 2, :], B[h % 2][:, :], DH ** -0.5,
                                              amask, MUL, ADD))
                link(dve.tensor_reduce(mx[:, :, h:h + 1], s2, AX.X, MAX))
                dve.tensor_scalar(nmx[:, :, h:h + 1], mx[:, :, h:h + 1], -1.0, None, MUL).then_inc(att_m, 1)
            dve.wait_ge(att_o, HA)
            link(dve.reciprocal(den, den))
            for a in range(TT):
                last = dve.tensor_tensor(yab[:, a, 0:WA].rearrange("p (h d) -> p h d", d=DH),
                                         B[3 + 2 * a][:, :].rearrange("p (h d) -> p h d", d=DH),
                                         den[:, a, :].unsqueeze(2).to_broadcast([P, HA, DH]), MUL)
            last.then_inc(ya_rdy, 1)
            dve.wait_ge(ya_rdy, 1)
            for i in range(2):
                dve.wait_ge(vt_ps, i + 1)
                dve.tensor_copy(vtok[:, i, :], B[6 + i][:, :]).then_inc(vt_sb, 1)
            dve.wait_ge(wa_sb, 16)
            kv = COL["ev_k_k"]
            r_, k_ = mix[:, 0:4, :], mix[:, 4:8, :]
            for j in range(4):
                dve.tensor_scalar(kk[:, j, :], k_[:, j, :], cols[:, kv + j:kv + j + 1], None, MUL)
                for z in range(2):
                    last = dve.tensor_scalar(kd[:, z, j, :], ic[:, z, j, :], cols[:, ka + j:ka + j + 1],
                                             cmix[:, 20 + j:21 + j], MUL, ADD)
            link(last)
            dve.tensor_tensor(Cw_f, kk.rearrange("p j s -> p (j s)"), kk.rearrange("p j s -> p (j s)"),
                              MUL).then_inc(kk_sq, 1)
            for z in range(2):
                link(dve.tensor_tensor(kd[:, z], kd[:, z], k_, MUL))
            link(dve.tensor_tensor(Hw_f, kd[:, 0].rearrange("p j s -> p (j s)"),
                                   kd[:, 1].rearrange("p j s -> p (j s)"), ADD))
            rk = COL["ev_r_k"]
            for j in range(4):
                last = dve.scalar_tensor_tensor(Hw_f[:, SEQ * j:SEQ * j + SEQ], Hw_f[:, SEQ * j:SEQ * j + SEQ],
                                                cols[:, rk + j:rk + j + 1], r_[:, j, :], MUL, MUL)
            last.then_inc(bon_rdy, 1)
            dve.wait_ge(kk_std, 1)
            link(dve.reciprocal(Ew_f, Ew_f))
            link(dve.tensor_tensor(kk.rearrange("p j s -> p (j s)"), kk.rearrange("p j s -> p (j s)"), Ew_f, MUL))
            dve.wait_ge(bon_ps, 1)
            dve.tensor_copy(bonus.rearrange("p a h -> p (a h)"), B[5][:, 0:TT * HA]).then_inc(bon_cp, 1)
            E5 = -float(np.exp(-0.5))
            link(dve.tensor_scalar(sw.rearrange("p z j s -> p (z j s)"), sw.rearrange("p z j s -> p (z j s)"),
                                   E5, None, MUL))
            for z in range(2):
                for j in range(4):
                    for c in range(TT):
                        o, i = Cw[:, j, c, :], sw[:, z, j, P * c:P * c + P]
                        if z:
                            o, i = o[:, ::-1], i[:, ::-1]
                        last = dve.tensor_tensor_scan(o, ones[:, :], i, 0.0, MUL, ADD)
                link(last)
                m8 = "p j c s -> p (j c) s"
                c8 = Cw.rearrange(m8)
                link(dve.tensor_copy(cmid, c8[:, :, 63]))
                link(dve.tensor_tensor(c8, c8, cmid.unsqueeze(2).to_broadcast([P, 8, P]), SUB))
                link(dve.tensor_copy(sscale, c8[:, :, P - 1 if z == 0 else 0]))
                dve.tensor_tensor(Hw, Cw, sw[:, z].rearrange("p j (c s) -> p j c s", c=TT), SUB).then_inc(dec_c, 1)
                dve.wait_ge(dec_e, z + 1)
                r4, kk4 = (v.rearrange("p j (c s) -> p j c s", c=TT) for v in (r_, kk))
                for c in range(TT):
                    dve.tensor_tensor(arF[z][:, :, c, 1, :], r4[:, :, c], Cw[:, :, c], MUL)
                    dve.tensor_tensor(arF[z][:, :, c, 0, :], kk4[:, :, c], Hw[:, :, c], MUL)
                dve.tensor_tensor(kF[z], kd[:, z].rearrange("p j (c s) -> p j c s", c=TT), Ew, MUL)
                link(dve.tensor_tensor(Ew, Ew, kk4, MUL))
                link(dve.tensor_tensor(bF[z], ic[:, z].rearrange("p j (c s) -> p j c s", c=TT), Ew, MUL))
                cf, cs = (0, 1) if z == 0 else (1, 0)
                end2, mid2 = (v.rearrange("p (j c) -> p j c", c=TT) for v in (eend, emid))
                link(dve.tensor_tensor(sfac[:, z, :], end2[:, :, cf], mid2[:, :, cs], MUL))
            dve.tensor_copy(cmid[:, 0:1], sfac[:, 0, 0:1]).then_inc(fac_rdy, 1)

            def inv_adds(p):
                Tm, Pm = INVB[p][0], INVB[p][1]
                for lev in range(1, NLEV):
                    for g in range(2):
                        dve.wait_ge(pt_ps, inv_seq(p, lev, g))
                        odd = INV[p][g][0] == 0
                        pv = odd_even(Pm[g], lev, odd)
                        last = dve.tensor_tensor(pv, packed(B[2 + g], lev, 0), pv, ADD)
                        if lev < NLEV - 1:
                            tv = odd_even(Tm[g], lev, not odd)
                            last = dve.tensor_tensor(tv, packed(B[2 + g], lev, 64), tv, ADD)
                        last.then_inc(tp_sb, 1)

            for p, (z, c) in enumerate(RW):
                for i in range(8):
                    dve.wait_ge(sc_ps, 8 * p + i + 1)
                    if p and i % 4 == 0:
                        dve.wait_ge(y_ps, 2 * p)
                    dve.tensor_tensor(scg[i // 4][:, i % 4], B[4 + i % 2][:, :].rearrange("p (m s) -> p m s", m=4),
                                      smask[:, z], MUL).then_inc(sc_sb, 1)
                inv_adds(p)
                for g in range(2):
                    if p < 2:
                        dve.wait_ge(s_ps, 2 * p + g + 1)
                        for i in range(2):
                            j = 2 * g + i
                            last = dve.scalar_tensor_tensor(S0[z][:, j, :], B[g][:, P * i:P * i + P],
                                                            sfac[:, z, j:j + 1], bones[:, :], MUL, MUL)
                        last.then_inc(s_sb, 1)
                for g in range(2):
                    dve.wait_ge(y_ps, 2 * p + g + 1)
                    dst = yab[:, c, WA + 256 * g:WA + 256 * g + 256]
                    if p < 2:
                        dve.tensor_copy(dst, B[4 + g][:, 0:256]).then_inc(y_sb, 1)
                    else:
                        dve.tensor_tensor(dst, B[4 + g][:, 0:256], dst, ADD).then_inc(y_sb, 1)
            dve.wait_ge(y_sb, 8)
            yb = yab[:, :, WA:2 * WA].rearrange("p a (h d) -> p a h d", d=DH)
            w1 = xn[:, 0:2, 0:WA].rearrange("p a (h d) -> p a h d", d=DH)
            mean = hs[:, :, 8:16]
            link(dve.tensor_reduce(mean, yb, AX.X, ADD))
            link(dve.tensor_scalar(mean, mean, -1.0 / DH, None, MUL))
            for a in range(TT):
                link(dve.tensor_tensor(yb[:, a], yb[:, a], mean[:, a, :].unsqueeze(2).to_broadcast([P, HA, DH]), ADD))
                link(dve.tensor_tensor(w1[:, a], yb[:, a], yb[:, a], MUL))
            dve.tensor_reduce(hs[:, :, 0:8], w1, AX.X, ADD).then_inc(ln_sum, 1)
            dve.wait_ge(ln_std, 1)
            link(dve.reciprocal(hsr[:, :, 0:8], hsr[:, :, 0:8]))
            dve.wait_ge(gate_sb, 2)
            dve.wait_ge(vt_sb, 2)
            for a in range(TT):
                y1 = yab[:, a, WA:2 * WA]
                dve.tensor_tensor(w1[:, a], vtok[:, a, :].rearrange("p (h d) -> p h d", d=DH),
                                  bonus[:, a, :].unsqueeze(2).to_broadcast([P, HA, DH]), MUL)
                link(dve.tensor_tensor(yb[:, a], yb[:, a], hsr[:, a, 0:8].unsqueeze(2).to_broadcast([P, HA, DH]), MUL))
                link(dve.tensor_tensor(y1, y1, lnw_row, MUL))
                link(dve.tensor_tensor(y1, y1, lnb_row, ADD))
                link(dve.tensor_tensor(y1, y1, xn[:, a, 0:WA], ADD))
                link(dve.tensor_tensor(y1, y1, gate[:, a, :], MUL))
            dve.tensor_copy(bonus[:, 0, 0:1], hs[:, 0, 0:1]).then_inc(yab_rdy, 1)

            def residual(layer):
                for n in range(2):
                    for a in range(TT):
                        dve.wait_ge(o_ps, 4 * layer + 2 * n + a + 1)
                        v = x_sb[:, a, 512 * n:512 * n + 512]
                        last = dve.tensor_tensor(v, B[4 + 2 * n + a][:, :], v, ADD)
                    last.then_inc(x_rdy, 1)
                dve.wait_ge(x_rdy, 2 * layer + 2)

            residual(0)
            if UPTO >= 2:
                norm(1, "ev_ffn_norm")
                for i in range(FF // P):
                    dve.wait_ge(gu_act, i + 1)
                    if i >= 8 and i % 4 == 0:
                        dve.wait_ge(dn_ps, (i - 8) // 4 + 1)
                    dve.tensor_tensor(hf[:, i % 8, :], B[i % 3][:, SEQ:2 * SEQ], fsil[:, i % 3, :],
                                      MUL).then_inc(gu_sb, 1)
                residual(1)
            if UPTO >= 3:
                norm(2, "od_mix_norm")
                dve.wait_ge(ba_sb, 1)
                for a in range(TT):
                    link(dve.tensor_tensor(glog[:, a, :], alpha[:, a, :], dt_row, ADD))
                link(dve.tensor_scalar(gs, glog, -1.0, None, MUL))
                dve.tensor_tensor(gs, gs, glog, MAX).then_inc(sp_y, 1)
                dve.wait_ge(sp_l, 1)
                link(dve.scalar_tensor_tensor(glog, glog, 0.0, gs, MAX, ADD))
                for a in range(TT):
                    last = dve.scalar_tensor_tensor(glog[:, a, :], glog[:, a, :], -1.0, ea, MUL, MUL)
                last.then_inc(g_rdy, 1)
                dve.wait_ge(gc_ps, 1)
                dve.tensor_copy(gc.rearrange("p a n -> p (a n)"), B[7][:, 0:16])
                link(dve.tensor_copy(gl_.rearrange("p a n -> p (a n)"), B[7][:, 16:32]))
                dve.tensor_tensor(gt, gl_, gc, SUB).then_inc(gc_rdy, 1)
                dve.wait_ge(cv_sb, 6)
                flat = "p j s -> p (j s)"
                link(dve.tensor_tensor(cu.rearrange(flat), cbx[:, 4:8, :].rearrange(flat),
                                       cbx[:, 8:12, :].rearrange(flat), MUL))
                cc, cd = COL["od_conv_c"], COL["od_conv_dn"]

                def conv(dst, src, k, col, n):
                    shift_mix(dst, src, k, cols[:, col + n + k:col + n + k + 1], cols[:, col + k:col + k + 1],
                              cols[:, col + 2 * n + k:col + 2 * n + k + 1])

                for k in range(4):
                    conv(yTo, cu, k, cc, 4)
                dve.tensor_tensor(yTo[:, 0:4, :].rearrange(flat), yTo[:, 0:4, :].rearrange(flat),
                                  cbx[:, 0:4, :].rearrange(flat), MUL).then_inc(yc_rdy, 1)
                dve.wait_ge(cv_sb, 12)
                for i in range(3):
                    for k in range(4 * i, 4 * i + 4):
                        conv(qkvc, qkvr, k, cd, 12)
                    dve.tensor_copy(cntf, gt[:, 0, 0:1]).then_inc(conv_rdy, 1)
                for i in range(2):
                    dve.wait_ge(silu_rdy, i + 1)
                    v = qkvc[:, 4 * i:4 * i + 4, :].rearrange(flat)
                    dve.tensor_tensor(xn[:, i, :], v, v, MUL).then_inc(l2_sq, 1)
                dve.wait_ge(l2_std, 4)
                link(dve.reciprocal(xn[:, :, :], xn[:, :, :]))
                q2, k2 = qkvc[:, 0:4, :].rearrange(flat), qkvc[:, 4:8, :].rearrange(flat)
                dve.scalar_tensor_tensor(q2, q2, DHD ** -0.5, xn[:, 0, :], MUL, MUL)
                dve.tensor_tensor(k2, k2, xn[:, 1, :], MUL).then_inc(qk2_rdy, 1)
                for p in range(4, 6):
                    for g in range(2):
                        z, c = INV[p][g]
                        n = 2 * (p - 4) + g
                        dve.wait_ge(row_ps, n + 1)
                        rb = B[4 + g][:, :].rearrange("p (u s) -> p u s", u=4)
                        if p == 5 and g == 0:
                            dve.wait_ge(oo_ps, 2)
                            dve.wait_ge(am_rdy, inv_seq(4, NLEV - 1, 1))
                        for u in range(4):
                            col = gc[:, c, 4 * z + u:4 * z + u + 1]
                            dve.tensor_scalar(attn[g][:, u, :], rb[:, u, :], col, 0.0, SUB, MIN)
                            last = dve.tensor_scalar(Do[g][:, u, :], rb[:, u, :], col, 0.0, SUB, MAX)
                        last.then_inc(dd_rdy, 1)
                    for g in range(2):
                        z, c = INV[p][g]
                        n = 2 * (p - 4) + g
                        dve.wait_ge(dd_exp, n + 1)
                        dve.wait_ge(kk2_sb, 2)
                        for u in range(4):
                            last = dve.scalar_tensor_tensor(Ao[g][:, u, :], kkm[c][:, u, :],
                                                            beta[:, c, 4 * z + u:4 * z + u + 1], Do[g][:, u, :],
                                                            MUL, MUL)
                        last.then_inc(oa_rdy, 1)
                        link(dve.tensor_tensor(attn[g], attn[g], kqm[c], MUL))
                        link(dve.tensor_tensor(attn[g], attn[g],
                                               smask[:, z, 1, :].unsqueeze(1).to_broadcast([P, 4, P]), MUL))
                        if p == 5:
                            dve.tensor_tensor(qe[g], qe[g], qkvc[:, 0:4, P * c:P * c + P], MUL)
                            link(dve.tensor_tensor(ke[g], ke[g], qkvc[:, 4:8, P * c:P * c + P], MUL))
                    inv_adds(p)
                    for g in range(2):
                        z, c = INV[p][g]
                        n = 2 * (p - 4) + g
                        vt = vto[:, c, :].rearrange("p (u v) -> p u v", u=4)
                        bb = beta[:, c, 4 * z:4 * z + 4].unsqueeze(2).to_broadcast([P, 4, P])
                        dve.wait_ge(tk_sb, 4)
                        if p == 5:
                            dve.wait_ge(ks_ps, g + 1)
                            link(dve.tensor_tensor(Ro[g], vt, B[4 + g][:, :].rearrange("p (u s) -> p u s", u=4), SUB))
                            dve.tensor_tensor(Ro[g], Ro[g], bb, MUL).then_inc(or_rdy, 1)
                        else:
                            dve.tensor_tensor(Ro[g], vt, bb, MUL).then_inc(or_rdy, 1)
                    for g in range(2):
                        z, c = INV[p][g]
                        if p == 4:
                            dve.wait_ge(ou_sb, g + 1)
                            dve.wait_ge(ge_rdy, 1)
                            dve.tensor_tensor(qe[g], Uo[g], ge[:, c, 4 * z:4 * z + 4].unsqueeze(2).to_broadcast(
                                [P, 4, P]), MUL).then_inc(ous_rdy, 1)
                            dve.wait_ge(os_ps, g + 1)
                            dve.tensor_copy(S0o[z], B[g][:, :].rearrange("p (u s) -> p u s", u=4)).then_inc(os_sb, 1)
                    for g in range(2):
                        z, c = INV[p][g]
                        dve.wait_ge(oo_ps, 2 * (p - 4) + g + 1)
                        if p == 4:
                            dve.tensor_copy(osum[:, c, :], B[4 + g][:, :]).then_inc(oo_sb, 1)
                        else:
                            dve.tensor_tensor(osum[:, c, :], B[4 + g][:, :], osum[:, c, :], ADD).then_inc(oo_sb, 1)
                dve.wait_ge(oo_sb, 4)
                w2 = xn[:, :, 0:512]
                link(dve.tensor_tensor(w2, osum, osum, MUL))
                o4 = "p a (h d) -> p a h d"
                dve.tensor_reduce(hs[:, :, 0:4], w2.rearrange(o4, h=4), AX.X, ADD).then_inc(on_sum, 1)
                dve.wait_ge(on_std, 1)
                link(dve.reciprocal(hsr[:, :, 0:4], hsr[:, :, 0:4]))
                dve.wait_ge(z_sb, 2)
                link(dve.tensor_tensor(osum, osum, zt, MUL))
                for a in range(TT):
                    v = osum[:, a, :].rearrange("p (h d) -> p h d", h=4)
                    link(dve.tensor_tensor(v, v, hsr[:, a, 0:4].unsqueeze(2).to_broadcast([P, 4, P]), MUL))
                    last = dve.tensor_tensor(v, v, dn_row.unsqueeze(1).to_broadcast([P, 4, P]), MUL)
                last.then_inc(yd_rdy, 1)
                residual(2)
            if UPTO >= 4:
                norm(3, "od_ffn_norm")
                for e in range(NE):
                    dve.memset(ew[:, e:e + 1], float(NE - e))
                dve.wait_ge(rt_ps, 1)
                lg = B[7][:, 0:TT * NE].rearrange("p (a e) -> p a e", a=TT)
                link(dve.tensor_reduce(m1, lg, AX.X, MAX))
                dve.tensor_scalar(m2, m1, -1.0, None, MUL).then_inc(rt_max, 1)
                dve.wait_ge(rt_exp, 1)
                link(dve.reciprocal(esum, esum))
                link(dve.tensor_tensor(prob, prob, esum.unsqueeze(2).to_broadcast([P, TT, NE]), MUL))

                def best(src, m, oh):
                    link(dve.tensor_reduce(m, src, AX.X, MAX))
                    link(dve.tensor_tensor(esc, src, m.unsqueeze(2).to_broadcast([P, TT, NE]), ALU.is_equal))
                    link(dve.tensor_tensor(esc, esc, ew.unsqueeze(1).to_broadcast([P, TT, NE]), MUL))
                    link(dve.tensor_reduce(esum, esc, AX.X, MAX))
                    link(dve.tensor_tensor(oh, esc, esum.unsqueeze(2).to_broadcast([P, TT, NE]), ALU.is_equal))

                best(prob, m1, oh1)
                link(dve.scalar_tensor_tensor(gates, oh1, -2.0, prob, MUL, ADD))
                best(gates, m2, oh2)
                link(dve.tensor_tensor(esum, m1, m2, ADD))
                link(dve.reciprocal(esum, esum))
                link(dve.tensor_tensor(m1, m1, esum, MUL))
                link(dve.tensor_tensor(m2, m2, esum, MUL))
                link(dve.tensor_tensor(esc, oh1, m1.unsqueeze(2).to_broadcast([P, TT, NE]), MUL))
                link(dve.tensor_tensor(gates, oh2, m2.unsqueeze(2).to_broadcast([P, TT, NE]), MUL))
                link(dve.tensor_tensor(gates, gates, esc, ADD))
                dve.tensor_tensor(asg, oh1, oh2, ADD).then_inc(as_rdy, 1)
                dve.wait_ge(rank_ps, 1)
                link(dve.scalar_tensor_tensor(rank, B[6][:, 0:16].rearrange("p (a e) -> p a e", a=TT), 1.0, asg,
                                              ADD, MUL))
                link(dve.tensor_scalar(rank, rank, -1.0, None, ADD))
                link(dve.tensor_reduce(cntf, B[6][:, 16:24], AX.X, MAX))
                dve.tensor_scalar(flag[:, :], cntf, float(P), None, ALU.is_gt).then_inc(flag_rdy, 1)
                dve.memset(ang[:, 0, 0:1], 0.0).then_inc(cmb_sb, 1)
                fw = COL["od_ffn_norm"]

                def expert(ps, i):
                    b1, b2, b7 = NE * ps + 1, 2 * NE * ps + 1, NC_E * NE * ps + 1
                    for a in range(TT):
                        dve.tensor_scalar(sel[:, a, :], iot[:, :], rank[:, a, bass.ds(i, 1)], None, ALU.is_equal)
                        last = dve.tensor_scalar(selg[:, a, :], iot[:, :], rank[:, a, bass.ds(i, 1)],
                                                 gates[:, a, bass.ds(i, 1)], ALU.is_equal, MUL)
                    last.then_inc(sel_rdy, 1)
                    for r in range(2):
                        dve.wait_ge(xg_ps, i * 2 + b2 + r)
                        dve.tensor_tensor(xg[:, 4 * r:4 * r + 4, :], B[6 + r][:, :].rearrange("p (k s) -> p k s", k=4),
                                          cols[:, fw + 4 * r:fw + 4 * r + 4].unsqueeze(2).to_broadcast([P, 4, P]),
                                          MUL).then_inc(xg_sb, 1)
                    for j in range(NC_E):
                        dve.wait_ge(eg_act, i * NC_E + b7 + j)
                        dve.wait_ge(eu_ps, i * NC_E + b7 + j)
                        dve.tensor_tensor(ehr[:, j % 2, :], B[2 + j % 2][:, :], esil[:, j % 2, :],
                                          MUL).then_inc(eh_rdy, 1)
                    for q in range(4):
                        dve.wait_ge(cmb_ps, i * 4 + 4 * NE * ps + q + 1)
                        v = x_sb[:, q % 2, 512 * (q // 2):512 * (q // 2) + 512]
                        dve.tensor_tensor(v, B[q][:, :], v, ADD).then_inc(cmb_sb, 1)

                with dve.Fori(0, NE) as i:
                    expert(0, i)
                link(dve.tensor_scalar(rank, rank, float(P), None, SUB))
                dve.wait_ge(flag_rdy, 1)
                with dve.If(dve.value_load(flag[0:1, 0:1], min_val=0, max_val=1) > 0):
                    with dve.Fori(0, NE) as i:
                        expert(1, i)
                dve.memset(ang[:, 0, 0:1], 0.0).then_inc(x_rdy, 2)

        @block.tensor
        def _(pe):
            def weights(kind, n):
                s, _, cnt = where[kind, n]
                pe.wait_ge(landed[s], cnt)
                return ring[:, s * SLOT:(s + 1) * SLOT]

            def norm(ni):
                pe.wait_ge(xn_rdy, ni + 1)
                for k in range(KT):
                    for a in range(TT):
                        last = pe.transpose(B[k // 2][:, SEQ * (k % 2) + P * a:SEQ * (k % 2) + P * a + P],
                                            xn[:, a, P * k:P * k + P], ident[:, :])
                    if k % 2:
                        last.then_inc(xnT_ps, 1)
                pe.wait_ge(hT_act, ni + 1)
                pe.wait_ge(hT_dve, ni + 1)

            pe.wait_ge(pool_const, 1)
            pe.wait_ge(vec_in, 16 * len(VEC0 + VEC1))
            pe.transpose(B[7][:, 0:N0], vecrows[0:N0, 0, :], ident[0:N0, 0:N0])
            pe.transpose(B[7][:, P:P + N1], vecrows[0:N1, 1, :], ident[0:N1, 0:N1]).then_inc(vec_tp, 1)
            norm(0)
            pe.wait_ge(cols_rdy, 1)
            for n in range(3):
                w = weights("ev_in", n)
                w8 = w.rearrange("p (k n) -> p k n", k=KT)
                for a in range(TT):
                    for k in range(KT):
                        last = pe.matmul(B[2 * n + a][:, :], hT[:, k, P * a:P * a + P], w8[:, k, :],
                                         start=(k == 0), stop=(k == KT - 1))
                    last.then_inc(qkv_ps, 1)
            for n in range(3, 6):
                w = weights("ev_in", n)
                w8 = w.rearrange("p (k n) -> p k n", k=KT)
                for f in range(4):
                    m = (n - 3) * 2 + f // 2
                    if m >= 2 and f % 2 == 0:
                        pe.wait_ge(raw_sb, m - 1)
                    for k in range(KT):
                        last = pe.matmul(B[6 + m % 2][:, SEQ * (f % 2):SEQ * (f % 2) + SEQ],
                                         w8[:, k, P * f:P * f + P], hT[:, k, :], start=(k == 0), stop=(k == KT - 1))
                    if f % 2:
                        last.then_inc(raw_ps, 1)
            w = weights("lora1", 0)[:, 0:KT * 384].rearrange("p (k n) -> p k n", k=KT)
            pe.wait_ge(hx_rdy, 1)
            pe.wait_ge(qkv_sb, 6)
            for i in range(3):
                for k in range(KT):
                    last = pe.matmul(B[i][:, 0:SEQ], w[:, k, P * i:P * i + P],
                                     hxT[:, k, :], start=(k == 0), stop=(k == KT - 1))
                last.then_inc(lora_ps, 1)
            w = weights("lora2", 0)
            for m in range(16):
                i, z, j = m // 8, (m // 4) % 2, m % 4
                if m == 0 or m == 8:
                    pe.wait_ge(lora_sb, 1 + m // 8)
                if m >= 6 and m % 2 == 0:
                    pe.wait_ge(wa_sb, m - 4)
                r = slice(64 * z, 64 * z + 64)
                last = pe.matmul(B[3 + (m // 2) % 3][:, SEQ * (m % 2):SEQ * (m % 2) + SEQ],
                                 w[r, 512 * i + P * j:512 * i + P * j + P], lora[r, i, :], start=True, stop=True)
                if m % 2:
                    last.then_inc(wa_ps, 1)
            pe.wait_ge(lora_sb, 3)
            for a in range(TT):
                pe.matmul(B[a][:, :], lora[:, 2, P * a:P * a + P], w[:, 1024:1536],
                          start=True, stop=True).then_inc(gate_ps, 1)
            pe.wait_ge(qk_rdy, 1)
            pe.wait_ge(wa_sb, 16)
            pe.wait_ge(raw_sb, 6)
            for i in range(4):
                for jj in range(2):
                    for a in range(TT):
                        c0 = 512 * (i // 2) + P * (2 * (i % 2) + jj)
                        last = pe.transpose(B[4 + i][:, SEQ * jj + P * a:SEQ * jj + P * a + P],
                                            qkv[:, a, c0:c0 + P], ident[:, :])
                last.then_inc(qkT_ps, 1)
            pe.wait_ge(qkT_sb, 4)
            pe.wait_ge(gate_sb, 2)

            def scores(h):
                r = slice(64 * (h % 2), 64 * (h % 2) + 64)
                if h >= 2:
                    pe.wait_ge(att_m, h - 1)
                for a in range(TT):
                    last = pe.matmul(B[h % 2][:, SEQ * a:SEQ * a + SEQ], qT[r, h // 2, P * a:P * a + P],
                                     kTt[r, h // 2, :], start=True, stop=True)
                last.then_inc(att_s, 1)

            def values(h):
                pe.wait_ge(att_c, h + 1)
                for a in range(TT):
                    for b in range(TT):
                        last = pe.matmul(B[3 + 2 * a][:, DH * h:DH * h + DH],
                                         att_pT[:, h % 2, SEQ * a + P * b:SEQ * a + P * b + P],
                                         qkv[:, b, D + DH * h:D + DH * h + DH], start=(b == 0), stop=(b == TT - 1))
                last.then_inc(att_o, 1)

            scores(0)
            for h in range(HA):
                if h + 1 < HA:
                    scores(h + 1)
                if h:
                    values(h - 1)
                pe.wait_ge(att_e, h + 1)
                if h >= 2:
                    pe.wait_ge(att_c, h - 1)
                for a in range(TT):
                    for b in range(TT):
                        last = pe.transpose(B[2 + 2 * (h % 2)][:, SEQ * a + P * b:SEQ * a + P * b + P],
                                            sm_p[:, h % 2, SEQ * a + P * b:SEQ * a + P * b + P], ident[:, :])
                last.then_inc(att_t, 1)
            values(HA - 1)
            pe.wait_ge(mix_rdy, 1)
            for a in range(TT):
                for j in range(4):
                    last = pe.transpose(B[6 + a][:, P * j:P * j + P], mix[:, 8 + j, P * a:P * a + P], ident[:, :])
                last.then_inc(vt_ps, 1)
            pe.wait_ge(vt_sb, 2)
            pe.wait_ge(kk_sq, 1)
            for i in range(2):
                pe.matmul(B[6 + i][:, :], bones[:, :], Cw_f[:, 512 * i:512 * i + 512],
                          start=True, stop=True).then_inc(kk_ps, 1)
            pe.wait_ge(bon_rdy, 1)
            pe.wait_ge(ya_rdy, 1)
            for a in range(TT):
                for j in range(4):
                    last = pe.matmul(B[5][:, HA * a:HA * a + HA], Hw_f[:, SEQ * j + P * a:SEQ * j + P * a + P],
                                     head_ind[:, j, :], start=(j == 0), stop=(j == 3))
            last.then_inc(bon_ps, 1)

            def invert(p):
                Tm, Pm, Xm, Am = INVB[p]
                for g in range(2):
                    pe.wait_ge(t0_rdy, 2 * p + g + 1)
                    for u in range(4):
                        last = pe.transpose(B[2 + g][:, P * u:P * u + P], Tm[g][:, u, :], ident[:, :])
                    last.then_inc(p0_ps, 1)
                for lev in range(1, NLEV):
                    for g in range(2):
                        n = inv_seq(p, lev, g)
                        odd = INV[p][g][0] == 0
                        if lev == 1:
                            pe.wait_ge(p0_sb, 2 * p + g + 1)
                        else:
                            pe.wait_ge(tp_sb, n - 2)
                        pe.wait_ge(am_rdy, n)
                        pm = odd_even(Pm[g], lev, odd)
                        for u in range(4):
                            if lev < NLEV - 1:
                                o, i = B[g][:, P * u:P * u + P], Pm[g][:, u, :]
                            else:
                                o, i = B[g][:, P * u:P * u + 64], pm[:, u, 0, :]
                            last = pe.matmul(o, Am[g][:, u, :], i, start=True, stop=True)
                        last.then_inc(x_ps, 1)
                    for g in range(2):
                        n = inv_seq(p, lev, g)
                        odd = INV[p][g][0] == 0
                        pe.wait_ge(x_cp, n)
                        xm = odd_even(Xm[g], lev, odd)
                        tm = odd_even(Tm[g], lev, not odd)
                        for u in range(4):
                            last = pe.matmul(packed(B[2 + g], lev, 0)[:, u], Tm[g][:, u, :], xm[:, u],
                                             start=True, stop=True)
                            if lev < NLEV - 1:
                                last = pe.matmul(packed(B[2 + g], lev, 64)[:, u], Xm[g][:, u, :], tm[:, u],
                                                 start=True, stop=True)
                        last.then_inc(pt_ps, 1)

            pe.wait_ge(fac_rdy, 1)
            pe.wait_ge(bon_cp, 1)
            for p, (z, c) in enumerate(RW):
                if p < 2:
                    if p:
                        pe.wait_ge(u_sb, 2)
                    for i, f in enumerate((bF, kF)):
                        for j in range(4):
                            last = pe.transpose(B[6 + i][:, P * j:P * j + P], f[z][:, j, c, :], ident[:, :])
                        last.then_inc(tok_ps, 1)
                for i in range(8):
                    h, g = i, i // 4
                    r = slice(64 * (h % 2), 64 * (h % 2) + 64)
                    j = h // 2
                    n = 8 * p + i
                    if i >= 2:
                        pe.wait_ge(sc_sb, n - 1)
                    elif p:
                        pe.wait_ge(y_sb, 2 * p)
                    bank = B[4 + i % 2]
                    ar = arF[z][r, j, c].rearrange("p m s -> p (m s)")
                    pe.matmul(bank[:, 0:2 * P], kF[z][r, j, c, :], ar, start=True, stop=True)
                    pe.matmul(bank[:, 2 * P:3 * P], bF[z][r, j, c, :], arF[z][r, j, c, 1, :], start=True, stop=True)
                    pe.matmul(bank[:, 3 * P:4 * P], arF[z][r, j, c, 0, :], bF[z][r, j, c, :],
                              start=True, stop=True).then_inc(sc_ps, 1)
                invert(p)
                if p < 2:
                    pe.wait_ge(tok_sb, 2 * p + 2)
                else:
                    pe.wait_ge(s_sb, 2 * (p - 2) + 2)
                pe.wait_ge(sc_sb, 8 * p + 8)
                vv = vtok[:, c, :]
                for g in range(2):
                    for q in range(2):
                        j = 2 * g + q
                        if p >= 2:
                            pe.matmul(B[4 + g][:, P * q:P * q + P], arF[z][:, j, c, 0, :], S0[z][:, j, :],
                                      start=True, stop=False, skip_group_check=True)
                        for i in range(2):
                            u, h = 2 * q + i, 4 * g + 2 * q + i
                            last = pe.matmul(B[4 + g][:, DH * u:DH * u + DH], scg[g][:, u, 0, :],
                                             vv[:, DH * h:DH * h + DH], start=(p < 2), stop=True,
                                             skip_group_check=True)
                    last.then_inc(r_ps, 1)
                for g in range(2):
                    pe.wait_ge(r_sb, 2 * p + g + 1)
                    pe.wait_ge(tp_sb, inv_seq(p, NLEV - 1, g))
                    for u in range(4):
                        last = pe.matmul(B[6 + g][:, DH * u:DH * u + DH], Pm[g][:, u, :], Rm[g][:, u, :],
                                         start=True, stop=True)
                    last.then_inc(u_ps, 1)
                for g in range(2):
                    pe.wait_ge(u_sb, 2 * p + g + 1)
                    if p < 2:
                        for q in range(2):
                            j = 2 * g + q
                            o = B[g][:, P * q:P * q + P]
                            pe.matmul(o, tokbk[:, 0, j, :], Um[g][:, 2 * q:2 * q + 2, :].rearrange("p u v -> p (u v)"),
                                      start=True, stop=False)
                            last = pe.matmul(o, tokbk[:, 1, j, :], vv[:, P * j:P * j + P], start=False, stop=True)
                        last.then_inc(s_ps, 1)
                    for q in range(2):
                        j = 2 * g + q
                        if p >= 2:
                            pe.matmul(B[4 + g][:, P * q:P * q + P], arF[z][:, j, c, 1, :], S0[z][:, j, :],
                                      start=True, stop=False, skip_group_check=True)
                        for i in range(2):
                            u, h = 2 * q + i, 4 * g + 2 * q + i
                            o = B[4 + g][:, DH * u:DH * u + DH]
                            pe.matmul(o, scg[g][:, u, 1, :], vv[:, DH * h:DH * h + DH], start=(p < 2), stop=False,
                                      skip_group_check=True)
                            last = pe.matmul(o, scg[g][:, u, 2, :], Um[g][:, u, :], start=False, stop=True,
                                             skip_group_check=True)
                    last.then_inc(y_ps, 1)

            def out_projection(layer, kind):
                lhs = yT if layer == 0 else yTo
                for n in range(2):
                    w8 = weights(kind, n).rearrange("p (k n) -> p k n", k=KT)
                    for a in range(TT):
                        for k in range(KT):
                            last = pe.matmul(B[4 + 2 * n + a][:, :], lhs[:, k, P * a:P * a + P], w8[:, k, :],
                                             start=(k == 0), stop=(k == KT - 1))
                        last.then_inc(o_ps, 1)

            pe.wait_ge(yab_rdy, 1)
            for i in range(4):
                for jj in range(2):
                    for a in range(TT):
                        k = 2 * i + jj
                        last = pe.transpose(B[i][:, SEQ * jj + P * a:SEQ * jj + P * a + P],
                                            yab[:, a, P * k:P * k + P], ident[:, :])
                last.then_inc(yT_ps, 1)
            pe.wait_ge(yT_sb, 4)
            out_projection(0, "ev_out")
            if UPTO >= 2:
                norm(1)
                pe.wait_ge(x_rdy, 2)

                def ffn_down(m):
                    k = min(4, FF // P - 4 * m)
                    wd = weights("ffn_down", m)[:, 0:k * D].rearrange("p (k n) -> p k n", k=k)
                    pe.wait_ge(gu_sb, 4 * m + k)
                    end = m == FF // 512
                    for n in range(2):
                        for a in range(TT):
                            for f in range(k):
                                last = pe.matmul(B[4 + 2 * n + a][:, :], hf[:, (4 * m + f) % 8, P * a:P * a + P],
                                                 wd[:, f, 512 * n:512 * n + 512], start=(m == 0 and f == 0),
                                                 stop=(end and f == k - 1))
                            if end:
                                last.then_inc(o_ps, 1)
                    if not end:
                        last.then_inc(dn_ps, 1)

                for n in range(FF // 256):
                    w8 = weights("ffn_in", n).rearrange("p (k n) -> p k n", k=KT)
                    for f in range(2):
                        i = 2 * n + f
                        if i >= 3:
                            pe.wait_ge(gu_sb, i - 2)
                        for half in range(2):
                            for k in range(KT):
                                c0 = SEQ * half + P * f
                                last = pe.matmul(B[i % 3][:, SEQ * half:SEQ * half + SEQ], w8[:, k, c0:c0 + P],
                                                 hT[:, k, :], start=(k == 0), stop=(k == KT - 1))
                        last.then_inc(gu_ps, 1)
                    if n and n % 2 == 0:
                        ffn_down(n // 2 - 1)
                ffn_down(FF // 512)
            if UPTO >= 3:
                norm(2)
                pe.wait_ge(wsmall_in, 32)
                pe.wait_ge(x_rdy, 4)
                for a in range(TT):
                    for k in range(KT):
                        last = pe.matmul(B[6][:, 16 * a:16 * a + 16], hT[:, k, P * a:P * a + P], ba_w[:, k, :],
                                         start=(k == 0), stop=(k == KT - 1))
                last.then_inc(ba_ps, 1)
                for n in range(6):
                    w8 = weights("od_in", n).rearrange("p (k n) -> p k n", k=KT)
                    for f in range(4):
                        m = 2 * n + f // 2
                        if m >= 4 and f % 2 == 0:
                            pe.wait_ge(cv_sb, m - 3)
                        for k in range(KT):
                            last = pe.matmul(B[m % 4][:, SEQ * (f % 2):SEQ * (f % 2) + SEQ],
                                             w8[:, k, P * f:P * f + P], hT[:, k, :], start=(k == 0), stop=(k == KT - 1))
                        if f % 2:
                            last.then_inc(cv_ps, 1)
                w8 = weights("od_in", 6).rearrange("p (k n) -> p k n", k=KT)
                for a in range(TT):
                    for k in range(KT):
                        last = pe.matmul(B[4 + a][:, :], hT[:, k, P * a:P * a + P], w8[:, k, :],
                                         start=(k == 0), stop=(k == KT - 1))
                    last.then_inc(z_ps, 1)
                pe.wait_ge(g_rdy, 1)
                for c in range(TT):
                    for z in range(2):
                        pe.matmul(B[7][:, 8 * c + 4 * z:8 * c + 4 * z + 4], tri[:, 2 + z, :],
                                  glog[:, c, 4 * z:4 * z + 4], start=True, stop=True)
                    last = pe.matmul(B[7][:, 16 + 8 * c:24 + 8 * c], ones[:, :], glog[:, c, :], start=True, stop=True)
                last.then_inc(gc_ps, 1)
                pe.wait_ge(cv_sb, 12)
                for i in range(4):
                    pe.wait_ge(l2_sq, i // 2 + 1)
                    pe.matmul(B[i][:, :], ones[:, :], xn[:, i // 2, 512 * (i % 2):512 * (i % 2) + 512],
                              start=True, stop=True).then_inc(l2_ps, 1)
                pe.wait_ge(qk2_rdy, 1)
                pe.wait_ge(z_sb, 2)
                pe.wait_ge(gc_rdy, 1)
                for c in range(TT):
                    cs = slice(P * c, P * c + P)
                    for h in range(HD):
                        pe.matmul(B[c][:, P * h:P * h + P], qkvc[:, 4 + h, cs], qkvc[:, 4 + h, cs], start=True, stop=True)
                        last = pe.matmul(B[2 + c][:, P * h:P * h + P], qkvc[:, 4 + h, cs], qkvc[:, h, cs],
                                         start=True, stop=True)
                    last.then_inc(kk2_ps, 1)
                pe.wait_ge(silu_rdy, 3)
                for i in range(4):
                    for h in range(HD):
                        last = pe.transpose(B[4 + i][:, P * h:P * h + P],
                                            qkvc[:, 4 + 4 * (i // 2) + h, P * (i % 2):P * (i % 2) + P], ident[:, :])
                    last.then_inc(tk_ps, 1)
                pe.wait_ge(tk_sb, 4)
                for p in range(4, 6):
                    for g in range(2):
                        z, c = INV[p][g]
                        if p == 5:
                            pe.wait_ge(oo_sb, g + 1)
                        for u in range(4):
                            last = pe.matmul(B[4 + g][:, P * u:P * u + P],
                                             glog[:, c, 4 * z + u:4 * z + u + 1].to_broadcast([P, P]),
                                             tri[:, 2 + z, :], start=True, stop=True)
                        last.then_inc(row_ps, 1)
                    pe.wait_ge(os_sb if p == 5 else kk2_sb, 2)
                    invert(p)
                    if p == 5:
                        for g in range(2):
                            z, c = INV[p][g]
                            for u in range(4):
                                last = pe.matmul(B[4 + g][:, P * u:P * u + P], ke[g][:, u, :], S0o[z][:, u, :],
                                                 start=True, stop=True)
                            last.then_inc(ks_ps, 1)
                    for g in range(2):
                        pe.wait_ge(or_rdy, 2 * (p - 4) + g + 1)
                        pe.wait_ge(tp_sb, inv_seq(p, NLEV - 1, g))
                        for u in range(4):
                            last = pe.matmul(B[6 + g][:, P * u:P * u + P], INVB[p][1][g][:, u, :], Ro[g][:, u, :],
                                             start=True, stop=True)
                        last.then_inc(ou_ps, 1)
                    if p == 4:
                        for g in range(2):
                            z, c = INV[p][g]
                            pe.wait_ge(ous_rdy, g + 1)
                            for u in range(4):
                                last = pe.matmul(B[g][:, P * u:P * u + P], ktok[:, c, P * u:P * u + P],
                                                 qe[g][:, u, :], start=True, stop=True)
                            last.then_inc(os_ps, 1)
                    for g in range(2):
                        z, c = INV[p][g]
                        pe.wait_ge(ou_sb, 2 * (p - 4) + g + 1)
                        for u in range(4):
                            o = B[4 + g][:, P * u:P * u + P]
                            if p == 5:
                                pe.matmul(o, qe[g][:, u, :], S0o[z][:, u, :], start=True, stop=False)
                            last = pe.matmul(o, attn[g][:, u, :], Uo[g][:, u, :], start=(p == 4), stop=True)
                        last.then_inc(oo_ps, 1)
                pe.wait_ge(yd_rdy, 1)
                for i in range(2):
                    for jj in range(2):
                        for a in range(TT):
                            k = 2 * i + jj
                            last = pe.transpose(B[i][:, SEQ * jj + P * a:SEQ * jj + P * a + P],
                                                osum[:, a, P * k:P * k + P], ident[:, :])
                    last.then_inc(yd_ps, 1)
                pe.wait_ge(yd_sb, 2)
                pe.wait_ge(yc_rdy, 1)
                out_projection(2, "od_out")
            if UPTO >= 4:
                norm(3)
                pe.wait_ge(x_rdy, 6)
                for a in range(TT):
                    for k in range(KT):
                        last = pe.matmul(B[7][:, NE * a:NE * a + NE], hT[:, k, P * a:P * a + P], router_w[:, k, :],
                                         start=(k == 0), stop=(k == KT - 1))
                last.then_inc(rt_ps, 1)
                pe.wait_ge(as_rdy, 1)
                pe.matmul(B[6][:, 0:8], tri[:, 1, :], asg[:, 0, :], start=True, stop=True)
                pe.matmul(B[6][:, 8:16], tri[:, 1, :], asg[:, 1, :], start=True, stop=False)
                pe.matmul(B[6][:, 8:16], ones[:, :], asg[:, 0, :], start=False, stop=True)
                pe.matmul(B[6][:, 16:24], ones[:, :], asg[:, 0, :], start=True, stop=False)
                pe.matmul(B[6][:, 16:24], ones[:, :], asg[:, 1, :], start=False, stop=True).then_inc(rank_ps, 1)

                def expert(ps, i):
                    b1, b2, b7 = NE * ps + 1, 2 * NE * ps + 1, NC_E * NE * ps + 1

                    def arrived(r):
                        s = r % NSLOT
                        per = 16 * len(order) // NSLOT
                        pe.wait_ge(landed[s], i * per + (count[s] + per * NE * ps + 16 * (r // NSLOT + 1)))
                        return ring[:, s * SLOT:(s + 1) * SLOT]

                    pe.wait_ge(sel_rdy, i + b1)
                    pe.wait_ge(cmb_sb, i * 4 + (4 * NE * ps + 1))
                    for k in range(KT):
                        for a in range(TT):
                            last = pe.matmul(B[6 + k // 4][:, P * (k % 4):P * (k % 4) + P], xn[:, a, P * k:P * k + P],
                                             sel[:, a, :], start=(a == 0), stop=(a == TT - 1))
                        if k % 4 == 3:
                            last.then_inc(xg_ps, 1)
                    for a in range(TT):
                        last = pe.transpose(B[4][:, P * a:P * a + P], selg[:, a, :], ident[:, :])
                    last.then_inc(st_ps, 1)

                    def project(kind, j):
                        w8 = arrived(order.index((kind, j))).rearrange("p (k n) -> p k n", k=KT)
                        for k in range(KT):
                            if j == 0 and k % 4 == 0:
                                pe.wait_ge(xg_sb, i * 2 + b2 + k // 4)
                            last = pe.matmul(B[j % 2 + (0 if kind == "gate" else 2)][:, :], xg[:, k, :], w8[:, k, :],
                                             start=(k == 0), stop=(k == KT - 1))
                        last.then_inc(eg_ps if kind == "gate" else eu_ps, 1)

                    def turn(j):
                        pe.wait_ge(eh_rdy, i * NC_E + b7 + j)
                        for k in range(EC // P):
                            last = pe.transpose(B[6 + j % 2][:, P * k:P * k + P], ehr[:, j % 2, P * k:P * k + P],
                                                ident[:, :])
                        last.then_inc(ht_ps, 1)

                    def down(j):
                        wd = arrived(order.index(("down", j))).rearrange("p (k n) -> p k n", k=EC // P)
                        if j == 0:
                            pe.wait_ge(st_sb, i + b1)
                        pe.wait_ge(ht_sb, i * NC_E + b7 + j)
                        for n in range(2):
                            for k in range(EC // P):
                                last = pe.matmul(B[4 + n][:, :], ehT[:, j % 2, k, :], wd[:, k, 512 * n:512 * n + 512],
                                                 start=(j == 0 and k == 0), stop=(j == NC_E - 1 and k == EC // P - 1))
                        last.then_inc(ed_ps, 1)

                    for j in range(NC_E):
                        project("gate", j)
                        if j:
                            turn(j - 1)
                        project("up", j)
                        if j:
                            down(j - 1)
                    turn(NC_E - 1)
                    down(NC_E - 1)
                    for n in range(2):
                        pe.wait_ge(ey_sb, i * 2 + b2 + n)
                        for a in range(TT):
                            pe.matmul(B[2 * n + a][:, :], selgT[:, P * a:P * a + P], ysb[:, 512 * n:512 * n + 512],
                                      start=True, stop=True).then_inc(cmb_ps, 1)

                with pe.Fori(0, NE) as i:
                    expert(0, i)
                pe.wait_ge(flag_rdy, 1)
                with pe.If(pe.value_load(flag[0:1, 0:1], min_val=0, max_val=1) > 0):
                    with pe.Fori(0, NE) as i:
                        expert(1, i)


_INS = ["x", "positions", "ev_mix_norm", "ev_w_in", "ev_q_norm", "ev_k_norm", "ev_shift_mu", "ev_lora_mu", "ev_w0",
        "ev_w1", "ev_w2", "ev_a0", "ev_a1", "ev_a2", "ev_g1", "ev_g2", "ev_k_k", "ev_k_a", "ev_r_k", "ev_ln_w",
        "ev_ln_b", "ev_w_out", "ev_ffn_norm", "ev_ffn_gate", "ev_ffn_up", "ev_ffn_down", "od_mix_norm", "od_w_in",
        "od_conv_c", "od_conv_dn", "od_A_log", "od_dt_bias", "od_dn_norm", "od_w_out", "od_ffn_norm", "od_router",
        "od_moe_gate", "od_moe_up", "od_moe_down"]


def kernel(**inputs):
    import concourse.bacc as bacc
    from concourse.bass_utils import run_bass_kernel_spmd
    nc = bacc.Bacc("TRN2", target_bir_lowering=False, num_devices=1)
    arrays, aps = {}, {}
    for name in _INS:
        a = np.ascontiguousarray(inputs[name])
        arrays[f"in_{name}"] = a
        aps[name] = nc.dram_tensor(f"in_{name}", a.shape, mybir.dt.from_np(a.dtype), kind="ExternalInput").ap()
    out = nc.dram_tensor("out_x", (1, SEQ, D), F32, kind="ExternalOutput").ap()
    hybrid_trunk(nc, aps, out)
    r = run_bass_kernel_spmd(nc, [arrays], core_ids=[0])
    return r.results[0]["out_x"]
```

```python
import numpy as np
import concourse.bass as bass
from concourse import mybir
from contextlib import ExitStack

F32 = mybir.dt.float32
F32R = mybir.dt.float32r
I32 = mybir.dt.int32
ACT = mybir.ActivationFunctionType
ALU = mybir.AluOpType
AX = mybir.AxisListType
ADD, SUB, MUL, MAX, MIN = ALU.add, ALU.subtract, ALU.mult, ALU.max, ALU.min

P = 128
D = 1024
SEQ = 256
TT = SEQ // P
KT = D // P
HA, DH = 8, 64
WA = HA * DH
HD, DHD = 4, 128
WC = 512
FF = 2816
FE = 3584
NE = 8
ROPE_HALF = 8
NORM_EPS = 1e-6
L2_EPS = 1e-6
LN_EPS = 64e-5
NEG = -1e30
UPTO = 4

SLOT = 4096
NSTAT = 3
HALF = 2048
NHALF = 7
NSTAGE = 3
EC = 512
NC_E = FE // EC
NLEV = 7

VEC0 = [("ev_mix_norm", 8), ("ev_shift_mu", 24), ("ev_lora_mu", 16), ("ev_w0", 8), ("ev_a0", 8), ("ev_k_k", 4),
        ("ev_k_a", 4), ("ev_r_k", 4), ("ev_ffn_norm", 8), ("od_mix_norm", 8), ("od_ffn_norm", 8)]
VEC1 = [("od_conv_c", 12), ("od_conv_dn", 36)]


ACT_STEPS = {n: i + 1 for i, n in enumerate(
    "sin_rdy qk_std kk_std ln_std ba_sb sp_l ge_rdy on_std rt_exp".split())}
DVE_STEPS = {n: i + 1 for i, n in enumerate(
    ("red_rdy qk_sum qk_rdy mix_rdy ya_rdy kk_sq bon_rdy bon_cp fac_rdy ln_sum yab_rdy "
     "sp_y g_rdy gc_rdy yc_rdy qk2_rdy on_sum yd_rdy rt_max as_rdy").split())}


def layout():
    at, out = 0, {}
    for name, n in VEC0 + VEC1:
        out[name] = at
        at += n
    return out, at


def expert_chunks():
    out = []
    for j in range(NC_E):
        out += [("gate", j), ("up", j)]
        if j:
            out.append(("down", j - 1))
    return out + [("down", NC_E - 1)]


def static_chunks():
    out = [("ev_in", n, 1) for n in range(6)] + [("lora1", 0, 5), ("lora2", 0, 3)]
    out += [("ev_out", n, 1) for n in range(2)]
    if UPTO >= 2:
        for n in range(FF // 256):
            out.append(("ffn_in", n, 2))
            if n and n % 2 == 0:
                out.append(("ffn_down", n // 2 - 1, 1))
        out.append(("ffn_down", FF // 512, 1))
    if UPTO >= 3:
        out += [("od_in", n, 1) for n in range(7)] + [("od_out", n, 1) for n in range(2)]
    return out


def hybrid_trunk(nc, A, out):
    COL, NCOL = layout()
    N0 = sum(n for _, n in VEC0)
    N1 = sum(n for _, n in VEC1)
    chunks = static_chunks()
    before, count, where = [None] * NSTAT, [0] * NSTAT, {}
    for i, (kind, n, dmas) in enumerate(chunks):
        s = i % NSTAT
        count[s] += 16 * dmas
        where[kind, n] = (s, before[s], count[s])
        before[s] = (kind, n)
    order = [(kind, j, h) for kind, j in expert_chunks() for h in range(2)]
    PER = len(order)
    at_half = {k: r for r, k in enumerate(order)}

    ctx = ExitStack()
    with ctx:
        def sb(name, shape, dt=F32):
            return ctx.enter_context(nc.sbuf_tensor(name, shape, dt))

        def sem(name):
            return ctx.enter_context(nc.semaphore(name))

        ring = sb("ring", [P, NHALF * HALF])
        x_sb = sb("x_sb", [P, TT, D])
        xn = sb("xn", [P, TT, D])
        arena = sb("arena", [P, 11272])
        eps_col = sb("eps_col", [P, 2])
        router_w = sb("router_w", [P, KT, NE])
        ba_w = sb("ba_w", [P, KT, 16])
        flag = sb("flag", [P, 1], I32)
        vecrows = sb("vecrows", [P, 2, P])
        cols = sb("cols", [P, NCOL])
        cmix = sb("cmix", [P, 24])
        ident = sb("ident", [P, P])
        ones = sb("ones", [P, P])
        bones = sb("bones", [P, P])
        head_ind = sb("head_ind", [P, 4, HA])
        tri = sb("tri", [P, 4, P])
        smask = sb("smask", [P, 2, 4, P])
        levmask = sb("levmask", [P, 2, NLEV, P])
        iot = sb("iot", [P, P])
        iota_i = sb("iota_i", [P, P], I32)
        xor_i = sb("xor_i", [P, P], I32)
        rows = sb("rows", [P, 64 + 64 + 512 + 512 + 128 + 8 + 8])
        pos_i = sb("pos_i", [P, TT], I32)
        small = sb("small", [P, 768])

        BC_QN, BC_KN, BC_LW, BC_LB, BC_DN, BC_AL, BC_DT = np.cumsum([0, 64, 64, 512, 512, 128, 8]).tolist()
        qn_row, kn_row = rows[:, BC_QN:BC_QN + 64], rows[:, BC_KN:BC_KN + 64]
        lnw_row, lnb_row = rows[:, BC_LW:BC_LW + 512], rows[:, BC_LB:BC_LB + 512]
        dn_row = rows[:, BC_DN:BC_DN + 128]
        alog_row, dt_row = rows[:, BC_AL:BC_AL + 8], rows[:, BC_DT:BC_DT + 8]

        with nc.sbuf_tensor("scr", [P, NSTAGE * 2 * HALF + KT * SEQ], F32) as scr:
            pass
        split = sb("split", [P, NSTAGE * 2 * HALF + KT * SEQ], F32R)
        ehr_ = sb("ehr_", [P, 2 * 2 * 4 * P], F32R)
        wst = split[:, 0:NSTAGE * 2 * HALF].rearrange("p (b t n) -> p b t n", b=NSTAGE, t=2)
        xgs = split[:, NSTAGE * 2 * HALF:NSTAGE * 2 * HALF + KT * SEQ].rearrange("p (t k s) -> p t k s", t=2, k=KT)
        ehs = ehr_[:, :].rearrange("p (b t k s) -> p b t k s", b=2, t=2, k=4)
        hT = scr[:, NSTAGE * 2 * HALF:NSTAGE * 2 * HALF + KT * SEQ].rearrange("p (k s) -> p k s", k=KT)

        B = [ctx.enter_context(nc.psum_tensor(f"bank{i}", [P, 512], F32)) for i in range(8)]

        class Region:

            def __init__(self, base, at, size):
                self.base, self.at, self.end = base, at, at + size

            def take(self, *shape):
                n = int(np.prod(shape))
                assert self.at + n <= self.end, (self.at, n, self.end)
                v = self.base[:, self.at:self.at + n]
                self.at += n
                if len(shape) > 1:
                    names = "abcd"[:len(shape)]
                    spec = f"p ({' '.join(names)}) -> p {' '.join(names)}"
                    v = v.rearrange(spec, **dict(zip(names, shape)))
                return v

        sm = Region(small, 0, 768)
        ssq, std, rstd = sm.take(TT), sm.take(TT), sm.take(TT)
        cosT, sinT = sm.take(TT, ROPE_HALF), sm.take(TT, ROPE_HALF)
        ang, red, freq = sm.take(TT, ROPE_HALF), sm.take(TT, ROPE_HALF), sm.take(ROPE_HALF)
        posf = sm.take(TT)
        hs, hsr = sm.take(TT, 16), sm.take(TT, 16)
        mx, nmx, den = sm.take(TT, HA), sm.take(TT, HA), sm.take(TT, HA)
        bonus = sm.take(TT, HA)
        sfac = sm.take(2, 4)
        cmid, emid, eend, sscale = sm.take(HA), sm.take(HA), sm.take(HA), sm.take(HA)

        SCR0 = 0
        g_vtok = Region(scr, SCR0, 4096)
        vtok, gate = g_vtok.take(TT, WA), g_vtok.take(TT, WA)
        yab = g_vtok.take(TT, D)
        FZ = SCR0 + 4096
        g_f = Region(scr, FZ, 8192)
        qkv = g_f.take(TT, 3 * WA)
        qT, kTt = g_f.take(4, SEQ), g_f.take(4, SEQ)
        sm_s, sm_p, att_pT = g_f.take(2, 512), g_f.take(2, 512), g_f.take(2, 512)
        g_f2 = Region(scr, FZ, 8192)
        arF = [g_f2.take(4, TT, 2, P) for _ in range(2)]
        bF = [g_f2.take(4, TT, P) for _ in range(2)]
        kF = [g_f2.take(4, TT, P) for _ in range(2)]
        g_g = Region(arena, 0, 11272)
        raw, mix, hxT = g_g.take(12, SEQ), g_g.take(12, SEQ), g_g.take(KT, SEQ)
        sw, lora = g_g.take(2, 4, SEQ), g_g.take(3, SEQ)
        g_g2 = Region(arena, 0, 11272)
        ic, kk = g_g2.take(2, 4, SEQ), g_g2.take(4, SEQ)
        kd = hxT.rearrange("p (z j) s -> p z j s", z=2)
        g_g3 = Region(arena, 0, 11272)
        scg = [g_g3.take(4, 4, P) for _ in range(2)]
        Tm = [g_g3.take(4, P) for _ in range(2)]
        Pm = [g_g3.take(4, P) for _ in range(2)]
        Xm = [g_g3.take(4, P) for _ in range(2)]
        Am = [g_g3.take(4, P) for _ in range(2)]
        Rm = [g_g3.take(4, DH) for _ in range(2)]
        Um = [g_g3.take(4, DH) for _ in range(2)]
        tokbk = g_g3.take(2, 4, P)
        S0 = [g_g3.take(4, P) for _ in range(2)]
        Cw = xn[:, 0, :].rearrange("p (j c s) -> p j c s", j=4, c=TT)
        Ew = xn[:, 1, :].rearrange("p (j c s) -> p j c s", j=4, c=TT)
        Hw = hT[:, 0:4, :].rearrange("p j (c s) -> p j c s", c=TT)
        Cw_f, Ew_f = xn[:, 0, :], xn[:, 1, :]
        Hw_f = hT[:, 0:4, :].rearrange("p j s -> p (j s)")
        amask = yab[:, 1, WA:2 * WA]
        dist = arena[:, 0:512].bitcast(I32)
        bits = arena[:, 512:1024].bitcast(I32)
        mw1, mw2 = arena[:, 1024:1536], arena[:, 1536:2048]
        yT = arena[:, 0:KT * SEQ].rearrange("p (k s) -> p k s", k=KT)

        g_n = Region(arena, 2048, 9000)
        hf, fsil = g_n.take(8, SEQ), g_n.take(3, SEQ)
        g_o = Region(arena, 0, 11272)
        qkvr, qkvc, cbx = g_o.take(12, SEQ), g_o.take(12, SEQ), g_o.take(12, SEQ)
        cu, zt = g_o.take(4, SEQ), g_o.take(TT, 512)
        g_o2 = Region(arena, 0, 3072)
        Ao = [g_o2.take(4, P) for _ in range(2)]
        attn = [g_o2.take(4, P) for _ in range(2)]
        Do = [g_o2.take(4, P) for _ in range(2)]
        g_o3 = Region(arena, 6144, 4096)
        INVB = [(Tm, Pm, Xm, Am)] * 4 + [tuple([g_o3.take(4, P) for _ in range(2)] for _ in range(4))] * 2
        g_o4 = Region(scr, SCR0, NSTAGE * 2 * HALF)
        yTo, ktok, vto, osum = g_o4.take(KT, SEQ), g_o4.take(TT, 512), g_o4.take(TT, 512), g_o4.take(TT, 512)
        kkm = [g_o4.take(4, P) for _ in range(TT)]
        kqm = [g_o4.take(4, P) for _ in range(TT)]
        Ro = [g_o4.take(4, P) for _ in range(2)]
        Uo = [g_o4.take(4, P) for _ in range(2)]
        S0o = [g_o4.take(4, P) for _ in range(2)]
        qe = [g_o4.take(4, P) for _ in range(2)]
        ke = [g_o4.take(4, P) for _ in range(2)]
        beta, alpha, gl_, gc = sm.take(TT, 8), sm.take(TT, 8), sm.take(TT, 8), sm.take(TT, 8)
        gt, gs, ea, ge = sm.take(TT, 8), sm.take(TT, 8), sm.take(8), sm.take(TT, 8)
        glog = sm.take(TT, 8)
        g_e = Region(arena, 0, 11272)
        xg = g_e.take(KT, P)
        esil, ehr = g_e.take(2, 512), g_e.take(2, 512)
        ysb, sel, selg, selgT = g_e.take(D), g_e.take(TT, P), g_e.take(TT, P), g_e.take(TT * P)
        prob, oh1, oh2, esc = sm.take(TT, NE), sm.take(TT, NE), sm.take(TT, NE), sm.take(TT, NE)
        gates_ext, rank_ext = sm.take(TT, NE + 1), sm.take(TT, NE + 1)
        gates, rank = gates_ext[:, :, 0:NE], rank_ext[:, :, 0:NE]
        asg, ew = sm.take(TT, NE), sm.take(NE)
        m1, m2, esum = sm.take(TT), sm.take(TT), sm.take(TT)
        cntf = sm.take(1)

        landed = [sem(f"landed{i}") for i in range(NSTAT)]
        landed_e = [sem(f"landed_e{i}") for i in range(NHALF)]
        x_in = sem("x_in")
        vec_in = sem("vec_in")
        rows_in = sem("rows_in")
        pos_in = sem("pos_in")
        stored = sem("stored")
        sp_pace = sem("sp_pace")
        act_step = sem("act_step")
        dve_step = sem("dve_step")
        dve_chain = sem("dve_chain")
        act_chain = sem("act_chain")
        pool_chain = sem("pool_chain")
        pool_const = sem("pool_const")
        dve_const = sem("dve_const")
        vec_tp = sem("vec_tp")
        cols_rdy = sem("cols_rdy")
        std_rdy = sem("std_rdy")
        xn_rdy = sem("xn_rdy")
        xnT_ps = sem("xnT_ps")
        hT_act = sem("hT_act")
        hT_dve = sem("hT_dve")
        x_rdy = sem("x_rdy")
        qkv_ps = sem("qkv_ps")
        qkv_sb = sem("qkv_sb")
        raw_ps = sem("raw_ps")
        raw_sb = sem("raw_sb")
        hx_rdy = sem("hx_rdy")
        lora_ps = sem("lora_ps")
        lora_sb = sem("lora_sb")
        wa_ps = sem("wa_ps")
        wa_sb = sem("wa_sb")
        gate_ps = sem("gate_ps")
        gate_sb = sem("gate_sb")
        vt_ps = sem("vt_ps")
        vt_sb = sem("vt_sb")
        kk_ps = sem("kk_ps")
        bon_ps = sem("bon_ps")
        qkT_ps = sem("qkT_ps")
        qkT_sb = sem("qkT_sb")
        att_s = sem("att_s")
        att_m = sem("att_m")
        att_e = sem("att_e")
        att_t = sem("att_t")
        att_c = sem("att_c")
        att_o = sem("att_o")
        dec_c = sem("dec_c")
        dec_e = sem("dec_e")
        tok_ps = sem("tok_ps")
        tok_sb = sem("tok_sb")
        sc_ps = sem("sc_ps")
        sc_sb = sem("sc_sb")
        t0_rdy = sem("t0_rdy")
        p0_ps = sem("p0_ps")
        p0_sb = sem("p0_sb")
        am_rdy = sem("am_rdy")
        x_ps = sem("x_ps")
        x_cp = sem("x_cp")
        pt_ps = sem("pt_ps")
        tp_sb = sem("tp_sb")
        r_ps = sem("r_ps")
        r_sb = sem("r_sb")
        u_ps = sem("u_ps")
        u_sb = sem("u_sb")
        y_ps = sem("y_ps")
        y_sb = sem("y_sb")
        s_ps = sem("s_ps")
        s_sb = sem("s_sb")
        yT_ps = sem("yT_ps")
        yT_sb = sem("yT_sb")
        o_ps = sem("o_ps")
        gu_ps = sem("gu_ps")
        gu_act = sem("gu_act")
        gu_sb = sem("gu_sb")
        dn_ps = sem("dn_ps")
        cv_ps = sem("cv_ps")
        mask_rdy = sem("mask_rdy")
        wsmall_in, cv_sb, z_ps, z_sb, ba_ps = (sem(n) for n in (
            "wsmall_in", "cv_sb", "z_ps", "z_sb", "ba_ps"))
        gc_ps = sem("gc_ps")
        conv_rdy, silu_rdy, l2_sq, l2_ps, l2_std = (sem(n) for n in (
            "conv_rdy", "silu_rdy", "l2_sq", "l2_ps", "l2_std"))
        kk2_ps, kk2_sb, tk_ps, tk_sb = (sem(n) for n in ("kk2_ps", "kk2_sb", "tk_ps", "tk_sb"))
        row_ps, dd_rdy, dd_exp, oa_rdy = (sem(n) for n in ("row_ps", "dd_rdy", "dd_exp", "oa_rdy"))
        ks_ps, or_rdy, ou_ps, ou_sb, ous_rdy, os_ps, os_sb, oo_ps, oo_sb = (sem(n) for n in (
            "ks_ps", "or_rdy", "ou_ps", "ou_sb", "ous_rdy", "os_ps", "os_sb", "oo_ps", "oo_sb"))
        yd_ps, yd_sb = (sem(n) for n in (
            "yd_ps", "yd_sb"))
        rt_ps, rank_ps, flag_rdy = (sem(n) for n in (
            "rt_ps", "rank_ps", "flag_rdy"))
        sel_rdy, xg_ps, xg_sb, st_ps, st_sb = (sem(n) for n in ("sel_rdy", "xg_ps", "xg_sb", "st_ps", "st_sb"))
        w_hi, w_lo, half_ps, x_hi, x_lo = (sem(n) for n in ("w_hi", "w_lo", "half_ps", "x_hi", "x_lo"))
        eg_act, eh_rdy, ht_ps, ht_hi, ht_lo = (sem(n) for n in ("eg_act", "eh_rdy", "ht_ps", "ht_hi", "ht_lo"))
        ey_sb, cmb_ps, cmb_sb = (sem(n) for n in ("ey_sb", "cmb_ps", "cmb_sb"))


        def odd_even(m, lev, odd):
            b = 1 << lev
            return m.rearrange("p u (k two b) -> p u k two b", two=2, b=b)[:, :, :, 1 if odd else 0, :]

        def packed(bank, lev, at):
            b = 1 << lev
            return bank[:, :].rearrange("p (u w) -> p u w", u=4)[:, :, at:at + 64].rearrange(
                "p u (k b) -> p u k b", b=b)

        RW = [(0, 0), (1, 1), (0, 1), (1, 0)]
        INV = [[(z, c), (z, c)] for z, c in RW] + [[(0, 0), (1, 1)], [(0, 1), (1, 0)]]

        def inv_seq(p, lev, g):
            return (p * (NLEV - 1) + lev - 1) * 2 + g + 1

        def used_up(kind, n):
            return {"ev_in": (qkv_ps, 2 * n + 2) if n < 3 else (raw_ps, 2 * (n - 3) + 2), "lora1": (lora_ps, 3),
                    "lora2": (gate_ps, 2), "ev_out": (o_ps, 2 * n + 2), "ffn_in": (gu_ps, 2 * n + 2),
                    "ffn_down": (dn_ps, n + 1) if n < FF // 512 else (o_ps, 8),
                    "od_in": (cv_ps, 2 * n + 2) if n < 6 else (z_ps, 2), "od_out": (o_ps, 8 + 2 * n + 2)}[kind]

        duties = {r: [] for r in range(PER + 1)}
        duties[3].append(("tokens", 0))
        for j in range(NC_E):
            g1, u1 = at_half["gate", j, 1], at_half["up", j, 1]
            duties[g1 + 3].append(("silu", j))
            duties[u1 + 3].append(("product", j))
            duties[at_half["gate", j + 1, 1] + 3 if j + 1 < NC_E else PER].append(("turned", j))

        def used_half(i, ps, r):
            return i * PER + (NE * PER * ps + NSTAGE + r + 1)

        block = ctx.enter_context(nc.Block())

        @block.sync
        def _(sp):
            def load(kind, n):
                s, prev, _ = where[kind, n]
                if prev:
                    sp.wait_ge(*used_up(*prev))
                v = ring[:, s * SLOT:(s + 1) * SLOT]
                v8 = v.rearrange("p (k n) -> p k n", k=KT)
                kt = "o (k p) n -> p (o k) n"
                if kind == "ev_in":
                    parts = [(v8, A["ev_w_in"][:, :, 512 * n:512 * n + 512].rearrange(kt, p=P))]
                elif kind == "lora1":
                    w = v[:, 0:KT * 384].rearrange("p (k n) -> p k n", k=KT)
                    parts = [(w[:, :, 64 * z:64 * z + 64], A["ev_w1"][:, z].rearrange(kt, p=P)) for z in range(2)]
                    parts += [(w[:, :, 128 + 64 * z:192 + 64 * z], A["ev_a1"][:, z].rearrange(kt, p=P)) for z in range(2)]
                    parts += [(w[:, :, 256:384], A["ev_g1"].rearrange(kt, p=P))]
                elif kind == "lora2":
                    parts = [(v[:, 0:512], A["ev_w2"].rearrange("o z r c -> (o z r) c")),
                             (v[:, 512:1024], A["ev_a2"].rearrange("o z r c -> (o z r) c")),
                             (v[:, 1024:1536], A["ev_g2"].rearrange("o r c -> (o r) c"))]
                elif kind in ("ev_out", "od_out"):
                    w = A["ev_w_out" if kind == "ev_out" else "od_w_out"]
                    parts = [(v8, w[:, :, 512 * n:512 * n + 512].rearrange(kt, p=P))]
                elif kind == "ffn_in":
                    parts = [(v8[:, :, 256 * i:256 * i + 256],
                              A[w][:, :, 256 * n:256 * n + 256].rearrange(kt, p=P))
                             for i, w in enumerate(("ev_ffn_gate", "ev_ffn_up"))]
                elif kind == "ffn_down":
                    k = min(4, FF // P - 4 * n)
                    parts = [(v[:, 0:k * D].rearrange("p (k n) -> p k n", k=k),
                              A["ev_ffn_down"][:, 512 * n:512 * n + k * P, :].rearrange(kt, p=P))]
                elif kind == "od_in":
                    parts = [(v8, A["od_w_in"][:, :, 512 * n:512 * n + 512].rearrange(kt, p=P))]
                for dst, src in parts:
                    sp.dma_start(dst, src).then_inc(landed[s], 16)

            sp.dma_start(x_sb[:, :, :], A["x"].rearrange("b (a p) n -> p (b a) n", p=P)).then_inc(x_in, 16)
            for r0, vecs, t in ((0, VEC0, 0), (N0, VEC1, 1)):
                for name, n in vecs:
                    a = A[name]
                    if name == "ev_r_k":
                        src = a.rearrange("o (t h) d -> (o t) (h d)", h=2)
                    elif len(a.shape) == 2:
                        src = a.rearrange("o (t p) -> (o t) p", p=P)
                    else:
                        src = a.rearrange("o m (t p) -> (o m t) p", p=P)
                    r = COL[name] - r0
                    sp.dma_start(vecrows[r:r + n, t, :], src).then_inc(vec_in, 16)
            load(*chunks[0][:2])
            sp.dma_start(pos_i[:, :], A["positions"].rearrange("b (a p) -> p (b a)", p=P),
                         allow_slow_non_contiguous=True).then_inc(pos_in, 16)
            for name, at, n in (("ev_q_norm", BC_QN, 64), ("ev_k_norm", BC_KN, 64), ("ev_ln_w", BC_LW, 512),
                                ("ev_ln_b", BC_LB, 512), ("od_dn_norm", BC_DN, 128)):
                sp.dma_start(rows[:, at:at + n], A[name].to_broadcast([P, n])).then_inc(rows_in, 16)
            for name, at in (("od_A_log", BC_AL), ("od_dt_bias", BC_DT)):
                sp.dma_start(rows[:, at:at + 8],
                             A[name].rearrange("o z h -> o (z h)").to_broadcast([P, 8])).then_inc(rows_in, 16)
            if UPTO >= 3:
                sp.dma_start(ba_w[:, :, :], A["od_w_in"][:, :, 7 * 512:7 * 512 + 16].rearrange(
                    "o (k p) n -> p (o k) n", p=P)).then_inc(wsmall_in, 16)
                sp.dma_start(router_w[:, :, :], A["od_router"].rearrange(
                    "o (k p) n -> p (o k) n", p=P)).then_inc(wsmall_in, 16)
            for kind, n, _ in chunks[1:]:
                load(kind, n)
            if UPTO >= 4:
                wg, wu, wd = (A[n][0] for n in ("od_moe_gate", "od_moe_up", "od_moe_down"))

                def expert_load(e, r):
                    kind, j, h = order[r]
                    v = ring[:, (r % NHALF) * HALF:(r % NHALF + 1) * HALF]
                    if kind == "down":
                        f0 = EC * j + EC // 2 * h
                        src = wd[e, f0:f0 + EC // 2, :].rearrange("o (k p) n -> p (o k) n", p=P)
                        v = v.rearrange("p (k n) -> p k n", k=EC // P // 2)
                    else:
                        src = (wg if kind == "gate" else wu)[e, D // 2 * h:D // 2 * h + D // 2,
                                                             EC * j:EC * j + EC].rearrange("o (k p) n -> p (o k) n", p=P)
                        v = v.rearrange("p (k n) -> p k n", k=KT // 2)
                    sp.dma_start(v, src).then_inc(landed_e[r % NHALF], 16)

                def expert_pass(ps):
                    for r in range(NHALF):
                        if ps:
                            sp.wait_ge(w_lo, NE * PER * ps - NHALF + r + 1)
                        elif r < 2 * NSTAT:
                            sp.wait_ge(*used_up(*before[r // 2]))
                        expert_load(slice(0, 1), r)
                    with sp.Fori(0, NE - 1) as i:
                        for r in range(NHALF, PER + NHALF):
                            sp.wait_ge(w_lo, i * PER + (NE * PER * ps + r - NHALF + 1))
                            if order[r % PER][1:] == (0, 0):
                                sp.sem_inc(sp_pace, 1)
                            expert_load(bass.ds(i + 1 if r >= PER else i, 1), r % PER)
                    for r in range(NHALF, PER):
                        sp.wait_ge(w_lo, (NE - 1) * PER + NE * PER * ps + r - NHALF + 1)
                        expert_load(slice(NE - 1, NE), r)

                expert_pass(0)
                sp.wait_ge(flag_rdy, 1)
                with sp.If(sp.value_load(flag[0:1, 0:1], min_val=0, max_val=1) > 0):
                    expert_pass(1)
            sp.wait_ge(x_rdy, 2 * UPTO)
            sp.dma_start(out.rearrange("b (a p) n -> p (b a) n", p=P), x_sb[:, :, :]).then_inc(stored, 16)
            sp.wait_ge(stored, 16)

        @block.gpsimd
        def _(pool):
            chain = [0]

            def link(ins):
                chain[0] += 1
                ins.then_inc(pool_chain, 1)
                pool.wait_ge(pool_chain, chain[0])

            link(pool.memset(ident[:, :], 0.0))
            link(pool.affine_select(out=ident[:, :], in_=ident[:, :], compare_op=ALU.not_equal, fill=1.0, base=0,
                                    pattern=[[-1, P]], channel_multiplier=1))
            link(pool.memset(ones[:, :], 1.0))
            pool.iota(iot[:, :], pattern=[[1, P]], base=0, channel_multiplier=0,
                      allow_small_or_imprecise_dtypes=True)
            pool.iota(iota_i[:, :], pattern=[[1, P]], base=0, channel_multiplier=0)
            for a in range(TT):
                pool.iota(dist[:, SEQ * a:SEQ * a + SEQ], pattern=[[-1, SEQ]], base=SEQ + P * a, channel_multiplier=1)
            link(pool.iota(xor_i[:, :], pattern=[[0, P]], base=0, channel_multiplier=1))
            pool.affine_select(out=tri[:, 0, :], in_=ones[:, :], compare_op=ALU.is_gt, fill=0.0, base=0,
                               pattern=[[-1, P]], channel_multiplier=1)
            pool.affine_select(out=tri[:, 1, :], in_=ones[:, :], compare_op=ALU.is_gt, fill=0.0, base=0,
                               pattern=[[1, P]], channel_multiplier=-1)
            pool.affine_select(out=tri[:, 2, :], in_=ones[:, :], compare_op=ALU.is_ge, fill=0.0, base=0,
                               pattern=[[1, P]], channel_multiplier=-1)
            pool.affine_select(out=tri[:, 3, :], in_=ones[:, :], compare_op=ALU.is_ge, fill=0.0, base=0,
                               pattern=[[-1, P]], channel_multiplier=1)
            link(pool.memset(bones[:, :], 0.0))
            link(pool.memset(head_ind[:, :, :], 0.0))
            link(pool.memset(bones[0:64, 0:64], 1.0))
            link(pool.memset(bones[64:128, 64:128], 1.0))
            for j in range(4):
                link(pool.memset(head_ind[0:64, j, 2 * j:2 * j + 1], 1.0))
                link(pool.memset(head_ind[64:128, j, 2 * j + 1:2 * j + 2], 1.0))
            for z in range(2):
                s, i = (1, 2) if z == 0 else (0, 3)
                pool.tensor_copy(smask[:, z, 0, :], tri[:, s, :])
                pool.tensor_copy(smask[:, z, 1, :], tri[:, i, :])
                pool.tensor_copy(smask[:, z, 2, :], tri[:, i, :])
                last = pool.tensor_copy(smask[:, z, 3, :], tri[:, 1 - s, :])
            last.then_inc(pool_const, 1)

            def invert(p, mats):
                for g in range(2):
                    z = INV[p][g][0]
                    pool.wait_ge(*mats[g][1])
                    if p:
                        pool.wait_ge(pt_ps, inv_seq(p - 1, NLEV - 1, g))
                    m0 = levmask[:, z, 0, :].unsqueeze(1).to_broadcast([P, 4, P])
                    Tm, Am = INVB[p][0], INVB[p][3]
                    link(pool.tensor_tensor(Tm[g], mats[g][0], m0, MUL))
                    pool.tensor_tensor(Tm[g], Tm[g], ident[:, :].unsqueeze(1).to_broadcast([P, 4, P]),
                                       ADD).then_inc(t0_rdy, 1)
                for lev in range(1, NLEV):
                    for g in range(2):
                        z = INV[p][g][0]
                        if lev > 1:
                            pool.wait_ge(x_ps, inv_seq(p, lev - 1, g))
                        m = levmask[:, z, lev, :].unsqueeze(1).to_broadcast([P, 4, P])
                        pool.tensor_tensor(Am[g], mats[g][0], m, MUL).then_inc(am_rdy, 1)

            pool.wait_ge(dve_const, 1)
            for p in range(4):
                invert(p, [(scg[g][:, :, 3, :], (sc_sb, 8 * p + 4 * g + 4)) for g in range(2)])
            if UPTO >= 3:
                for p in range(4, 6):
                    invert(p, [(Ao[g], (oa_rdy, 2 * (p - 4) + g + 1)) for g in range(2)])

        @block.scalar
        def _(act):
            chain = [0]

            def link(ins):
                chain[0] += 1
                ins.then_inc(act_chain, 1)
                act.wait_ge(act_chain, chain[0])

            def norm(ni, name):
                if ni == 0:
                    act.wait_ge(x_in, 16)
                else:
                    act.wait_ge(x_rdy, 2 * ni)
                act.activation(xn[:, 0, :], x_sb[:, 0, :], ACT.Square, accum_out=ssq[:, 0:1])
                link(act.activation(xn[:, 1, :], x_sb[:, 1, :], ACT.Square, accum_out=ssq[:, 1:2]))
                act.activation(std, ssq, ACT.Sqrt, scale=1.0 / D, bias=eps_col[:, 0:1]).then_inc(std_rdy, 1)
                if ni == 0:
                    act.wait_ge(cols_rdy, 1)
                for k in range(KT // 2):
                    act.wait_ge(xnT_ps, 4 * ni + k // 2 + 1)
                    last = act.activation(hT[:, k, :], B[k // 2][:, SEQ * (k % 2):SEQ * (k % 2) + SEQ], ACT.Copy,
                                          scale=cols[:, COL[name] + k:COL[name] + k + 1])
                last.then_inc(hT_act, 1)

            act.wait_ge(dve_const, 1)
            norm(0, "ev_mix_norm")
            for i in range(6):
                act.wait_ge(qkv_ps, i + 1)
                act.activation(qkv[:, i % 2, 512 * (i // 2):512 * (i // 2) + 512], B[i][:, :],
                               ACT.Copy).then_inc(qkv_sb, 1)
            act.wait_ge(dve_step, DVE_STEPS["red_rdy"])
            act.activation(sinT, red, ACT.Sin)
            act.activation(cosT, ang, ACT.Sin).then_inc(act_step, 1)
            act.wait_ge(dve_step, DVE_STEPS["qk_sum"])
            act.activation(hsr, hs, ACT.Sqrt, scale=1.0 / DH, bias=eps_col[:, 0:1]).then_inc(act_step, 1)
            act.wait_ge(mask_rdy, 1)
            for m in range(6):
                act.wait_ge(raw_ps, m + 1)
                act.activation(raw[:, 2 * m:2 * m + 2, :], B[6 + m % 2][:, :].rearrange("p (t s) -> p t s", t=2),
                               ACT.Copy).then_inc(raw_sb, 1)
            for i, f in enumerate((ACT.Tanh, ACT.Copy, ACT.Sigmoid)):
                act.wait_ge(lora_ps, i + 1)
                act.activation(lora[:, i, :], B[i][:, 0:SEQ], f).then_inc(lora_sb, 1)
            for i in range(2):
                if i:
                    act.wait_ge(dve_step, DVE_STEPS["mix_rdy"])
                for z in range(2):
                    for j in range(4):
                        m = i * 8 + z * 4 + j
                        act.wait_ge(wa_ps, m // 2 + 1)
                        b = COL["ev_w0" if i == 0 else "ev_a0"] + 4 * z + j
                        src = B[3 + (m // 2) % 3][:, SEQ * (m % 2):SEQ * (m % 2) + SEQ]
                        act.activation((sw, ic)[i][:, z, j, :], src, ACT.Sigmoid,
                                       bias=cols[:, b:b + 1]).then_inc(wa_sb, 1)
            for a in range(TT):
                act.wait_ge(gate_ps, a + 1)
                act.activation(gate[:, a, :], B[a][:, :], ACT.Copy).then_inc(gate_sb, 1)
            for i in range(4):
                act.wait_ge(qkT_ps, i + 1)
                dst = (qT, kTt)[i // 2][:, 2 * (i % 2):2 * (i % 2) + 2, :]
                act.activation(dst, B[4 + i][:, :].rearrange("p (j s) -> p j s", j=2), ACT.Copy).then_inc(qkT_sb, 1)
            for h in range(HA):
                act.wait_ge(att_m, h + 1)
                for a in range(TT):
                    last = act.activation(sm_p[:, h % 2, SEQ * a:SEQ * a + SEQ], sm_s[:, h % 2, SEQ * a:SEQ * a + SEQ],
                                          ACT.Exp, bias=nmx[:, a, h:h + 1], accum_out=den[:, a, h:h + 1])
                last.then_inc(att_e, 1)
                act.wait_ge(att_t, h + 1)
                act.activation(att_pT[:, h % 2, :], B[2 + 2 * (h % 2)][:, :], ACT.Copy).then_inc(att_c, 1)
            act.wait_ge(kk_ps, 2)
            for i in range(2):
                last = act.activation(Ew_f[:, 512 * i:512 * i + 512], B[6 + i][:, :], ACT.Sqrt, bias=eps_col[:, 0:1])
            last.then_inc(act_step, 1)
            for z in range(2):
                act.wait_ge(dec_c, z + 1)
                act.activation(Ew, Cw, ACT.Exp, scale=-1.0)
                act.activation(emid, cmid, ACT.Exp)
                act.activation(eend, sscale, ACT.Exp)
                link(act.activation(Cw, Cw, ACT.Exp))
                act.activation(Hw, Hw, ACT.Exp).then_inc(dec_e, 1)

            def inv_copies(p):
                Pm, Xm = INVB[p][1], INVB[p][2]
                for g in range(2):
                    act.wait_ge(p0_ps, 2 * p + g + 1)
                    act.activation(Pm[g], B[2 + g][:, :].rearrange("p (u s) -> p u s", u=4),
                                   ACT.Copy).then_inc(p0_sb, 1)
                for lev in range(1, NLEV):
                    for g in range(2):
                        n = inv_seq(p, lev, g)
                        act.wait_ge(x_ps, n)
                        if lev < NLEV - 1:
                            act.activation(Xm[g], B[g][:, :].rearrange("p (u s) -> p u s", u=4),
                                           ACT.Copy).then_inc(x_cp, 1)
                        else:
                            odd = INV[p][g][0] == 0
                            act.activation(odd_even(Xm[g], lev, odd)[:, :, 0, :], packed(B[g], lev, 0)[:, :, 0, :],
                                           ACT.Copy).then_inc(x_cp, 1)

            for p, (z, c) in enumerate(RW):
                first = p < 2
                if first:
                    for i in range(2):
                        act.wait_ge(tok_ps, 2 * p + i + 1)
                        act.activation(tokbk[:, i, :, :], B[6 + i][:, :].rearrange("p (j s) -> p j s", j=4),
                                       ACT.Copy).then_inc(tok_sb, 1)
                inv_copies(p)
                for g in range(2):
                    act.wait_ge(r_ps, 2 * p + g + 1)
                    act.activation(Rm[g], B[4 + g][:, 0:256].rearrange("p (u v) -> p u v", u=4), ACT.Copy,
                                   scale=-1.0).then_inc(r_sb, 1)
                for g in range(2):
                    act.wait_ge(u_ps, 2 * p + g + 1)
                    act.activation(Um[g], B[6 + g][:, 0:256].rearrange("p (u v) -> p u v", u=4),
                                   ACT.Copy).then_inc(u_sb, 1)
            act.wait_ge(dve_step, DVE_STEPS["ln_sum"])
            act.activation(hsr[:, :, 0:8], hs[:, :, 0:8], ACT.Sqrt, scale=1.0 / DH,
                           bias=eps_col[:, 1:2]).then_inc(act_step, 1)
            for i in range(4):
                act.wait_ge(yT_ps, i + 1)
                act.activation(yT[:, 2 * i:2 * i + 2, :], B[i][:, :].rearrange("p (j s) -> p j s", j=2),
                               ACT.Copy).then_inc(yT_sb, 1)
            if UPTO >= 2:
                norm(1, "ev_ffn_norm")
                for i in range(FF // P):
                    act.wait_ge(gu_ps, i + 1)
                    if i >= 3:
                        act.wait_ge(gu_sb, i - 2)
                    act.activation(fsil[:, i % 3, :], B[i % 3][:, 0:SEQ], ACT.Silu).then_inc(gu_act, 1)
            if UPTO >= 3:
                norm(2, "od_mix_norm")
                for m in range(12):
                    act.wait_ge(cv_ps, m + 1)
                    dst = cbx[:, 2 * m:2 * m + 2, :] if m < 6 else qkvr[:, 2 * m - 12:2 * m - 10, :]
                    act.activation(dst, B[m % 4][:, :].rearrange("p (t s) -> p t s", t=2), ACT.Copy).then_inc(cv_sb, 1)
                for a in range(TT):
                    act.wait_ge(z_ps, a + 1)
                    act.activation(zt[:, a, :], B[4 + a][:, :], ACT.Silu).then_inc(z_sb, 1)
                act.wait_ge(ba_ps, 1)
                ba = B[6][:, 0:TT * 16].rearrange("p (a n) -> p a n", a=TT)
                act.activation(beta, ba[:, :, 0:8], ACT.Sigmoid)
                act.activation(alpha, ba[:, :, 8:16], ACT.Copy).then_inc(act_step, 1)
                act.wait_ge(dve_step, DVE_STEPS["sp_y"])
                link(act.activation(gs, gs, ACT.Exp, scale=-1.0))
                act.activation(ea, alog_row, ACT.Exp)
                act.activation(gs, gs, ACT.Ln, bias=1.0).then_inc(act_step, 1)
                act.wait_ge(dve_step, DVE_STEPS["gc_rdy"])
                act.activation(ge, gt, ACT.Exp).then_inc(act_step, 1)
                for i in range(3):
                    act.wait_ge(conv_rdy, i + 1)
                    v = qkvc[:, 4 * i:4 * i + 4, :]
                    act.activation(v, v, ACT.Silu).then_inc(silu_rdy, 1)
                for i in range(4):
                    act.wait_ge(l2_ps, i + 1)
                    act.activation(xn[:, i // 2, 512 * (i % 2):512 * (i % 2) + 512], B[i][:, :], ACT.Sqrt,
                                   bias=eps_col[:, 0:1]).then_inc(l2_std, 1)
                for c in range(TT):
                    act.wait_ge(kk2_ps, c + 1)
                    act.activation(kkm[c], B[c][:, :].rearrange("p (u s) -> p u s", u=4), ACT.Copy)
                    act.activation(kqm[c], B[2 + c][:, :].rearrange("p (u s) -> p u s", u=4),
                                   ACT.Copy).then_inc(kk2_sb, 1)
                for i in range(4):
                    act.wait_ge(tk_ps, i + 1)
                    act.activation((ktok, vto)[i // 2][:, i % 2, :], B[4 + i][:, :], ACT.Copy).then_inc(tk_sb, 1)
                for p in range(4, 6):
                    for g in range(2):
                        n = 2 * (p - 4) + g + 1
                        act.wait_ge(dd_rdy, n)
                        act.activation(attn[g], attn[g], ACT.Exp)
                        last = act.activation(Do[g], Do[g], ACT.Exp, scale=-1.0)
                        if p == 5:
                            act.activation(qe[g], B[4 + g][:, :].rearrange("p (u s) -> p u s", u=4), ACT.Exp)
                            last = act.activation(ke[g], B[4 + g][:, :].rearrange("p (u s) -> p u s", u=4), ACT.Exp)
                        last.then_inc(dd_exp, 1)
                    inv_copies(p)
                    for g in range(2):
                        act.wait_ge(ou_ps, 2 * (p - 4) + g + 1)
                        act.activation(Uo[g], B[6 + g][:, :].rearrange("p (u s) -> p u s", u=4),
                                       ACT.Copy).then_inc(ou_sb, 1)
                act.wait_ge(dve_step, DVE_STEPS["on_sum"])
                act.activation(hsr[:, :, 0:4], hs[:, :, 0:4], ACT.Sqrt, scale=1.0 / DHD,
                               bias=eps_col[:, 0:1]).then_inc(act_step, 1)
                for i in range(2):
                    act.wait_ge(yd_ps, i + 1)
                    act.activation(yTo[:, 4 + 2 * i:6 + 2 * i, :], B[i][:, :].rearrange("p (j s) -> p j s", j=2),
                                   ACT.Copy).then_inc(yd_sb, 1)
            if UPTO >= 4:
                norm(3, "od_ffn_norm")
                act.wait_ge(dve_step, DVE_STEPS["rt_max"])
                for a in range(TT):
                    last = act.activation(prob[:, a, :], B[7][:, NE * a:NE * a + NE], ACT.Exp, bias=m2[:, a:a + 1],
                                          accum_out=esum[:, a:a + 1])
                last.then_inc(act_step, 1)

                def expert(ps, i):
                    b1, b2, b7 = NE * ps + 1, 2 * NE * ps + 1, NC_E * NE * ps + 1

                    def duty(what, j):
                        if what == "tokens":
                            act.wait_ge(st_ps, i + b1)
                            act.activation(selgT, B[4][:, 0:TT * P], ACT.Copy).then_inc(st_sb, 1)
                            for r in range(2):
                                act.wait_ge(xg_sb, i * 2 + b2 + r)
                                act.activation(xgs[:, 0, 4 * r:4 * r + 4, :], xg[:, 4 * r:4 * r + 4, :],
                                               ACT.Copy).then_inc(x_hi, 1)
                        elif what == "silu":
                            act.wait_ge(half_ps, used_half(i, ps, at_half["gate", j, 1]))
                            act.activation(esil[:, j % 2, :], B[j % 2][:, :], ACT.Silu).then_inc(eg_act, 1)
                        elif what == "turned":
                            act.wait_ge(ht_ps, i * NC_E + b7 + j)
                            act.activation(ehs[:, j % 2, 0], B[6 + j % 2][:, :].rearrange("p (k s) -> p k s", k=4),
                                           ACT.Copy).then_inc(ht_hi, 1)

                    for r in range(PER + 1):
                        for what, j in duties[r]:
                            duty(what, j)
                        if r < PER:
                            act.wait_ge(landed_e[r % NHALF],
                                        i * (16 * PER // NHALF) + (16 * PER // NHALF * NE * ps + 16 * (r // NHALF + 1)))
                            act.wait_ge(half_ps, used_half(i, ps, r - NSTAGE))
                            act.activation(wst[:, r % NSTAGE, 0, :], ring[:, (r % NHALF) * HALF:(r % NHALF + 1) * HALF],
                                           ACT.Copy).then_inc(w_hi, 1)
                    act.wait_ge(half_ps, used_half(i, ps, PER - 1))
                    for n in range(2):
                        act.activation(ysb[:, 512 * n:512 * n + 512], B[4 + n][:, :], ACT.Copy).then_inc(ey_sb, 1)

                with act.Fori(0, NE) as i:
                    expert(0, i)
                act.wait_ge(flag_rdy, 1)
                with act.If(act.value_load(flag[0:1, 0:1], min_val=0, max_val=1) > 0):
                    with act.Fori(0, NE) as i:
                        expert(1, i)

        @block.vector
        def _(dve):
            chain = [0]

            def link(ins):
                chain[0] += 1
                ins.then_inc(dve_chain, 1)
                dve.wait_ge(dve_chain, chain[0])

            def norm(ni, name):
                dve.wait_ge(std_rdy, ni + 1)
                link(dve.reciprocal(rstd, std))
                dve.tensor_scalar(xn[:, 0, :], x_sb[:, 0, :], rstd[:, 0:1], None, MUL)
                dve.tensor_scalar(xn[:, 1, :], x_sb[:, 1, :], rstd[:, 1:2], None, MUL).then_inc(xn_rdy, 1)
                for k in range(KT // 2, KT):
                    dve.wait_ge(xnT_ps, 4 * ni + k // 2 + 1)
                    last = dve.tensor_scalar(hT[:, k, :], B[k // 2][:, SEQ * (k % 2):SEQ * (k % 2) + SEQ],
                                             cols[:, COL[name] + k:COL[name] + k + 1], None, MUL)
                last.then_inc(hT_dve, 1)
                dve.wait_ge(hT_dve, ni + 1)
                dve.wait_ge(hT_act, ni + 1)

            dve.memset(eps_col[:, 0:1], NORM_EPS)
            dve.memset(eps_col[:, 1:2], LN_EPS)
            inv_freq = np.power(np.float32(500000.0), -np.arange(ROPE_HALF, dtype=np.float32) / np.float32(ROPE_HALF))
            for i in range(ROPE_HALF):
                dve.memset(freq[:, i:i + 1], float(inv_freq[i]))
            dve.wait_ge(pool_const, 1)
            link(dve.tensor_tensor(xor_i[:, :], xor_i[:, :], iota_i[:, :], ALU.bitwise_xor))
            for lev in range(NLEV):
                link(dve.tensor_scalar(iota_i[:, :], xor_i[:, :], lev, None, ALU.logical_shift_right))
                for z in range(2):
                    link(dve.scalar_tensor_tensor(levmask[:, z, lev, :], iota_i[:, :], 1.0, tri[:, z, :],
                                                  ALU.is_equal, MUL))
            dve.tensor_scalar(levmask[:, :, :, :].rearrange("p z l s -> p (z l s)"),
                              levmask[:, :, :, :].rearrange("p z l s -> p (z l s)"), -1.0, None,
                              MUL).then_inc(dve_const, 1)
            link(dve.tensor_copy(mw1, dist))
            link(dve.tensor_scalar(mw2, mw1, float(SEQ - 64), None, ALU.is_ge))
            link(dve.scalar_tensor_tensor(mw2, mw1, float(SEQ + 64), mw2, ALU.is_le, MUL))
            for dil in (4, 16):
                link(dve.tensor_scalar(bits, dist, dil - 1, None, ALU.bitwise_and))
                link(dve.scalar_tensor_tensor(mw2, bits, 0.0, mw2, ALU.is_equal, ADD))
            link(dve.tensor_scalar(mw1, mw2, 0.5, NEG, ALU.is_lt, MUL))
            link(dve.tensor_scalar(amask, mw2, 1.5, float(np.log(2.0)), ALU.is_ge, MUL))
            link(dve.tensor_tensor(amask, amask, mw1, ADD))
            link(dve.tensor_scalar(mw1, mw2, 2.5, float(np.log(1.5)), ALU.is_ge, MUL))
            dve.tensor_tensor(amask, amask, mw1, ADD).then_inc(mask_rdy, 1)
            dve.wait_ge(mask_rdy, 1)
            dve.wait_ge(vec_tp, 1)
            dve.tensor_copy(cols[:, 0:N0], B[7][:, 0:N0])
            dve.tensor_copy(cols[:, N0:NCOL], B[7][:, P:P + N1]).then_inc(cols_rdy, 1)
            dve.wait_ge(cols_rdy, 1)
            mu, lm = COL["ev_shift_mu"], COL["ev_lora_mu"]
            dve.scalar_tensor_tensor(cmix[:, 0:12], cols[:, mu:mu + 12], -1.0, cols[:, mu + 12:mu + 24], MUL, SUB)
            dve.scalar_tensor_tensor(cmix[:, 12:20], cols[:, lm:lm + 8], -1.0, cols[:, lm + 8:lm + 16], MUL, SUB)
            ka = COL["ev_k_a"]
            link(dve.tensor_scalar(cmix[:, 20:24], cols[:, ka:ka + 4], -1.0, None, MUL))
            link(dve.tensor_scalar(cmix[:, :], cmix[:, :], 1.0, None, ADD))
            norm(0, "ev_mix_norm")

            def shift_mix(dst, src, k, c0, m0, m1):
                link(dve.tensor_scalar(dst[:, k, :], src[:, k, :], c0, None, MUL))
                link(dve.scalar_tensor_tensor(dst[:, k, 1:SEQ], src[:, k, 0:SEQ - 1], m0, dst[:, k, 1:SEQ], MUL, ADD))
                link(dve.scalar_tensor_tensor(dst[:, k, 0:SEQ - 1], src[:, k, 1:SEQ], m1, dst[:, k, 0:SEQ - 1],
                                              MUL, ADD))

            for k in range(KT):
                shift_mix(hxT, hT, k, cmix[:, 12 + k:13 + k], cols[:, lm + k:lm + k + 1],
                          cols[:, lm + 8 + k:lm + 9 + k])
            dve.memset(bonus[:, :, :], 0.0).then_inc(hx_rdy, 1)
            dve.wait_ge(pos_in, 16)
            link(dve.tensor_copy(posf, pos_i[:, :]))
            for a in range(TT):
                link(dve.tensor_scalar(ang[:, a, :], freq, posf[:, a:a + 1], None, MUL))
            MAGIC = 12582912.0
            link(dve.tensor_scalar(red, ang, 1.0 / (2 * np.pi), MAGIC, MUL, ADD))
            link(dve.tensor_scalar(red, red, -MAGIC, None, ADD))
            C1 = 6.28125
            C2 = float(np.float32(0.0019353071795864769).view(np.int32) & -4096 and
                       np.array(np.float32(0.0019353071795864769).view(np.int32) & -4096, np.int32).view(np.float32))
            C3 = float(2 * np.pi - C1 - C2)
            for cc in (C1, C2, C3):
                link(dve.scalar_tensor_tensor(ang, red, -cc, ang, MUL, ADD))
            PI = 3.1415925
            link(dve.tensor_scalar(red, ang, PI, -PI, MIN, MAX))
            link(dve.tensor_scalar(ang, red, -1.0, None, MUL))
            link(dve.tensor_tensor(ang, ang, red, MAX))
            dve.tensor_scalar(ang, ang, -1.0, float(np.pi / 2), MUL, ADD).then_inc(dve_step, 1)
            dve.wait_ge(rows_in, 16 * 7)
            dve.wait_ge(qkv_sb, 6)
            link(dve.tensor_tensor(xn[:, :, :], qkv[:, :, 0:D], qkv[:, :, 0:D], MUL))
            dve.tensor_reduce(hs, xn[:, :, :].rearrange("p a (h d) -> p a h d", d=DH), AX.X, ADD).then_inc(dve_step, 1)
            dve.wait_ge(act_step, ACT_STEPS["qk_std"])
            link(dve.reciprocal(hsr, hsr))
            qk4 = qkv[:, :, 0:D].rearrange("p a (h d) -> p a h d", d=DH)
            for a in range(TT):
                link(dve.tensor_tensor(qk4[:, a], qk4[:, a], hsr[:, a, :].unsqueeze(2).to_broadcast([P, 16, DH]), MUL))
                for i, row in enumerate((qn_row, kn_row)):
                    v = qk4[:, a, 8 * i:8 * i + 8, :]
                    link(dve.tensor_tensor(v, v, row.unsqueeze(1).to_broadcast([P, 8, DH]), MUL))
            dve.wait_ge(act_step, ACT_STEPS["sin_rdy"])
            rt = xn[:, :, 0:4 * 16 * ROPE_HALF].rearrange("p a (i h e) -> p a i h e", i=4, h=16)
            for a in range(TT):
                x1, x2 = qk4[:, a, :, 0:ROPE_HALF], qk4[:, a, :, ROPE_HALF:2 * ROPE_HALF]
                co = cosT[:, a, :].unsqueeze(1).to_broadcast([P, 16, ROPE_HALF])
                si = sinT[:, a, :].unsqueeze(1).to_broadcast([P, 16, ROPE_HALF])
                dve.tensor_tensor(rt[:, a, 0], x1, co, MUL)
                dve.tensor_tensor(rt[:, a, 1], x2, si, MUL)
                dve.tensor_tensor(rt[:, a, 2], x2, co, MUL)
                link(dve.tensor_tensor(rt[:, a, 3], x1, si, MUL))
                dve.tensor_tensor(x1, rt[:, a, 0], rt[:, a, 1], SUB)
                last = dve.tensor_tensor(x2, rt[:, a, 2], rt[:, a, 3], ADD)
            last.then_inc(dve_step, 1)
            dve.wait_ge(raw_sb, 6)
            for t in range(12):
                shift_mix(mix, raw, t, cmix[:, t:t + 1], cols[:, mu + t:mu + t + 1], cols[:, mu + 12 + t:mu + 13 + t])
            dve.memset(bonus[:, :, :], 0.0).then_inc(dve_step, 1)
            for h in range(HA):
                dve.wait_ge(att_s, h + 1)
                if h > 1:
                    dve.wait_ge(att_e, h - 1)
                s2 = sm_s[:, h % 2, :].rearrange("p (a s) -> p a s", a=TT)
                link(dve.scalar_tensor_tensor(sm_s[:, h % 2, :], B[h % 2][:, :], DH ** -0.5,
                                              amask, MUL, ADD))
                link(dve.tensor_reduce(mx[:, :, h:h + 1], s2, AX.X, MAX))
                dve.tensor_scalar(nmx[:, :, h:h + 1], mx[:, :, h:h + 1], -1.0, None, MUL).then_inc(att_m, 1)
            dve.wait_ge(att_o, HA)
            link(dve.reciprocal(den, den))
            for a in range(TT):
                last = dve.tensor_tensor(yab[:, a, 0:WA].rearrange("p (h d) -> p h d", d=DH),
                                         B[3 + 2 * a][:, :].rearrange("p (h d) -> p h d", d=DH),
                                         den[:, a, :].unsqueeze(2).to_broadcast([P, HA, DH]), MUL)
            last.then_inc(dve_step, 1)
            dve.wait_ge(dve_step, DVE_STEPS["ya_rdy"])
            for i in range(2):
                dve.wait_ge(vt_ps, i + 1)
                dve.tensor_copy(vtok[:, i, :], B[6 + i][:, :]).then_inc(vt_sb, 1)
            dve.wait_ge(wa_sb, 16)
            kv = COL["ev_k_k"]
            r_, k_ = mix[:, 0:4, :], mix[:, 4:8, :]
            for j in range(4):
                dve.tensor_scalar(kk[:, j, :], k_[:, j, :], cols[:, kv + j:kv + j + 1], None, MUL)
                for z in range(2):
                    last = dve.tensor_scalar(kd[:, z, j, :], ic[:, z, j, :], cols[:, ka + j:ka + j + 1],
                                             cmix[:, 20 + j:21 + j], MUL, ADD)
            link(last)
            dve.tensor_tensor(Cw_f, kk.rearrange("p j s -> p (j s)"), kk.rearrange("p j s -> p (j s)"),
                              MUL).then_inc(dve_step, 1)
            for z in range(2):
                link(dve.tensor_tensor(kd[:, z], kd[:, z], k_, MUL))
            link(dve.tensor_tensor(Hw_f, kd[:, 0].rearrange("p j s -> p (j s)"),
                                   kd[:, 1].rearrange("p j s -> p (j s)"), ADD))
            rk = COL["ev_r_k"]
            for j in range(4):
                last = dve.scalar_tensor_tensor(Hw_f[:, SEQ * j:SEQ * j + SEQ], Hw_f[:, SEQ * j:SEQ * j + SEQ],
                                                cols[:, rk + j:rk + j + 1], r_[:, j, :], MUL, MUL)
            last.then_inc(dve_step, 1)
            dve.wait_ge(act_step, ACT_STEPS["kk_std"])
            link(dve.reciprocal(Ew_f, Ew_f))
            link(dve.tensor_tensor(kk.rearrange("p j s -> p (j s)"), kk.rearrange("p j s -> p (j s)"), Ew_f, MUL))
            dve.wait_ge(bon_ps, 1)
            dve.tensor_copy(bonus.rearrange("p a h -> p (a h)"), B[5][:, 0:TT * HA]).then_inc(dve_step, 1)
            E5 = -float(np.exp(-0.5))
            link(dve.tensor_scalar(sw.rearrange("p z j s -> p (z j s)"), sw.rearrange("p z j s -> p (z j s)"),
                                   E5, None, MUL))
            for z in range(2):
                for j in range(4):
                    for c in range(TT):
                        o, i = Cw[:, j, c, :], sw[:, z, j, P * c:P * c + P]
                        if z:
                            o, i = o[:, ::-1], i[:, ::-1]
                        last = dve.tensor_tensor_scan(o, ones[:, :], i, 0.0, MUL, ADD)
                link(last)
                m8 = "p j c s -> p (j c) s"
                c8 = Cw.rearrange(m8)
                link(dve.tensor_copy(cmid, c8[:, :, 63]))
                link(dve.tensor_tensor(c8, c8, cmid.unsqueeze(2).to_broadcast([P, 8, P]), SUB))
                link(dve.tensor_copy(sscale, c8[:, :, P - 1 if z == 0 else 0]))
                dve.tensor_tensor(Hw, Cw, sw[:, z].rearrange("p j (c s) -> p j c s", c=TT), SUB).then_inc(dec_c, 1)
                dve.wait_ge(dec_e, z + 1)
                r4, kk4 = (v.rearrange("p j (c s) -> p j c s", c=TT) for v in (r_, kk))
                for c in range(TT):
                    dve.tensor_tensor(arF[z][:, :, c, 1, :], r4[:, :, c], Cw[:, :, c], MUL)
                    dve.tensor_tensor(arF[z][:, :, c, 0, :], kk4[:, :, c], Hw[:, :, c], MUL)
                dve.tensor_tensor(kF[z], kd[:, z].rearrange("p j (c s) -> p j c s", c=TT), Ew, MUL)
                link(dve.tensor_tensor(Ew, Ew, kk4, MUL))
                link(dve.tensor_tensor(bF[z], ic[:, z].rearrange("p j (c s) -> p j c s", c=TT), Ew, MUL))
                cf, cs = (0, 1) if z == 0 else (1, 0)
                end2, mid2 = (v.rearrange("p (j c) -> p j c", c=TT) for v in (eend, emid))
                link(dve.tensor_tensor(sfac[:, z, :], end2[:, :, cf], mid2[:, :, cs], MUL))
            dve.tensor_copy(cmid[:, 0:1], sfac[:, 0, 0:1]).then_inc(dve_step, 1)

            def inv_adds(p):
                Tm, Pm = INVB[p][0], INVB[p][1]
                for lev in range(1, NLEV):
                    for g in range(2):
                        dve.wait_ge(pt_ps, inv_seq(p, lev, g))
                        odd = INV[p][g][0] == 0
                        pv = odd_even(Pm[g], lev, odd)
                        last = dve.tensor_tensor(pv, packed(B[2 + g], lev, 0), pv, ADD)
                        if lev < NLEV - 1:
                            tv = odd_even(Tm[g], lev, not odd)
                            last = dve.tensor_tensor(tv, packed(B[2 + g], lev, 64), tv, ADD)
                        last.then_inc(tp_sb, 1)

            for p, (z, c) in enumerate(RW):
                for i in range(8):
                    dve.wait_ge(sc_ps, 8 * p + i + 1)
                    if p and i % 4 == 0:
                        dve.wait_ge(y_ps, 2 * p)
                    dve.tensor_tensor(scg[i // 4][:, i % 4], B[4 + i % 2][:, :].rearrange("p (m s) -> p m s", m=4),
                                      smask[:, z], MUL).then_inc(sc_sb, 1)
                inv_adds(p)
                for g in range(2):
                    if p < 2:
                        dve.wait_ge(s_ps, 2 * p + g + 1)
                        for i in range(2):
                            j = 2 * g + i
                            last = dve.scalar_tensor_tensor(S0[z][:, j, :], B[g][:, P * i:P * i + P],
                                                            sfac[:, z, j:j + 1], bones[:, :], MUL, MUL)
                        last.then_inc(s_sb, 1)
                for g in range(2):
                    dve.wait_ge(y_ps, 2 * p + g + 1)
                    dst = yab[:, c, WA + 256 * g:WA + 256 * g + 256]
                    if p < 2:
                        dve.tensor_copy(dst, B[4 + g][:, 0:256]).then_inc(y_sb, 1)
                    else:
                        dve.tensor_tensor(dst, B[4 + g][:, 0:256], dst, ADD).then_inc(y_sb, 1)
            dve.wait_ge(y_sb, 8)
            yb = yab[:, :, WA:2 * WA].rearrange("p a (h d) -> p a h d", d=DH)
            w1 = xn[:, 0:2, 0:WA].rearrange("p a (h d) -> p a h d", d=DH)
            mean = hs[:, :, 8:16]
            link(dve.tensor_reduce(mean, yb, AX.X, ADD))
            link(dve.tensor_scalar(mean, mean, -1.0 / DH, None, MUL))
            for a in range(TT):
                link(dve.tensor_tensor(yb[:, a], yb[:, a], mean[:, a, :].unsqueeze(2).to_broadcast([P, HA, DH]), ADD))
                link(dve.tensor_tensor(w1[:, a], yb[:, a], yb[:, a], MUL))
            dve.tensor_reduce(hs[:, :, 0:8], w1, AX.X, ADD).then_inc(dve_step, 1)
            dve.wait_ge(act_step, ACT_STEPS["ln_std"])
            link(dve.reciprocal(hsr[:, :, 0:8], hsr[:, :, 0:8]))
            dve.wait_ge(gate_sb, 2)
            dve.wait_ge(vt_sb, 2)
            for a in range(TT):
                y1 = yab[:, a, WA:2 * WA]
                dve.tensor_tensor(w1[:, a], vtok[:, a, :].rearrange("p (h d) -> p h d", d=DH),
                                  bonus[:, a, :].unsqueeze(2).to_broadcast([P, HA, DH]), MUL)
                link(dve.tensor_tensor(yb[:, a], yb[:, a], hsr[:, a, 0:8].unsqueeze(2).to_broadcast([P, HA, DH]), MUL))
                link(dve.tensor_tensor(y1, y1, lnw_row, MUL))
                link(dve.tensor_tensor(y1, y1, lnb_row, ADD))
                link(dve.tensor_tensor(y1, y1, xn[:, a, 0:WA], ADD))
                link(dve.tensor_tensor(y1, y1, gate[:, a, :], MUL))
            dve.tensor_copy(bonus[:, 0, 0:1], hs[:, 0, 0:1]).then_inc(dve_step, 1)

            def residual(layer):
                for n in range(2):
                    for a in range(TT):
                        dve.wait_ge(o_ps, 4 * layer + 2 * n + a + 1)
                        v = x_sb[:, a, 512 * n:512 * n + 512]
                        last = dve.tensor_tensor(v, B[4 + 2 * n + a][:, :], v, ADD)
                    last.then_inc(x_rdy, 1)
                dve.wait_ge(x_rdy, 2 * layer + 2)

            residual(0)
            if UPTO >= 2:
                norm(1, "ev_ffn_norm")
                for i in range(FF // P):
                    dve.wait_ge(gu_act, i + 1)
                    if i >= 8 and i % 4 == 0:
                        dve.wait_ge(dn_ps, (i - 8) // 4 + 1)
                    dve.tensor_tensor(hf[:, i % 8, :], B[i % 3][:, SEQ:2 * SEQ], fsil[:, i % 3, :],
                                      MUL).then_inc(gu_sb, 1)
                residual(1)
            if UPTO >= 3:
                norm(2, "od_mix_norm")
                dve.wait_ge(act_step, ACT_STEPS["ba_sb"])
                for a in range(TT):
                    link(dve.tensor_tensor(glog[:, a, :], alpha[:, a, :], dt_row, ADD))
                link(dve.tensor_scalar(gs, glog, -1.0, None, MUL))
                dve.tensor_tensor(gs, gs, glog, MAX).then_inc(dve_step, 1)
                dve.wait_ge(act_step, ACT_STEPS["sp_l"])
                link(dve.scalar_tensor_tensor(glog, glog, 0.0, gs, MAX, ADD))
                for a in range(TT):
                    last = dve.scalar_tensor_tensor(glog[:, a, :], glog[:, a, :], -1.0, ea, MUL, MUL)
                last.then_inc(dve_step, 1)
                dve.wait_ge(gc_ps, 1)
                dve.tensor_copy(gc.rearrange("p a n -> p (a n)"), B[7][:, 0:16])
                link(dve.tensor_copy(gl_.rearrange("p a n -> p (a n)"), B[7][:, 16:32]))
                dve.tensor_tensor(gt, gl_, gc, SUB).then_inc(dve_step, 1)
                dve.wait_ge(cv_sb, 6)
                flat = "p j s -> p (j s)"
                link(dve.tensor_tensor(cu.rearrange(flat), cbx[:, 4:8, :].rearrange(flat),
                                       cbx[:, 8:12, :].rearrange(flat), MUL))
                cc, cd = COL["od_conv_c"], COL["od_conv_dn"]

                def conv(dst, src, k, col, n):
                    shift_mix(dst, src, k, cols[:, col + n + k:col + n + k + 1], cols[:, col + k:col + k + 1],
                              cols[:, col + 2 * n + k:col + 2 * n + k + 1])

                for k in range(4):
                    conv(yTo, cu, k, cc, 4)
                dve.tensor_tensor(yTo[:, 0:4, :].rearrange(flat), yTo[:, 0:4, :].rearrange(flat),
                                  cbx[:, 0:4, :].rearrange(flat), MUL).then_inc(dve_step, 1)
                dve.wait_ge(cv_sb, 12)
                for i in range(3):
                    for k in range(4 * i, 4 * i + 4):
                        conv(qkvc, qkvr, k, cd, 12)
                    dve.tensor_copy(cntf, gt[:, 0, 0:1]).then_inc(conv_rdy, 1)
                for i in range(2):
                    dve.wait_ge(silu_rdy, i + 1)
                    v = qkvc[:, 4 * i:4 * i + 4, :].rearrange(flat)
                    dve.tensor_tensor(xn[:, i, :], v, v, MUL).then_inc(l2_sq, 1)
                dve.wait_ge(l2_std, 4)
                link(dve.reciprocal(xn[:, :, :], xn[:, :, :]))
                q2, k2 = qkvc[:, 0:4, :].rearrange(flat), qkvc[:, 4:8, :].rearrange(flat)
                dve.scalar_tensor_tensor(q2, q2, DHD ** -0.5, xn[:, 0, :], MUL, MUL)
                dve.tensor_tensor(k2, k2, xn[:, 1, :], MUL).then_inc(dve_step, 1)
                for p in range(4, 6):
                    for g in range(2):
                        z, c = INV[p][g]
                        n = 2 * (p - 4) + g
                        dve.wait_ge(row_ps, n + 1)
                        rb = B[4 + g][:, :].rearrange("p (u s) -> p u s", u=4)
                        if p == 5 and g == 0:
                            dve.wait_ge(oo_ps, 2)
                            dve.wait_ge(am_rdy, inv_seq(4, NLEV - 1, 1))
                        for u in range(4):
                            col = gc[:, c, 4 * z + u:4 * z + u + 1]
                            dve.tensor_scalar(attn[g][:, u, :], rb[:, u, :], col, 0.0, SUB, MIN)
                            last = dve.tensor_scalar(Do[g][:, u, :], rb[:, u, :], col, 0.0, SUB, MAX)
                        last.then_inc(dd_rdy, 1)
                    for g in range(2):
                        z, c = INV[p][g]
                        n = 2 * (p - 4) + g
                        dve.wait_ge(dd_exp, n + 1)
                        dve.wait_ge(kk2_sb, 2)
                        for u in range(4):
                            last = dve.scalar_tensor_tensor(Ao[g][:, u, :], kkm[c][:, u, :],
                                                            beta[:, c, 4 * z + u:4 * z + u + 1], Do[g][:, u, :],
                                                            MUL, MUL)
                        last.then_inc(oa_rdy, 1)
                        link(dve.tensor_tensor(attn[g], attn[g], kqm[c], MUL))
                        link(dve.tensor_tensor(attn[g], attn[g],
                                               smask[:, z, 1, :].unsqueeze(1).to_broadcast([P, 4, P]), MUL))
                        if p == 5:
                            dve.tensor_tensor(qe[g], qe[g], qkvc[:, 0:4, P * c:P * c + P], MUL)
                            link(dve.tensor_tensor(ke[g], ke[g], qkvc[:, 4:8, P * c:P * c + P], MUL))
                    inv_adds(p)
                    for g in range(2):
                        z, c = INV[p][g]
                        n = 2 * (p - 4) + g
                        vt = vto[:, c, :].rearrange("p (u v) -> p u v", u=4)
                        bb = beta[:, c, 4 * z:4 * z + 4].unsqueeze(2).to_broadcast([P, 4, P])
                        dve.wait_ge(tk_sb, 4)
                        if p == 5:
                            dve.wait_ge(ks_ps, g + 1)
                            link(dve.tensor_tensor(Ro[g], vt, B[4 + g][:, :].rearrange("p (u s) -> p u s", u=4), SUB))
                            dve.tensor_tensor(Ro[g], Ro[g], bb, MUL).then_inc(or_rdy, 1)
                        else:
                            dve.tensor_tensor(Ro[g], vt, bb, MUL).then_inc(or_rdy, 1)
                    for g in range(2):
                        z, c = INV[p][g]
                        if p == 4:
                            dve.wait_ge(ou_sb, g + 1)
                            dve.wait_ge(act_step, ACT_STEPS["ge_rdy"])
                            dve.tensor_tensor(qe[g], Uo[g], ge[:, c, 4 * z:4 * z + 4].unsqueeze(2).to_broadcast(
                                [P, 4, P]), MUL).then_inc(ous_rdy, 1)
                            dve.wait_ge(os_ps, g + 1)
                            dve.tensor_copy(S0o[z], B[g][:, :].rearrange("p (u s) -> p u s", u=4)).then_inc(os_sb, 1)
                    for g in range(2):
                        z, c = INV[p][g]
                        dve.wait_ge(oo_ps, 2 * (p - 4) + g + 1)
                        if p == 4:
                            dve.tensor_copy(osum[:, c, :], B[4 + g][:, :]).then_inc(oo_sb, 1)
                        else:
                            dve.tensor_tensor(osum[:, c, :], B[4 + g][:, :], osum[:, c, :], ADD).then_inc(oo_sb, 1)
                dve.wait_ge(oo_sb, 4)
                w2 = xn[:, :, 0:512]
                link(dve.tensor_tensor(w2, osum, osum, MUL))
                o4 = "p a (h d) -> p a h d"
                dve.tensor_reduce(hs[:, :, 0:4], w2.rearrange(o4, h=4), AX.X, ADD).then_inc(dve_step, 1)
                dve.wait_ge(act_step, ACT_STEPS["on_std"])
                link(dve.reciprocal(hsr[:, :, 0:4], hsr[:, :, 0:4]))
                dve.wait_ge(z_sb, 2)
                link(dve.tensor_tensor(osum, osum, zt, MUL))
                for a in range(TT):
                    v = osum[:, a, :].rearrange("p (h d) -> p h d", h=4)
                    link(dve.tensor_tensor(v, v, hsr[:, a, 0:4].unsqueeze(2).to_broadcast([P, 4, P]), MUL))
                    last = dve.tensor_tensor(v, v, dn_row.unsqueeze(1).to_broadcast([P, 4, P]), MUL)
                last.then_inc(dve_step, 1)
                residual(2)
            if UPTO >= 4:
                norm(3, "od_ffn_norm")
                dve.memset(gates_ext[:, :, NE:NE + 1], 0.0)
                dve.memset(rank_ext[:, :, NE:NE + 1], -1.0)
                for e in range(NE):
                    dve.memset(ew[:, e:e + 1], float(NE - e))
                dve.wait_ge(rt_ps, 1)
                lg = B[7][:, 0:TT * NE].rearrange("p (a e) -> p a e", a=TT)
                link(dve.tensor_reduce(m1, lg, AX.X, MAX))
                dve.tensor_scalar(m2, m1, -1.0, None, MUL).then_inc(dve_step, 1)
                dve.wait_ge(act_step, ACT_STEPS["rt_exp"])
                link(dve.reciprocal(esum, esum))
                link(dve.tensor_tensor(prob, prob, esum.unsqueeze(2).to_broadcast([P, TT, NE]), MUL))

                def best(src, m, oh):
                    link(dve.tensor_reduce(m, src, AX.X, MAX))
                    link(dve.tensor_tensor(esc, src, m.unsqueeze(2).to_broadcast([P, TT, NE]), ALU.is_equal))
                    link(dve.tensor_tensor(esc, esc, ew.unsqueeze(1).to_broadcast([P, TT, NE]), MUL))
                    link(dve.tensor_reduce(esum, esc, AX.X, MAX))
                    link(dve.tensor_tensor(oh, esc, esum.unsqueeze(2).to_broadcast([P, TT, NE]), ALU.is_equal))

                best(prob, m1, oh1)
                link(dve.scalar_tensor_tensor(gates, oh1, -2.0, prob, MUL, ADD))
                best(gates, m2, oh2)
                link(dve.tensor_tensor(esum, m1, m2, ADD))
                link(dve.reciprocal(esum, esum))
                link(dve.tensor_tensor(m1, m1, esum, MUL))
                link(dve.tensor_tensor(m2, m2, esum, MUL))
                link(dve.tensor_tensor(esc, oh1, m1.unsqueeze(2).to_broadcast([P, TT, NE]), MUL))
                link(dve.tensor_tensor(gates, oh2, m2.unsqueeze(2).to_broadcast([P, TT, NE]), MUL))
                link(dve.tensor_tensor(gates, gates, esc, ADD))
                dve.tensor_tensor(asg, oh1, oh2, ADD).then_inc(dve_step, 1)
                dve.wait_ge(rank_ps, 1)
                link(dve.scalar_tensor_tensor(rank, B[6][:, 0:16].rearrange("p (a e) -> p a e", a=TT), 1.0, asg,
                                              ADD, MUL))
                link(dve.tensor_scalar(rank, rank, -1.0, None, ADD))
                link(dve.tensor_reduce(cntf, B[6][:, 16:24], AX.X, MAX))
                dve.tensor_scalar(flag[:, :], cntf, float(P), None, ALU.is_gt).then_inc(flag_rdy, 1)
                dve.memset(ang[:, 0, 0:1], 0.0).then_inc(cmb_sb, 1)
                fw = COL["od_ffn_norm"]

                def select(e):
                    for a in range(TT):
                        dve.tensor_scalar(sel[:, a, :], iot[:, :], rank_ext[:, a, e], None, ALU.is_equal)
                        last = dve.tensor_scalar(selg[:, a, :], iot[:, :], rank_ext[:, a, e],
                                                 gates_ext[:, a, e], ALU.is_equal, MUL)
                    last.then_inc(sel_rdy, 1)

                def expert(ps, i):
                    b1, b2, b7 = NE * ps + 1, 2 * NE * ps + 1, NC_E * NE * ps + 1

                    def duty(what, j):
                        if what == "tokens":
                            for r in range(2):
                                dve.wait_ge(xg_ps, i * 2 + b2 + r)
                                dve.tensor_tensor(xg[:, 4 * r:4 * r + 4, :],
                                                  B[6 + r][:, :].rearrange("p (k s) -> p k s", k=4),
                                                  cols[:, fw + 4 * r:fw + 4 * r + 4].unsqueeze(2).to_broadcast([P, 4, P]),
                                                  MUL).then_inc(xg_sb, 1)
                            for r in range(2):
                                v = slice(4 * r, 4 * r + 4)
                                dve.wait_ge(x_hi, i * 2 + b2 + r)
                                dve.tensor_tensor(xgs[:, 1, v, :], xg[:, v, :], xgs[:, 0, v, :].bitcast(F32),
                                                  SUB).then_inc(x_lo, 1)
                        elif what == "product":
                            dve.wait_ge(eg_act, i * NC_E + b7 + j)
                            dve.wait_ge(half_ps, used_half(i, ps, at_half["up", j, 1]))
                            dve.tensor_tensor(ehr[:, j % 2, :], B[2 + j % 2][:, :], esil[:, j % 2, :],
                                              MUL).then_inc(eh_rdy, 1)
                        elif what == "turned":
                            dve.wait_ge(ht_hi, i * NC_E + b7 + j)
                            dve.tensor_tensor(ehs[:, j % 2, 1], B[6 + j % 2][:, :].rearrange("p (k s) -> p k s", k=4),
                                              ehs[:, j % 2, 0].bitcast(F32), SUB).then_inc(ht_lo, 1)

                    for r in range(PER + 1):
                        for what, j in duties[r]:
                            duty(what, j)
                        if r < PER:
                            dve.wait_ge(w_hi, i * PER + (NE * PER * ps + r + 1))
                            dve.tensor_tensor(wst[:, r % NSTAGE, 1, :], ring[:, (r % NHALF) * HALF:(r % NHALF + 1) * HALF],
                                              wst[:, r % NSTAGE, 0, :].bitcast(F32), SUB).then_inc(w_lo, 1)
                    dve.wait_ge(half_ps, used_half(i, ps, at_half["gate", NC_E - 1, 1]))
                    select(bass.ds(i + 1, 1))
                    for q in range(4):
                        dve.wait_ge(cmb_ps, i * 4 + 4 * NE * ps + q + 1)
                        v = x_sb[:, q % 2, 512 * (q // 2):512 * (q // 2) + 512]
                        dve.tensor_tensor(v, B[q][:, :], v, ADD).then_inc(cmb_sb, 1)

                select(slice(0, 1))
                with dve.Fori(0, NE) as i:
                    expert(0, i)
                link(dve.tensor_scalar(rank, rank, float(P), None, SUB))
                dve.wait_ge(flag_rdy, 1)
                with dve.If(dve.value_load(flag[0:1, 0:1], min_val=0, max_val=1) > 0):
                    select(slice(0, 1))
                    with dve.Fori(0, NE) as i:
                        expert(1, i)
                dve.memset(ang[:, 0, 0:1], 0.0).then_inc(x_rdy, 2)

        @block.tensor
        def _(pe):
            def weights(kind, n):
                s, _, cnt = where[kind, n]
                pe.wait_ge(landed[s], cnt)
                return ring[:, s * SLOT:(s + 1) * SLOT]

            def norm(ni):
                pe.wait_ge(xn_rdy, ni + 1)
                for k in range(KT):
                    for a in range(TT):
                        last = pe.transpose(B[k // 2][:, SEQ * (k % 2) + P * a:SEQ * (k % 2) + P * a + P],
                                            xn[:, a, P * k:P * k + P], ident[:, :])
                    if k % 2:
                        last.then_inc(xnT_ps, 1)
                pe.wait_ge(hT_act, ni + 1)
                pe.wait_ge(hT_dve, ni + 1)

            pe.wait_ge(pool_const, 1)
            pe.wait_ge(vec_in, 16 * len(VEC0 + VEC1))
            pe.transpose(B[7][:, 0:N0], vecrows[0:N0, 0, :], ident[0:N0, 0:N0])
            pe.transpose(B[7][:, P:P + N1], vecrows[0:N1, 1, :], ident[0:N1, 0:N1]).then_inc(vec_tp, 1)
            norm(0)
            pe.wait_ge(cols_rdy, 1)
            for n in range(3):
                w = weights("ev_in", n)
                w8 = w.rearrange("p (k n) -> p k n", k=KT)
                for a in range(TT):
                    for k in range(KT):
                        last = pe.matmul(B[2 * n + a][:, :], hT[:, k, P * a:P * a + P], w8[:, k, :],
                                         start=(k == 0), stop=(k == KT - 1))
                    last.then_inc(qkv_ps, 1)
            for n in range(3, 6):
                w = weights("ev_in", n)
                w8 = w.rearrange("p (k n) -> p k n", k=KT)
                for f in range(4):
                    m = (n - 3) * 2 + f // 2
                    if m >= 2 and f % 2 == 0:
                        pe.wait_ge(raw_sb, m - 1)
                    for k in range(KT):
                        last = pe.matmul(B[6 + m % 2][:, SEQ * (f % 2):SEQ * (f % 2) + SEQ],
                                         w8[:, k, P * f:P * f + P], hT[:, k, :], start=(k == 0), stop=(k == KT - 1))
                    if f % 2:
                        last.then_inc(raw_ps, 1)
            w = weights("lora1", 0)[:, 0:KT * 384].rearrange("p (k n) -> p k n", k=KT)
            pe.wait_ge(hx_rdy, 1)
            pe.wait_ge(qkv_sb, 6)
            for i in range(3):
                for k in range(KT):
                    last = pe.matmul(B[i][:, 0:SEQ], w[:, k, P * i:P * i + P],
                                     hxT[:, k, :], start=(k == 0), stop=(k == KT - 1))
                last.then_inc(lora_ps, 1)
            w = weights("lora2", 0)
            for m in range(16):
                i, z, j = m // 8, (m // 4) % 2, m % 4
                if m == 0 or m == 8:
                    pe.wait_ge(lora_sb, 1 + m // 8)
                if m >= 6 and m % 2 == 0:
                    pe.wait_ge(wa_sb, m - 4)
                r = slice(64 * z, 64 * z + 64)
                last = pe.matmul(B[3 + (m // 2) % 3][:, SEQ * (m % 2):SEQ * (m % 2) + SEQ],
                                 w[r, 512 * i + P * j:512 * i + P * j + P], lora[r, i, :], start=True, stop=True)
                if m % 2:
                    last.then_inc(wa_ps, 1)
            pe.wait_ge(lora_sb, 3)
            for a in range(TT):
                pe.matmul(B[a][:, :], lora[:, 2, P * a:P * a + P], w[:, 1024:1536],
                          start=True, stop=True).then_inc(gate_ps, 1)
            pe.wait_ge(dve_step, DVE_STEPS["qk_rdy"])
            pe.wait_ge(wa_sb, 16)
            pe.wait_ge(raw_sb, 6)
            for i in range(4):
                for jj in range(2):
                    for a in range(TT):
                        c0 = 512 * (i // 2) + P * (2 * (i % 2) + jj)
                        last = pe.transpose(B[4 + i][:, SEQ * jj + P * a:SEQ * jj + P * a + P],
                                            qkv[:, a, c0:c0 + P], ident[:, :])
                last.then_inc(qkT_ps, 1)
            pe.wait_ge(qkT_sb, 4)
            pe.wait_ge(gate_sb, 2)

            def scores(h):
                r = slice(64 * (h % 2), 64 * (h % 2) + 64)
                if h >= 2:
                    pe.wait_ge(att_m, h - 1)
                for a in range(TT):
                    last = pe.matmul(B[h % 2][:, SEQ * a:SEQ * a + SEQ], qT[r, h // 2, P * a:P * a + P],
                                     kTt[r, h // 2, :], start=True, stop=True)
                last.then_inc(att_s, 1)

            def values(h):
                pe.wait_ge(att_c, h + 1)
                for a in range(TT):
                    for b in range(TT):
                        last = pe.matmul(B[3 + 2 * a][:, DH * h:DH * h + DH],
                                         att_pT[:, h % 2, SEQ * a + P * b:SEQ * a + P * b + P],
                                         qkv[:, b, D + DH * h:D + DH * h + DH], start=(b == 0), stop=(b == TT - 1))
                last.then_inc(att_o, 1)

            scores(0)
            for h in range(HA):
                if h + 1 < HA:
                    scores(h + 1)
                if h:
                    values(h - 1)
                pe.wait_ge(att_e, h + 1)
                if h >= 2:
                    pe.wait_ge(att_c, h - 1)
                for a in range(TT):
                    for b in range(TT):
                        last = pe.transpose(B[2 + 2 * (h % 2)][:, SEQ * a + P * b:SEQ * a + P * b + P],
                                            sm_p[:, h % 2, SEQ * a + P * b:SEQ * a + P * b + P], ident[:, :])
                last.then_inc(att_t, 1)
            values(HA - 1)
            pe.wait_ge(dve_step, DVE_STEPS["mix_rdy"])
            for a in range(TT):
                for j in range(4):
                    last = pe.transpose(B[6 + a][:, P * j:P * j + P], mix[:, 8 + j, P * a:P * a + P], ident[:, :])
                last.then_inc(vt_ps, 1)
            pe.wait_ge(vt_sb, 2)
            pe.wait_ge(dve_step, DVE_STEPS["kk_sq"])
            for i in range(2):
                pe.matmul(B[6 + i][:, :], bones[:, :], Cw_f[:, 512 * i:512 * i + 512],
                          start=True, stop=True).then_inc(kk_ps, 1)
            pe.wait_ge(dve_step, DVE_STEPS["bon_rdy"])
            pe.wait_ge(dve_step, DVE_STEPS["ya_rdy"])
            for a in range(TT):
                for j in range(4):
                    last = pe.matmul(B[5][:, HA * a:HA * a + HA], Hw_f[:, SEQ * j + P * a:SEQ * j + P * a + P],
                                     head_ind[:, j, :], start=(j == 0), stop=(j == 3))
            last.then_inc(bon_ps, 1)

            def invert(p):
                Tm, Pm, Xm, Am = INVB[p]
                for g in range(2):
                    pe.wait_ge(t0_rdy, 2 * p + g + 1)
                    for u in range(4):
                        last = pe.transpose(B[2 + g][:, P * u:P * u + P], Tm[g][:, u, :], ident[:, :])
                    last.then_inc(p0_ps, 1)
                for lev in range(1, NLEV):
                    for g in range(2):
                        n = inv_seq(p, lev, g)
                        odd = INV[p][g][0] == 0
                        if lev == 1:
                            pe.wait_ge(p0_sb, 2 * p + g + 1)
                        else:
                            pe.wait_ge(tp_sb, n - 2)
                        pe.wait_ge(am_rdy, n)
                        pm = odd_even(Pm[g], lev, odd)
                        for u in range(4):
                            if lev < NLEV - 1:
                                o, i = B[g][:, P * u:P * u + P], Pm[g][:, u, :]
                            else:
                                o, i = B[g][:, P * u:P * u + 64], pm[:, u, 0, :]
                            last = pe.matmul(o, Am[g][:, u, :], i, start=True, stop=True)
                        last.then_inc(x_ps, 1)
                    for g in range(2):
                        n = inv_seq(p, lev, g)
                        odd = INV[p][g][0] == 0
                        pe.wait_ge(x_cp, n)
                        xm = odd_even(Xm[g], lev, odd)
                        tm = odd_even(Tm[g], lev, not odd)
                        for u in range(4):
                            last = pe.matmul(packed(B[2 + g], lev, 0)[:, u], Tm[g][:, u, :], xm[:, u],
                                             start=True, stop=True)
                            if lev < NLEV - 1:
                                last = pe.matmul(packed(B[2 + g], lev, 64)[:, u], Xm[g][:, u, :], tm[:, u],
                                                 start=True, stop=True)
                        last.then_inc(pt_ps, 1)

            pe.wait_ge(dve_step, DVE_STEPS["fac_rdy"])
            pe.wait_ge(dve_step, DVE_STEPS["bon_cp"])
            for p, (z, c) in enumerate(RW):
                if p < 2:
                    if p:
                        pe.wait_ge(u_sb, 2)
                    for i, f in enumerate((bF, kF)):
                        for j in range(4):
                            last = pe.transpose(B[6 + i][:, P * j:P * j + P], f[z][:, j, c, :], ident[:, :])
                        last.then_inc(tok_ps, 1)
                for i in range(8):
                    h, g = i, i // 4
                    r = slice(64 * (h % 2), 64 * (h % 2) + 64)
                    j = h // 2
                    n = 8 * p + i
                    if i >= 2:
                        pe.wait_ge(sc_sb, n - 1)
                    elif p:
                        pe.wait_ge(y_sb, 2 * p)
                    bank = B[4 + i % 2]
                    ar = arF[z][r, j, c].rearrange("p m s -> p (m s)")
                    pe.matmul(bank[:, 0:2 * P], kF[z][r, j, c, :], ar, start=True, stop=True)
                    pe.matmul(bank[:, 2 * P:3 * P], bF[z][r, j, c, :], arF[z][r, j, c, 1, :], start=True, stop=True)
                    pe.matmul(bank[:, 3 * P:4 * P], arF[z][r, j, c, 0, :], bF[z][r, j, c, :],
                              start=True, stop=True).then_inc(sc_ps, 1)
                invert(p)
                if p < 2:
                    pe.wait_ge(tok_sb, 2 * p + 2)
                else:
                    pe.wait_ge(s_sb, 2 * (p - 2) + 2)
                pe.wait_ge(sc_sb, 8 * p + 8)
                vv = vtok[:, c, :]
                for g in range(2):
                    for q in range(2):
                        j = 2 * g + q
                        if p >= 2:
                            pe.matmul(B[4 + g][:, P * q:P * q + P], arF[z][:, j, c, 0, :], S0[z][:, j, :],
                                      start=True, stop=False, skip_group_check=True)
                        for i in range(2):
                            u, h = 2 * q + i, 4 * g + 2 * q + i
                            last = pe.matmul(B[4 + g][:, DH * u:DH * u + DH], scg[g][:, u, 0, :],
                                             vv[:, DH * h:DH * h + DH], start=(p < 2), stop=True,
                                             skip_group_check=True)
                    last.then_inc(r_ps, 1)
                for g in range(2):
                    pe.wait_ge(r_sb, 2 * p + g + 1)
                    pe.wait_ge(tp_sb, inv_seq(p, NLEV - 1, g))
                    for u in range(4):
                        last = pe.matmul(B[6 + g][:, DH * u:DH * u + DH], Pm[g][:, u, :], Rm[g][:, u, :],
                                         start=True, stop=True)
                    last.then_inc(u_ps, 1)
                for g in range(2):
                    pe.wait_ge(u_sb, 2 * p + g + 1)
                    if p < 2:
                        for q in range(2):
                            j = 2 * g + q
                            o = B[g][:, P * q:P * q + P]
                            pe.matmul(o, tokbk[:, 0, j, :], Um[g][:, 2 * q:2 * q + 2, :].rearrange("p u v -> p (u v)"),
                                      start=True, stop=False)
                            last = pe.matmul(o, tokbk[:, 1, j, :], vv[:, P * j:P * j + P], start=False, stop=True)
                        last.then_inc(s_ps, 1)
                    for q in range(2):
                        j = 2 * g + q
                        if p >= 2:
                            pe.matmul(B[4 + g][:, P * q:P * q + P], arF[z][:, j, c, 1, :], S0[z][:, j, :],
                                      start=True, stop=False, skip_group_check=True)
                        for i in range(2):
                            u, h = 2 * q + i, 4 * g + 2 * q + i
                            o = B[4 + g][:, DH * u:DH * u + DH]
                            pe.matmul(o, scg[g][:, u, 1, :], vv[:, DH * h:DH * h + DH], start=(p < 2), stop=False,
                                      skip_group_check=True)
                            last = pe.matmul(o, scg[g][:, u, 2, :], Um[g][:, u, :], start=False, stop=True,
                                             skip_group_check=True)
                    last.then_inc(y_ps, 1)

            def out_projection(layer, kind):
                lhs = yT if layer == 0 else yTo
                for n in range(2):
                    w8 = weights(kind, n).rearrange("p (k n) -> p k n", k=KT)
                    for a in range(TT):
                        for k in range(KT):
                            last = pe.matmul(B[4 + 2 * n + a][:, :], lhs[:, k, P * a:P * a + P], w8[:, k, :],
                                             start=(k == 0), stop=(k == KT - 1))
                        last.then_inc(o_ps, 1)

            pe.wait_ge(dve_step, DVE_STEPS["yab_rdy"])
            for i in range(4):
                for jj in range(2):
                    for a in range(TT):
                        k = 2 * i + jj
                        last = pe.transpose(B[i][:, SEQ * jj + P * a:SEQ * jj + P * a + P],
                                            yab[:, a, P * k:P * k + P], ident[:, :])
                last.then_inc(yT_ps, 1)
            pe.wait_ge(yT_sb, 4)
            out_projection(0, "ev_out")
            if UPTO >= 2:
                norm(1)
                pe.wait_ge(x_rdy, 2)

                def ffn_down(m):
                    k = min(4, FF // P - 4 * m)
                    wd = weights("ffn_down", m)[:, 0:k * D].rearrange("p (k n) -> p k n", k=k)
                    pe.wait_ge(gu_sb, 4 * m + k)
                    end = m == FF // 512
                    for n in range(2):
                        for a in range(TT):
                            for f in range(k):
                                last = pe.matmul(B[4 + 2 * n + a][:, :], hf[:, (4 * m + f) % 8, P * a:P * a + P],
                                                 wd[:, f, 512 * n:512 * n + 512], start=(m == 0 and f == 0),
                                                 stop=(end and f == k - 1))
                            if end:
                                last.then_inc(o_ps, 1)
                    if not end:
                        last.then_inc(dn_ps, 1)

                for n in range(FF // 256):
                    w8 = weights("ffn_in", n).rearrange("p (k n) -> p k n", k=KT)
                    for f in range(2):
                        i = 2 * n + f
                        if i >= 3:
                            pe.wait_ge(gu_sb, i - 2)
                        for half in range(2):
                            for k in range(KT):
                                c0 = SEQ * half + P * f
                                last = pe.matmul(B[i % 3][:, SEQ * half:SEQ * half + SEQ], w8[:, k, c0:c0 + P],
                                                 hT[:, k, :], start=(k == 0), stop=(k == KT - 1))
                        last.then_inc(gu_ps, 1)
                    if n and n % 2 == 0:
                        ffn_down(n // 2 - 1)
                ffn_down(FF // 512)
            if UPTO >= 3:
                norm(2)
                pe.wait_ge(wsmall_in, 32)
                pe.wait_ge(x_rdy, 4)
                for a in range(TT):
                    for k in range(KT):
                        last = pe.matmul(B[6][:, 16 * a:16 * a + 16], hT[:, k, P * a:P * a + P], ba_w[:, k, :],
                                         start=(k == 0), stop=(k == KT - 1))
                last.then_inc(ba_ps, 1)
                for n in range(6):
                    w8 = weights("od_in", n).rearrange("p (k n) -> p k n", k=KT)
                    for f in range(4):
                        m = 2 * n + f // 2
                        if m >= 4 and f % 2 == 0:
                            pe.wait_ge(cv_sb, m - 3)
                        for k in range(KT):
                            last = pe.matmul(B[m % 4][:, SEQ * (f % 2):SEQ * (f % 2) + SEQ],
                                             w8[:, k, P * f:P * f + P], hT[:, k, :], start=(k == 0), stop=(k == KT - 1))
                        if f % 2:
                            last.then_inc(cv_ps, 1)
                w8 = weights("od_in", 6).rearrange("p (k n) -> p k n", k=KT)
                for a in range(TT):
                    for k in range(KT):
                        last = pe.matmul(B[4 + a][:, :], hT[:, k, P * a:P * a + P], w8[:, k, :],
                                         start=(k == 0), stop=(k == KT - 1))
                    last.then_inc(z_ps, 1)
                pe.wait_ge(dve_step, DVE_STEPS["g_rdy"])
                for c in range(TT):
                    for z in range(2):
                        pe.matmul(B[7][:, 8 * c + 4 * z:8 * c + 4 * z + 4], tri[:, 2 + z, :],
                                  glog[:, c, 4 * z:4 * z + 4], start=True, stop=True)
                    last = pe.matmul(B[7][:, 16 + 8 * c:24 + 8 * c], ones[:, :], glog[:, c, :], start=True, stop=True)
                last.then_inc(gc_ps, 1)
                pe.wait_ge(cv_sb, 12)
                for i in range(4):
                    pe.wait_ge(l2_sq, i // 2 + 1)
                    pe.matmul(B[i][:, :], ones[:, :], xn[:, i // 2, 512 * (i % 2):512 * (i % 2) + 512],
                              start=True, stop=True).then_inc(l2_ps, 1)
                pe.wait_ge(dve_step, DVE_STEPS["qk2_rdy"])
                pe.wait_ge(z_sb, 2)
                pe.wait_ge(dve_step, DVE_STEPS["gc_rdy"])
                for c in range(TT):
                    cs = slice(P * c, P * c + P)
                    for h in range(HD):
                        pe.matmul(B[c][:, P * h:P * h + P], qkvc[:, 4 + h, cs], qkvc[:, 4 + h, cs], start=True, stop=True)
                        last = pe.matmul(B[2 + c][:, P * h:P * h + P], qkvc[:, 4 + h, cs], qkvc[:, h, cs],
                                         start=True, stop=True)
                    last.then_inc(kk2_ps, 1)
                pe.wait_ge(silu_rdy, 3)
                for i in range(4):
                    for h in range(HD):
                        last = pe.transpose(B[4 + i][:, P * h:P * h + P],
                                            qkvc[:, 4 + 4 * (i // 2) + h, P * (i % 2):P * (i % 2) + P], ident[:, :])
                    last.then_inc(tk_ps, 1)
                pe.wait_ge(tk_sb, 4)
                for p in range(4, 6):
                    for g in range(2):
                        z, c = INV[p][g]
                        if p == 5:
                            pe.wait_ge(oo_sb, g + 1)
                        for u in range(4):
                            last = pe.matmul(B[4 + g][:, P * u:P * u + P],
                                             glog[:, c, 4 * z + u:4 * z + u + 1].to_broadcast([P, P]),
                                             tri[:, 2 + z, :], start=True, stop=True)
                        last.then_inc(row_ps, 1)
                    pe.wait_ge(os_sb if p == 5 else kk2_sb, 2)
                    invert(p)
                    if p == 5:
                        for g in range(2):
                            z, c = INV[p][g]
                            for u in range(4):
                                last = pe.matmul(B[4 + g][:, P * u:P * u + P], ke[g][:, u, :], S0o[z][:, u, :],
                                                 start=True, stop=True)
                            last.then_inc(ks_ps, 1)
                    for g in range(2):
                        pe.wait_ge(or_rdy, 2 * (p - 4) + g + 1)
                        pe.wait_ge(tp_sb, inv_seq(p, NLEV - 1, g))
                        for u in range(4):
                            last = pe.matmul(B[6 + g][:, P * u:P * u + P], INVB[p][1][g][:, u, :], Ro[g][:, u, :],
                                             start=True, stop=True)
                        last.then_inc(ou_ps, 1)
                    if p == 4:
                        for g in range(2):
                            z, c = INV[p][g]
                            pe.wait_ge(ous_rdy, g + 1)
                            for u in range(4):
                                last = pe.matmul(B[g][:, P * u:P * u + P], ktok[:, c, P * u:P * u + P],
                                                 qe[g][:, u, :], start=True, stop=True)
                            last.then_inc(os_ps, 1)
                    for g in range(2):
                        z, c = INV[p][g]
                        pe.wait_ge(ou_sb, 2 * (p - 4) + g + 1)
                        for u in range(4):
                            o = B[4 + g][:, P * u:P * u + P]
                            if p == 5:
                                pe.matmul(o, qe[g][:, u, :], S0o[z][:, u, :], start=True, stop=False)
                            last = pe.matmul(o, attn[g][:, u, :], Uo[g][:, u, :], start=(p == 4), stop=True)
                        last.then_inc(oo_ps, 1)
                pe.wait_ge(dve_step, DVE_STEPS["yd_rdy"])
                for i in range(2):
                    for jj in range(2):
                        for a in range(TT):
                            k = 2 * i + jj
                            last = pe.transpose(B[i][:, SEQ * jj + P * a:SEQ * jj + P * a + P],
                                                osum[:, a, P * k:P * k + P], ident[:, :])
                    last.then_inc(yd_ps, 1)
                pe.wait_ge(yd_sb, 2)
                pe.wait_ge(dve_step, DVE_STEPS["yc_rdy"])
                out_projection(2, "od_out")
            if UPTO >= 4:
                norm(3)
                pe.wait_ge(x_rdy, 6)
                for a in range(TT):
                    for k in range(KT):
                        last = pe.matmul(B[7][:, NE * a:NE * a + NE], hT[:, k, P * a:P * a + P], router_w[:, k, :],
                                         start=(k == 0), stop=(k == KT - 1))
                last.then_inc(rt_ps, 1)
                pe.wait_ge(dve_step, DVE_STEPS["as_rdy"])
                pe.matmul(B[6][:, 0:8], tri[:, 1, :], asg[:, 0, :], start=True, stop=True)
                pe.matmul(B[6][:, 8:16], tri[:, 1, :], asg[:, 1, :], start=True, stop=False)
                pe.matmul(B[6][:, 8:16], ones[:, :], asg[:, 0, :], start=False, stop=True)
                pe.matmul(B[6][:, 16:24], ones[:, :], asg[:, 0, :], start=True, stop=False)
                pe.matmul(B[6][:, 16:24], ones[:, :], asg[:, 1, :], start=False, stop=True).then_inc(rank_ps, 1)

                def expert(ps, i):
                    b1, b2, b7 = NE * ps + 1, 2 * NE * ps + 1, NC_E * NE * ps + 1

                    def product(o, hi, lo, r, cols_, start, stop):
                        wh, wl = (wst[:, r % NSTAGE, t, cols_] for t in range(2))
                        pe.matmul(o, hi, wh, start=start, stop=False)
                        pe.matmul(o, hi, wl, start=False, stop=False)
                        return pe.matmul(o, lo, wh, start=False, stop=stop)

                    pe.wait_ge(sel_rdy, i + ((NE + 1) * ps + 1))
                    for k in range(KT):
                        for a in range(TT):
                            last = pe.matmul(B[6 + k // 4][:, P * (k % 4):P * (k % 4) + P], xn[:, a, P * k:P * k + P],
                                             sel[:, a, :], start=(a == 0), stop=(a == TT - 1))
                        if k % 4 == 3:
                            last.then_inc(xg_ps, 1)
                    for a in range(TT):
                        last = pe.transpose(B[4][:, P * a:P * a + P], selg[:, a, :], ident[:, :])
                    last.then_inc(st_ps, 1)

                    def project(kind, j):
                        o = B[j % 2 + (0 if kind == "gate" else 2)][:, :]
                        for h in range(2):
                            r = at_half[kind, j, h]
                            if j == 0 and h == 0 and kind == "gate":
                                pe.wait_ge(cmb_sb, i * 4 + (4 * NE * ps + 1))
                            if j == 0 and kind == "gate":
                                pe.wait_ge(x_lo, i * 2 + b2 + h)
                            pe.wait_ge(w_lo, i * PER + (NE * PER * ps + r + 1))
                            for k in range(4):
                                last = product(o, xgs[:, 0, 4 * h + k, :], xgs[:, 1, 4 * h + k, :], r,
                                               slice(512 * k, 512 * k + 512), h == 0 and k == 0, h == 1 and k == 3)
                            last.then_inc(half_ps, 1)

                    def turn(j):
                        pe.wait_ge(eh_rdy, i * NC_E + b7 + j)
                        for k in range(EC // P):
                            last = pe.transpose(B[6 + j % 2][:, P * k:P * k + P], ehr[:, j % 2, P * k:P * k + P],
                                                ident[:, :])
                        last.then_inc(ht_ps, 1)

                    def down(j):
                        if j == 0:
                            pe.wait_ge(st_sb, i + b1)
                        pe.wait_ge(ht_lo, i * NC_E + b7 + j)
                        for h in range(2):
                            r = at_half["down", j, h]
                            pe.wait_ge(w_lo, i * PER + (NE * PER * ps + r + 1))
                            for n in range(2):
                                for k in range(2):
                                    last = product(B[4 + n][:, :], ehs[:, j % 2, 0, 2 * h + k, :],
                                                   ehs[:, j % 2, 1, 2 * h + k, :], r,
                                                   slice(D * k + 512 * n, D * k + 512 * n + 512),
                                                   j == 0 and h == 0 and k == 0, j == NC_E - 1 and h == 1 and k == 1)
                            last.then_inc(half_ps, 1)

                    for j in range(NC_E):
                        project("gate", j)
                        if j:
                            turn(j - 1)
                        project("up", j)
                        if j:
                            down(j - 1)
                    turn(NC_E - 1)
                    down(NC_E - 1)
                    for n in range(2):
                        pe.wait_ge(ey_sb, i * 2 + b2 + n)
                        for a in range(TT):
                            pe.matmul(B[2 * n + a][:, :], selgT[:, P * a:P * a + P], ysb[:, 512 * n:512 * n + 512],
                                      start=True, stop=True).then_inc(cmb_ps, 1)

                pe.sem_inc(half_ps, NSTAGE)
                with pe.Fori(0, NE) as i:
                    expert(0, i)
                pe.wait_ge(flag_rdy, 1)
                with pe.If(pe.value_load(flag[0:1, 0:1], min_val=0, max_val=1) > 0):
                    with pe.Fori(0, NE) as i:
                        expert(1, i)


_INS = ["x", "positions", "ev_mix_norm", "ev_w_in", "ev_q_norm", "ev_k_norm", "ev_shift_mu", "ev_lora_mu", "ev_w0",
        "ev_w1", "ev_w2", "ev_a0", "ev_a1", "ev_a2", "ev_g1", "ev_g2", "ev_k_k", "ev_k_a", "ev_r_k", "ev_ln_w",
        "ev_ln_b", "ev_w_out", "ev_ffn_norm", "ev_ffn_gate", "ev_ffn_up", "ev_ffn_down", "od_mix_norm", "od_w_in",
        "od_conv_c", "od_conv_dn", "od_A_log", "od_dt_bias", "od_dn_norm", "od_w_out", "od_ffn_norm", "od_router",
        "od_moe_gate", "od_moe_up", "od_moe_down"]


def kernel(**inputs):
    import concourse.bacc as bacc
    from concourse.bass_utils import run_bass_kernel_spmd
    nc = bacc.Bacc("TRN2", target_bir_lowering=False, num_devices=1)
    arrays, aps = {}, {}
    for name in _INS:
        a = np.ascontiguousarray(inputs[name])
        arrays[f"in_{name}"] = a
        aps[name] = nc.dram_tensor(f"in_{name}", a.shape, mybir.dt.from_np(a.dtype), kind="ExternalInput").ap()
    out = nc.dram_tensor("out_x", (1, SEQ, D), F32, kind="ExternalOutput").ap()
    hybrid_trunk(nc, aps, out)
    r = run_bass_kernel_spmd(nc, [arrays], core_ids=[0])
    return r.results[0]["out_x"]
```
